# Optimizing a Trainium2 kernel written in Bass

```python
import math
import jax, jax.numpy as jnp
from jax import lax
import numpy as np

D_MODEL = 1024
BATCH = 1
SEQ = 256
DEPTH = 2

N_A_LAYERS = DEPTH // 2
N_B_LAYERS = DEPTH - N_A_LAYERS

MLSTM_HEADS = 4
MLSTM_INNER = 2 * D_MODEL
MLSTM_HEAD_DIM = MLSTM_INNER // MLSTM_HEADS
CONV_WIDTH = 4
MLSTM_CHUNK = 128

ATTN_HEADS = 16
ATTN_HEAD_DIM = D_MODEL // ATTN_HEADS
MOBA_BLOCK = 256
MOBA_TOPK = 3
MOBA_QCHUNK = 32

N_EXPERTS = 16
N_GROUPS = 4
EXPERTS_PER_GROUP = N_EXPERTS // N_GROUPS
MOE_TOPK = 2
D_FF_EXPERT = 512
MOE_ROW_BLOCK = 256

DEEPNORM_ALPHA = (2.0 * DEPTH) ** 0.25
DEEPNORM_BETA = (8.0 * DEPTH) ** -0.25
LN_EPS = 1e-5
N_MOD_PER_LAYER = 6


def layer_norm(x, g, b):
    xf = x.astype(jnp.float32)
    mu = xf.mean(-1, keepdims=True)
    var = jnp.square(xf - mu).mean(-1, keepdims=True)
    return ((xf - mu) * lax.rsqrt(var + LN_EPS) * g + b).astype(x.dtype)

def modulate(x, shift, scale):
    return x * (1 + scale[:, None, :]) + shift[:, None, :]

def causal_conv(x, w, b):
    K, C = w.shape
    y = lax.conv_general_dilated(x, w[:, None, :], window_strides=(1,), padding=[(K - 1, 0)],
                                 dimension_numbers=('NWC', 'WIO', 'NWC'), feature_group_count=C)
    return y + b

def mlstm_chunkwise(q, k, v, log_i, log_f):
    B, H, S, Dh = q.shape
    L = MLSTM_CHUNK
    nc = S // L

    def to_chunks(t):
        return jnp.moveaxis(t.reshape(t.shape[:2] + (nc, L) + t.shape[3:]), 2, 0)

    causal = jnp.tril(jnp.ones((L, L), bool))

    def step(carry, inp):
        C, n, m = carry
        qc, kc, vc, ic, fc = inp
        b = jnp.cumsum(fc, axis=-1)
        d = jnp.where(causal, b[..., :, None] - b[..., None, :] + ic[..., None, :], -jnp.inf)
        a = b + m[..., None]
        m_t = jnp.maximum(a, d.max(-1))
        w_intra = jnp.exp(d - m_t[..., None])
        w_inter = jnp.exp(a - m_t)
        s = jnp.einsum('bhtd,bhsd->bhts', qc, kc) * w_intra
        num = jnp.einsum('bhts,bhsd->bhtd', s, vc) + w_inter[..., None] * jnp.einsum('bhvd,bhtd->bhtv', C, qc)
        den = s.sum(-1) + w_inter * jnp.einsum('bhd,bhtd->bht', n, qc)
        h = num / jnp.maximum(jnp.abs(den), jnp.exp(-m_t))[..., None]
        b_last = b[..., -1]
        w_s = b_last[..., None] - b + ic
        m_new = jnp.maximum(b_last + m, w_s.max(-1))
        decay = jnp.exp(b_last + m - m_new)
        w_s = jnp.exp(w_s - m_new[..., None])
        C_new = decay[..., None, None] * C + jnp.einsum('bhs,bhsv,bhsd->bhvd', w_s, vc, kc)
        n_new = decay[..., None] * n + jnp.einsum('bhs,bhsd->bhd', w_s, kc)
        return (C_new, n_new, m_new), h

    init = (jnp.zeros((B, H, Dh, Dh), jnp.float32), jnp.zeros((B, H, Dh), jnp.float32),
            jnp.zeros((B, H), jnp.float32))
    _, hs = lax.scan(step, init, (to_chunks(q), to_chunks(k), to_chunks(v), to_chunks(log_i), to_chunks(log_f)))
    return jnp.moveaxis(hs, 0, 2).reshape(B, H, S, Dh)

def mlstm_layer(h, w_in, conv_w, conv_b, wq, wk, wv, w_if, b_if, gn_g, skip, w_out):
    B, S, _ = h.shape
    NH, DH = MLSTM_HEADS, MLSTM_HEAD_DIM
    f32 = jnp.float32
    xm, z = jnp.split(h @ w_in, 2, axis=-1)
    xc = jax.nn.silu(causal_conv(xm, conv_w, conv_b))
    xc_h = xc.reshape(B, S, NH, DH)
    xm_h = xm.reshape(B, S, NH, DH)
    q = jnp.einsum('bshd,hde->bhse', xc_h, wq).astype(f32)
    k = (jnp.einsum('bshd,hde->bhse', xc_h, wk) * (DH ** -0.5)).astype(f32)
    v = jnp.einsum('bshd,hde->bhse', xm_h, wv).astype(f32)
    gates = jnp.transpose((xc @ w_if + b_if).astype(f32), (0, 2, 1))
    log_i = gates[:, :NH]
    log_f = jax.nn.log_sigmoid(gates[:, NH:])
    hh = mlstm_chunkwise(q, k, v, log_i, log_f)
    mu = hh.mean(-1, keepdims=True)
    var = jnp.square(hh - mu).mean(-1, keepdims=True)
    hh = (hh - mu) * lax.rsqrt(var + LN_EPS)
    hh = hh.transpose(0, 2, 1, 3).reshape(B, S, MLSTM_INNER).astype(h.dtype) * gn_g
    hh = (hh + skip * xc) * jax.nn.silu(z)
    return hh @ w_out

def shared_kv(x, shift, scale, w_kv):
    B, S, D = x.shape
    k, v = jnp.split(modulate(x, shift, scale) @ w_kv, 2, axis=-1)
    s_pad = -(-S // MOBA_BLOCK) * MOBA_BLOCK
    nblk = s_pad // MOBA_BLOCK

    def to_blocks(t):
        t = t.reshape(B, S, ATTN_HEADS, ATTN_HEAD_DIM).transpose(0, 2, 1, 3)
        t = jnp.pad(t, ((0, 0), (0, 0), (0, s_pad - S), (0, 0)))
        return t.reshape(B, ATTN_HEADS, nblk, MOBA_BLOCK, ATTN_HEAD_DIM)

    k_blocks, v_blocks = to_blocks(k), to_blocks(v)
    k_means = k_blocks.astype(jnp.float32).mean(3).astype(k.dtype)
    return k_blocks, v_blocks, k_means

def alibi_slopes(n_heads):
    return jnp.exp2(-8.0 * (jnp.arange(n_heads, dtype=jnp.float32) + 1.0) / n_heads)

def moba_attention(q, k_blocks, v_blocks, k_means, slopes):
    B, H, S, Dh = q.shape
    nblk = k_blocks.shape[2]
    topk = min(MOBA_TOPK, nblk)
    QC, BLK = MOBA_QCHUNK, MOBA_BLOCK
    nq = S // QC
    q_chunks = jnp.moveaxis(q.reshape(B, H, nq, QC, Dh), 2, 0)
    bi = jnp.arange(B)[:, None, None, None]
    hi = jnp.arange(H)[None, :, None, None]
    blk_ids = jnp.arange(nblk)
    offs = jnp.arange(BLK)
    f32 = jnp.float32

    def one_chunk(args):
        ci, qc = args
        t = ci * QC + jnp.arange(QC)
        own = (ci * QC) // BLK
        gate = jnp.einsum('bhtd,bhnd->bhtn', qc, k_means).astype(f32)
        gate = jnp.where(blk_ids < own, gate, -jnp.inf)
        _, sel = lax.top_k(gate, topk)
        valid = sel < own
        k_sel = k_blocks[bi, hi, sel]
        v_sel = v_blocks[bi, hi, sel].reshape(B, H, QC, topk * BLK, Dh)
        s_sel = jnp.einsum('bhtd,bhtjsd->bhtjs', qc, k_sel).astype(f32)
        pos_sel = sel[..., None] * BLK + offs
        dist_sel = (t[:, None, None] - pos_sel).astype(f32)
        s_sel = s_sel - slopes[:, None, None, None] * dist_sel
        s_sel = jnp.where(valid[..., None], s_sel, -jnp.inf).reshape(B, H, QC, topk * BLK)
        k_own = lax.dynamic_index_in_dim(k_blocks, own, axis=2, keepdims=False)
        v_own = lax.dynamic_index_in_dim(v_blocks, own, axis=2, keepdims=False)
        s_own = jnp.einsum('bhtd,bhsd->bhts', qc, k_own).astype(f32)
        pos_own = own * BLK + offs
        dist_own = (t[:, None] - pos_own[None, :]).astype(f32)
        s_own = jnp.where(dist_own >= 0, s_own - slopes[:, None, None] * dist_own, -jnp.inf)
        p = jax.nn.softmax(jnp.concatenate([s_sel, s_own], axis=-1), axis=-1).astype(v_blocks.dtype)
        return (jnp.einsum('bhts,bhtsd->bhtd', p[..., :topk * BLK], v_sel)
                + jnp.einsum('bhts,bhsd->bhtd', p[..., topk * BLK:], v_own))

    outs = lax.map(one_chunk, (jnp.arange(nq), q_chunks))
    return jnp.moveaxis(outs, 0, 2).reshape(B, H, S, Dh)

def moba_layer(h, wq, wo, k_blocks, v_blocks, k_means, slopes):
    B, S, D = h.shape
    q = (h @ wq).reshape(B, S, ATTN_HEADS, ATTN_HEAD_DIM).transpose(0, 2, 1, 3) * (ATTN_HEAD_DIM ** -0.5)
    o = moba_attention(q, k_blocks, v_blocks, k_means, slopes)
    return o.transpose(0, 2, 1, 3).reshape(B, S, D) @ wo

def route(x2, w_router, b_router):
    T = x2.shape[0]
    probs = jax.nn.softmax((x2 @ w_router).astype(jnp.float32), axis=-1)
    sel_scores = (probs + b_router).reshape(T, N_GROUPS, EXPERTS_PER_GROUP)
    grp_score = lax.top_k(sel_scores, MOE_TOPK)[0].sum(-1)
    g = jnp.argmax(grp_score, axis=-1)
    masked = jnp.where(jnp.arange(N_GROUPS)[None, :, None] == g[:, None, None], sel_scores, -jnp.inf)
    _, idx = lax.top_k(masked.reshape(T, N_EXPERTS), MOE_TOPK)
    w = jnp.take_along_axis(probs, idx, axis=-1)
    return idx, w / w.sum(-1, keepdims=True)

def moe_ffn(h, w_router, b_router, w_gate, w_up, w_down):
    B, S, D = h.shape
    T = B * S
    x2 = h.reshape(T, D)
    idx, wts = route(x2, w_router, b_router)
    n_assign = T * MOE_TOPK
    e_flat = idx.reshape(-1)
    tok_flat = jnp.repeat(jnp.arange(T, dtype=jnp.int32), MOE_TOPK)
    w_flat = wts.reshape(-1)
    order = jnp.argsort(e_flat)
    e_sorted = e_flat[order]
    counts = jnp.zeros((N_EXPERTS,), jnp.int32).at[e_flat].add(1)
    starts = jnp.cumsum(counts) - counts
    padded = (counts + MOE_ROW_BLOCK - 1) // MOE_ROW_BLOCK * MOE_ROW_BLOCK
    pends = jnp.cumsum(padded)
    pstarts = pends - padded
    dest = pstarts[e_sorted] + (jnp.arange(n_assign, dtype=jnp.int32) - starts[e_sorted])
    n_blocks = -(-n_assign // MOE_ROW_BLOCK) + N_EXPERTS
    cap = n_blocks * MOE_ROW_BLOCK
    buf_tok = jnp.zeros((cap,), jnp.int32).at[dest].set(tok_flat[order])
    buf_w = jnp.zeros((cap,), jnp.float32).at[dest].set(w_flat[order])
    block_start = jnp.arange(n_blocks, dtype=jnp.int32) * MOE_ROW_BLOCK
    block_expert = jnp.minimum(jnp.searchsorted(pends, block_start, side='right'), N_EXPERTS - 1)
    xs = x2[buf_tok].reshape(n_blocks, MOE_ROW_BLOCK, D)

    def expert_block(args):
        xb, e = args
        return (jax.nn.silu(xb @ w_gate[e]) * (xb @ w_up[e])) @ w_down[e]

    ys = lax.map(expert_block, (xs, block_expert)).reshape(cap, D)
    y = jnp.zeros((T, D), h.dtype).at[buf_tok].add(ys * buf_w[:, None].astype(ys.dtype))
    return y.reshape(B, S, D)

def first_inputs(seed: int = 0) -> dict:
    key = jax.random.key(seed)
    ks = jax.random.split(key, 27)
    D, DI, NH, DH = D_MODEL, MLSTM_INNER, MLSTM_HEADS, MLSTM_HEAD_DIM
    nA, nB = N_A_LAYERS, N_B_LAYERS

    def nrm(k, shape, s):
        return jax.random.normal(k, shape, jnp.float32) * s

    n_mod = DEPTH * N_MOD_PER_LAYER * D + 2 * D
    x = nrm(ks[0], (BATCH, SEQ, D), 1.0)
    c = nrm(ks[1], (BATCH, D), 1.0)
    w_ada = nrm(ks[2], (D, n_mod), 0.1 * D ** -0.5)
    b_ada = nrm(ks[3], (n_mod,), 0.01)
    ln_g = 1.0 + nrm(ks[4], (DEPTH, 2, D), 0.02)
    ln_b = nrm(ks[5], (DEPTH, 2, D), 0.02)
    a_w_in = nrm(ks[6], (nA, D, 2 * DI), D ** -0.5)
    a_conv_w = nrm(ks[7], (nA, CONV_WIDTH, DI), CONV_WIDTH ** -0.5)
    a_conv_b = nrm(ks[8], (nA, DI), 0.01)
    a_wq = nrm(ks[9], (nA, NH, DH, DH), DH ** -0.5)
    a_wk = nrm(ks[10], (nA, NH, DH, DH), DH ** -0.5)
    a_wv = nrm(ks[11], (nA, NH, DH, DH), DEEPNORM_BETA * DH ** -0.5)
    a_w_if = nrm(ks[12], (nA, DI, 2 * NH), 0.1 * DI ** -0.5)
    a_b_if = jnp.concatenate([nrm(ks[13], (nA, NH), 0.1),
                              jnp.linspace(3.0, 6.0, NH) + nrm(ks[14], (nA, NH), 0.1)], axis=-1)
    a_gn_g = 1.0 + nrm(ks[15], (nA, DI), 0.02)
    a_skip = 1.0 + nrm(ks[16], (nA, DI), 0.02)
    a_w_out = nrm(ks[17], (nA, DI, D), DEEPNORM_BETA * DI ** -0.5)
    b_w_kv = jnp.concatenate([nrm(ks[18], (D, D), D ** -0.5),
                              nrm(ks[19], (D, D), DEEPNORM_BETA * D ** -0.5)], axis=-1)
    b_wq = nrm(ks[20], (nB, D, D), D ** -0.5)
    b_wo = nrm(ks[21], (nB, D, D), DEEPNORM_BETA * D ** -0.5)
    moe_w_router = nrm(ks[22], (D, N_EXPERTS), D ** -0.5)
    moe_b_router = nrm(ks[23], (N_EXPERTS,), 0.01)
    moe_w_gate = nrm(ks[24], (DEPTH, N_EXPERTS, D, D_FF_EXPERT), D ** -0.5)
    moe_w_up = nrm(ks[25], (DEPTH, N_EXPERTS, D, D_FF_EXPERT), D ** -0.5)
    moe_w_down = nrm(ks[26], (DEPTH, N_EXPERTS, D_FF_EXPERT, D), DEEPNORM_BETA * D_FF_EXPERT ** -0.5)
    return {'x': x, 'c': c, 'w_ada': w_ada, 'b_ada': b_ada, 'ln_g': ln_g, 'ln_b': ln_b,
            'a_w_in': a_w_in, 'a_conv_w': a_conv_w, 'a_conv_b': a_conv_b, 'a_wq': a_wq, 'a_wk': a_wk,
            'a_wv': a_wv, 'a_w_if': a_w_if, 'a_b_if': a_b_if, 'a_gn_g': a_gn_g, 'a_skip': a_skip,
            'a_w_out': a_w_out, 'b_w_kv': b_w_kv, 'b_wq': b_wq, 'b_wo': b_wo,
            'moe_w_router': moe_w_router, 'moe_b_router': moe_b_router, 'moe_w_gate': moe_w_gate,
            'moe_w_up': moe_w_up, 'moe_w_down': moe_w_down}

def first_block(x, c, w_ada, b_ada, ln_g, ln_b, a_w_in, a_conv_w, a_conv_b, a_wq, a_wk, a_wv, a_w_if,
              a_b_if, a_gn_g, a_skip, a_w_out, b_w_kv, b_wq, b_wo, moe_w_router, moe_b_router,
              moe_w_gate, moe_w_up, moe_w_down):
    B, S, D = x.shape
    n_layer_mod = DEPTH * N_MOD_PER_LAYER * D
    cond = jax.nn.silu(c) @ w_ada + b_ada
    mods = cond[:, :n_layer_mod].reshape(B, DEPTH, 2, 3, D)
    kv_mod = cond[:, n_layer_mod:].reshape(B, 2, D)
    slopes = alibi_slopes(ATTN_HEADS)
    kv = None
    for layer in range(DEPTH):
        shift, scale, gate = mods[:, layer, 0, 0], mods[:, layer, 0, 1], 1.0 + mods[:, layer, 0, 2]
        h = modulate(x, shift, scale)
        if layer < N_A_LAYERS:
            i = layer
            y = mlstm_layer(h, a_w_in[i], a_conv_w[i], a_conv_b[i], a_wq[i], a_wk[i], a_wv[i], a_w_if[i],
                            a_b_if[i], a_gn_g[i], a_skip[i], a_w_out[i])
        else:
            if kv is None:
                kv = shared_kv(x, kv_mod[:, 0], kv_mod[:, 1], b_w_kv)
            j = layer - N_A_LAYERS
            y = moba_layer(h, b_wq[j], b_wo[j], kv[0], kv[1], kv[2], slopes)
        x = layer_norm(DEEPNORM_ALPHA * x + gate[:, None, :] * y, ln_g[layer, 0], ln_b[layer, 0])
        shift, scale, gate = mods[:, layer, 1, 0], mods[:, layer, 1, 1], 1.0 + mods[:, layer, 1, 2]
        h = modulate(x, shift, scale)
        y = moe_ffn(h, moe_w_router, moe_b_router, moe_w_gate[layer], moe_w_up[layer], moe_w_down[layer])
        x = layer_norm(DEEPNORM_ALPHA * x + gate[:, None, :] * y, ln_g[layer, 1], ln_b[layer, 1])
    return x


D_FF = 2816
FFN_RESID = 0.5
EPS = 1e-6
GM_WIDTH = 512
GM_GROUPS = 4
GM_GROUP_DIM = GM_WIDTH // GM_GROUPS
GM_CHUNK = 128
MLA_HEADS = 8
MLA_Q_RANK = 384
MLA_KV_RANK = 256
MLA_NOPE = 64
MLA_ROPE = 32
MLA_QK_DIM = MLA_NOPE + MLA_ROPE
MLA_V = 64
MLA_WIDTH = MLA_HEADS * MLA_V
ROPE_THETA = 10000.0
Q_BLOCK = 128
SSD_HEADS = 8
SSD_HEAD_DIM = 64
SSD_INNER = SSD_HEADS * SSD_HEAD_DIM
SSD_GROUPS = 2
SSD_STATE = 128
SSD_CONV = 4
SSD_CHUNK = 128
SSD_CONV_DIM = SSD_INNER + 2 * SSD_GROUPS * SSD_STATE
N_BRANCH = 3
BRANCH_WIDTH = 512
IN_WIDTHS = (2 * GM_WIDTH, MLA_Q_RANK, MLA_KV_RANK, MLA_ROPE, SSD_INNER, SSD_CONV_DIM, SSD_HEADS, N_BRANCH * D_MODEL)
IN_COLS = sum(IN_WIDTHS)
IN_OFFSETS = tuple(int(v) for v in np.cumsum(IN_WIDTHS)[:-1])


def rms_norm(x, gain):
    xf = x.astype(jnp.float32)
    y = xf * lax.rsqrt(jnp.mean(xf * xf, axis=-1, keepdims=True) + EPS)
    return (y * gain.astype(jnp.float32)).astype(x.dtype)

def swiglu_ffn(h, w_in, w_out):
    gate, up = jnp.split(h @ w_in, 2, axis=-1)
    return (jax.nn.silu(gate) * up) @ w_out

def apply_rope(x, cos, sin):
    x1, x2 = jnp.split(x, 2, axis=-1)
    return jnp.concatenate([x1 * cos - x2 * sin, x2 * cos + x1 * sin], axis=-1)

def gmlp_mixer(uv, v_gain, w_s, b_s):
    bsz, s, _ = uv.shape
    u, v = jnp.split(jax.nn.gelu(uv, approximate=False), 2, axis=-1)
    v = rms_norm(v, v_gain).reshape(bsz, s // GM_CHUNK, GM_CHUNK, GM_GROUPS, GM_GROUP_DIM)
    causal = jnp.tril(jnp.ones((GM_CHUNK, GM_CHUNK), dtype=bool))
    w = jnp.where(causal[None], w_s, 0.0).astype(v.dtype)
    sp = jnp.einsum('gts,bcsgd->bctgd', w, v) + b_s.T[:, :, None].astype(v.dtype)
    return u * sp.reshape(bsz, s, GM_WIDTH)

def blocked_causal_attention(q, k, v):
    bsz, s, nh, dqk = q.shape
    dv = v.shape[-1]
    nb = s // Q_BLOCK
    scale = dqk ** -0.5
    qb = q.reshape(bsz, nb, Q_BLOCK, nh, dqk).transpose(1, 0, 3, 2, 4)
    kt = k.transpose(0, 2, 1, 3)
    vt = v.transpose(0, 2, 1, 3)
    kpos = jnp.arange(s)

    def one_block(args):
        qi, i = args
        sc = jnp.einsum('bhqd,bhkd->bhqk', qi, kt, preferred_element_type=jnp.float32) * scale
        qpos = i * Q_BLOCK + jnp.arange(Q_BLOCK)
        sc = jnp.where(kpos[None, :] <= qpos[:, None], sc, -jnp.inf)
        p = jax.nn.softmax(sc, axis=-1).astype(vt.dtype)
        return jnp.einsum('bhqk,bhkd->bhqd', p, vt)

    out = lax.map(one_block, (qb, jnp.arange(nb)))
    return out.transpose(1, 0, 3, 2, 4).reshape(bsz, s, nh * dv)

def mla_mixer(c_q, c_kv, k_rope, cos, sin, q_norm, kv_norm, w_uq, w_ukv, q_gain, k_gain):
    bsz, s, _ = c_q.shape
    q = (rms_norm(c_q, q_norm) @ w_uq).reshape(bsz, s, MLA_HEADS, MLA_QK_DIM)
    kv = (rms_norm(c_kv, kv_norm) @ w_ukv).reshape(bsz, s, MLA_HEADS, MLA_NOPE + MLA_V)
    k_nope, v = jnp.split(kv, [MLA_NOPE], axis=-1)
    k_pe = jnp.broadcast_to(k_rope[:, :, None, :], (bsz, s, MLA_HEADS, MLA_ROPE))
    k = jnp.concatenate([k_nope, k_pe], axis=-1)
    q = rms_norm(q, q_gain)
    k = rms_norm(k, k_gain)
    q = jnp.concatenate([q[..., :MLA_NOPE], apply_rope(q[..., MLA_NOPE:], cos, sin)], axis=-1)
    k = jnp.concatenate([k[..., :MLA_NOPE], apply_rope(k[..., MLA_NOPE:], cos, sin)], axis=-1)
    return blocked_causal_attention(q, k, v)

def segsum(a):
    t = a.shape[-1]
    idx = jnp.arange(t)
    ax = jnp.where(idx[:, None] > idx[None, :], a[..., :, None], 0.0)
    ss = jnp.cumsum(ax, axis=-2)
    return jnp.where(idx[:, None] >= idx[None, :], ss, -jnp.inf)

def ssd_scan(xs, dt, a_log, b_in, c_in):
    bsz, s, nh, hp = xs.shape
    ng, ns = b_in.shape[2], b_in.shape[3]
    nr = nh // ng
    nc = s // SSD_CHUNK
    a = -jnp.exp(a_log.astype(jnp.float32))
    da = (dt * a).reshape(bsz, nc, SSD_CHUNK, ng, nr).transpose(0, 3, 4, 1, 2)
    xdt = (xs * dt[..., None].astype(xs.dtype)).reshape(bsz, nc, SSD_CHUNK, ng, nr, hp)
    bc = b_in.reshape(bsz, nc, SSD_CHUNK, ng, ns)
    cc = c_in.reshape(bsz, nc, SSD_CHUNK, ng, ns)
    cs = jnp.cumsum(da, axis=-1)
    dt_ = xs.dtype
    lmat = jnp.exp(segsum(da)).astype(dt_)
    cb = jnp.einsum('bclgn,bcsgn->bgcls', cc, bc)
    y_diag = jnp.einsum('bgrcls,bcsgrp->bclgrp', cb[:, :, None] * lmat, xdt)
    decay_states = jnp.exp(cs[..., -1:] - cs).astype(dt_)
    states = jnp.einsum('bclgn,bgrcl,bclgrp->bcgrpn', bc, decay_states, xdt)
    chunk_tot = jnp.pad(cs[..., -1], ((0, 0), (0, 0), (0, 0), (1, 0)))
    decay_chunk = jnp.exp(segsum(chunk_tot)).astype(dt_)
    states0 = jnp.concatenate([jnp.zeros_like(states[:, :1]), states], axis=1)
    new_states = jnp.einsum('bgrzc,bcgrpn->bzgrpn', decay_chunk, states0)
    states_in = new_states[:, :-1]
    y_off = jnp.einsum('bclgn,bcgrpn,bgrcl->bclgrp', cc, states_in, jnp.exp(cs).astype(dt_))
    return (y_diag + y_off).reshape(bsz, s, nh, hp)

def ssd_mixer(z, xbc, dt_raw, conv_w, conv_b, dt_bias, a_log, d_skip, norm_gain):
    bsz, s, _ = xbc.shape
    xbc = lax.conv_general_dilated(xbc, conv_w[:, None, :].astype(xbc.dtype), (1,), [(SSD_CONV - 1, 0)],
                                   dimension_numbers=('NWC', 'WIO', 'NWC'), feature_group_count=SSD_CONV_DIM)
    xbc = jax.nn.silu(xbc + conv_b.astype(xbc.dtype))
    xs, b_in, c_in = jnp.split(xbc, [SSD_INNER, SSD_INNER + SSD_GROUPS * SSD_STATE], axis=-1)
    xs = xs.reshape(bsz, s, SSD_HEADS, SSD_HEAD_DIM)
    b_in = b_in.reshape(bsz, s, SSD_GROUPS, SSD_STATE)
    c_in = c_in.reshape(bsz, s, SSD_GROUPS, SSD_STATE)
    dt = jax.nn.softplus(dt_raw.astype(jnp.float32) + dt_bias.astype(jnp.float32))
    y = ssd_scan(xs, dt, a_log, b_in, c_in) + xs * d_skip[:, None].astype(xs.dtype)
    y = y.reshape(bsz, s, SSD_INNER) * jax.nn.silu(z)
    y = rms_norm(y.reshape(bsz, s, SSD_GROUPS, SSD_INNER // SSD_GROUPS), norm_gain.reshape(SSD_GROUPS, -1))
    return y.reshape(bsz, s, SSD_INNER)

def second_inputs(seed: int = 0) -> dict:
    key = jax.random.key(seed)
    ks = jax.random.split(key, 32)
    f32 = jnp.float32

    def nrm(k, shape, scale):
        return jax.random.normal(k, shape, f32) * scale

    def gain(k, shape):
        return 1.0 + 0.05 * jax.random.normal(k, shape, f32)

    L = DEPTH
    x = jax.random.normal(ks[0], (BATCH, SEQ, D_MODEL), f32)
    offsets = jax.random.randint(ks[1], (BATCH, 1), 0, SEQ, dtype=jnp.int32)
    positions = offsets + jnp.arange(SEQ, dtype=jnp.int32)[None, :]
    dt0 = jnp.exp(jax.random.uniform(ks[2], (L, SSD_HEADS), f32, np.log(1e-3), np.log(1e-1)))
    return {
        'x': x,
        'positions': positions,
        'ffn1_norm': gain(ks[3], (L, D_MODEL)),
        'ffn1_w_in': nrm(ks[4], (L, D_MODEL, 2 * D_FF), D_MODEL ** -0.5),
        'ffn1_w_out': nrm(ks[5], (L, D_FF, D_MODEL), D_FF ** -0.5),
        'mix_norm': gain(ks[6], (L, D_MODEL)),
        'w_in': nrm(ks[7], (L, D_MODEL, IN_COLS), D_MODEL ** -0.5),
        'gm_v_norm': gain(ks[8], (L, GM_WIDTH)),
        'gm_w_s': nrm(ks[9], (L, GM_GROUPS, GM_CHUNK, GM_CHUNK), 0.5 * GM_CHUNK ** -0.5),
        'gm_b_s': 1.0 + 0.1 * jax.random.normal(ks[10], (L, GM_GROUPS, GM_CHUNK), f32),
        'mla_q_norm': gain(ks[11], (L, MLA_Q_RANK)),
        'mla_kv_norm': gain(ks[12], (L, MLA_KV_RANK)),
        'mla_w_uq': nrm(ks[13], (L, MLA_Q_RANK, MLA_HEADS * MLA_QK_DIM), MLA_Q_RANK ** -0.5),
        'mla_w_ukv': nrm(ks[14], (L, MLA_KV_RANK, MLA_HEADS * (MLA_NOPE + MLA_V)), MLA_KV_RANK ** -0.5),
        'mla_q_gain': gain(ks[15], (L, MLA_QK_DIM)),
        'mla_k_gain': gain(ks[16], (L, MLA_QK_DIM)),
        'ssd_conv_w': nrm(ks[17], (L, SSD_CONV, SSD_CONV_DIM), SSD_CONV ** -0.5),
        'ssd_conv_b': nrm(ks[18], (L, SSD_CONV_DIM), 0.02),
        'ssd_dt_bias': dt0 + jnp.log(-jnp.expm1(-dt0)),
        'ssd_a_log': jnp.log(jax.random.uniform(ks[19], (L, SSD_HEADS), f32, 1.0, 16.0)),
        'ssd_d': 1.0 + 0.1 * jax.random.normal(ks[20], (L, SSD_HEADS), f32),
        'ssd_norm': gain(ks[21], (L, SSD_INNER)),
        'w_branch': nrm(ks[22], (L, N_BRANCH, BRANCH_WIDTH, D_MODEL), BRANCH_WIDTH ** -0.5),
        'w_out': nrm(ks[23], (L, D_MODEL, D_MODEL), D_MODEL ** -0.5),
        'ffn2_norm': gain(ks[24], (L, D_MODEL)),
        'ffn2_w_in': nrm(ks[25], (L, D_MODEL, 2 * D_FF), D_MODEL ** -0.5),
        'ffn2_w_out': nrm(ks[26], (L, D_FF, D_MODEL), D_FF ** -0.5),
    }

def second_block(x, positions, ffn1_norm, ffn1_w_in, ffn1_w_out, mix_norm, w_in, gm_v_norm, gm_w_s, gm_b_s,
              mla_q_norm, mla_kv_norm, mla_w_uq, mla_w_ukv, mla_q_gain, mla_k_gain,
              ssd_conv_w, ssd_conv_b, ssd_dt_bias, ssd_a_log, ssd_d, ssd_norm,
              w_branch, w_out, ffn2_norm, ffn2_w_in, ffn2_w_out):
    bsz, s, _ = x.shape
    inv_freq = 1.0 / (ROPE_THETA ** (jnp.arange(0, MLA_ROPE, 2, dtype=jnp.float32) / MLA_ROPE))
    ang = positions.astype(jnp.float32)[..., None] * inv_freq
    cos = jnp.cos(ang)[:, :, None, :].astype(x.dtype)
    sin = jnp.sin(ang)[:, :, None, :].astype(x.dtype)
    for l in range(DEPTH):
        x = x + FFN_RESID * swiglu_ffn(rms_norm(x, ffn1_norm[l]), ffn1_w_in[l], ffn1_w_out[l])
        h = rms_norm(x, mix_norm[l])
        uv, c_q, c_kv, k_rope, z, xbc, dt_raw, gates = jnp.split(h @ w_in[l], IN_OFFSETS, axis=-1)
        y_a = gmlp_mixer(uv, gm_v_norm[l], gm_w_s[l], gm_b_s[l])
        y_b = mla_mixer(c_q, c_kv, k_rope, cos, sin, mla_q_norm[l], mla_kv_norm[l], mla_w_uq[l], mla_w_ukv[l],
                        mla_q_gain[l], mla_k_gain[l])
        y_c = ssd_mixer(z, xbc, dt_raw, ssd_conv_w[l], ssd_conv_b[l], ssd_dt_bias[l], ssd_a_log[l], ssd_d[l],
                        ssd_norm[l])
        g = jax.nn.sigmoid(gates).reshape(bsz, s, N_BRANCH, D_MODEL)
        merged = (g[:, :, 0] * (y_a @ w_branch[l, 0])
                  + g[:, :, 1] * (y_b @ w_branch[l, 1])
                  + g[:, :, 2] * (y_c @ w_branch[l, 2]))
        x = x + merged @ w_out[l]
        x = x + FFN_RESID * swiglu_ffn(rms_norm(x, ffn2_norm[l]), ffn2_w_in[l], ffn2_w_out[l])
    return x


def setup_inputs(seed=0):
    out = dict(first_inputs(seed))
    for name, value in second_inputs(seed + 1).items():
        if name != "x":
            out[name + "_2"] = value
    return out


def reference(
    x, c, w_ada, b_ada, ln_g, ln_b, a_w_in, a_conv_w, a_conv_b, a_wq, a_wk, a_wv, a_w_if,
    a_b_if, a_gn_g, a_skip, a_w_out, b_w_kv, b_wq, b_wo, moe_w_router, moe_b_router, moe_w_gate,
    moe_w_up, moe_w_down, positions_2, ffn1_norm_2, ffn1_w_in_2, ffn1_w_out_2, mix_norm_2,
    w_in_2, gm_v_norm_2, gm_w_s_2, gm_b_s_2, mla_q_norm_2, mla_kv_norm_2, mla_w_uq_2,
    mla_w_ukv_2, mla_q_gain_2, mla_k_gain_2, ssd_conv_w_2, ssd_conv_b_2, ssd_dt_bias_2,
    ssd_a_log_2, ssd_d_2, ssd_norm_2, w_branch_2, w_out_2, ffn2_norm_2, ffn2_w_in_2,
    ffn2_w_out_2,
):
    x = first_block(
        x, c, w_ada, b_ada, ln_g, ln_b, a_w_in, a_conv_w, a_conv_b, a_wq, a_wk, a_wv, a_w_if,
        a_b_if, a_gn_g, a_skip, a_w_out, b_w_kv, b_wq, b_wo, moe_w_router, moe_b_router,
        moe_w_gate, moe_w_up, moe_w_down,
    )
    return second_block(
        x, positions_2, ffn1_norm_2, ffn1_w_in_2, ffn1_w_out_2, mix_norm_2, w_in_2, gm_v_norm_2,
        gm_w_s_2, gm_b_s_2, mla_q_norm_2, mla_kv_norm_2, mla_w_uq_2, mla_w_ukv_2, mla_q_gain_2,
        mla_k_gain_2, ssd_conv_w_2, ssd_conv_b_2, ssd_dt_bias_2, ssd_a_log_2, ssd_d_2,
        ssd_norm_2, w_branch_2, w_out_2, ffn2_norm_2, ffn2_w_in_2, ffn2_w_out_2,
    )


_drawn_inputs = setup_inputs


def setup_inputs(seed=0):
    import zlib

    import numpy as np

    out = dict(_drawn_inputs(seed))
    spreads = {}
    factors = {'a_gn_g': 8.0,
     'a_skip': 8.0,
     'gm_v_norm_2': 7.39,
     'mla_q_norm_2': 8.0,
     'mla_kv_norm_2': 5.56,
     'mla_q_gain_2': 8.0,
     'mla_k_gain_2': 8.0,
     'ssd_conv_b_2': 3.019}
    for name, (base, spread) in spreads.items():
        noise = np.random.default_rng([zlib.crc32(name.encode()), seed]).standard_normal(out[name].shape)
        drawn = base * np.exp(spread * noise) if base else spread * noise
        out[name] = __import__('jax').numpy.asarray(drawn.astype(out[name].dtype))
    for name, factor in factors.items():
        out[name] = (out[name] * factor).astype(out[name].dtype)
    return out
```

```python
from contextlib import ExitStack

import numpy as np

import concourse.bass as bass
from concourse import mybir

F32 = mybir.dt.float32
I32 = mybir.dt.int32
ALU = mybir.AluOpType
ACT = mybir.ActivationFunctionType
AX = mybir.AxisListType

P = 128
T = 256
TT = T // P
D = 1024
DC = D // P
DEPTH = 2
ALPHA = float(np.float32((2.0 * DEPTH) ** 0.25))
LN_EPS = 1e-5
RMS_EPS = 1e-6
NEG = -1e30

NH = 4
DI = 2 * D
DIC = DI // P
DH = DI // NH
DHC = DH // P
CONV = 4
PAD = CONV - 1
AH = 16
AD = D // AH
NE = 16
NGRP = 4
EPG = NE // NGRP
FE = 512
FF = 2816
GMW = 512
GMG = 4
QR = 384
KVR = 256
MH = 8
NOPE = 64
ROPE = 32
HR = ROPE // 2
QK = NOPE + ROPE
MV = 64
SH = 8
SHD = 64
SI = SH * SHD
SG = 2
XBC = SI + 2 * SG * P
O_U, O_V, O_CQ, O_CKV, O_KR = 0, GMW, 2 * GMW, 2 * GMW + QR, 2 * GMW + QR + KVR
O_Z = O_KR + ROPE
O_XBC = O_Z + SI
O_DT = O_XBC + XBC
O_G = O_DT + SH
NB = 3

WSLOTS = 4
WCOLS = DC * (512 + SH)
ADA_FIRST = 6
ADA_IN = [list(range(ADA_FIRST + 2 * n, ADA_FIRST + 2 * n + 2)) for n in range(8)]
ADA_QKV = [[22, 23], [24, 25], [26, 27], []]
HB = 128
BODY = 4

TABLE = [
    [("b_ada", 112), ("c", 8), ("kvn", 4)],
    [("ln_g", 32), ("ln_b", 32), ("conv_w", 64)],
    [("conv_b", 16), ("gn_g", 16), ("skip", 16), ("ffn1", 16), ("mix", 16), ("ffn2", 16), ("gmv", 8), ("ssdn", 8),
     ("qn", 6)],
    [("conv_w2", 64), ("conv_b2", 16)],
]

SOURCES = {"b_ada": "b_ada", "c": "c", "kvn": "mla_kv_norm_2", "ln_g": "ln_g", "ln_b": "ln_b", "conv_w": "a_conv_w",
           "conv_b": "a_conv_b", "gn_g": "a_gn_g", "skip": "a_skip", "ffn1": "ffn1_norm_2", "mix": "mix_norm_2",
           "ffn2": "ffn2_norm_2", "gmv": "gm_v_norm_2", "ssdn": "ssd_norm_2", "qn": "mla_q_norm_2",
           "conv_w2": "ssd_conv_w_2", "conv_b2": "ssd_conv_b_2"}


class Signal:

    def __init__(self, sem):
        self.sem, self.seen = sem, {}

    def upto(self, who, n=1):
        self.seen[who] = self.seen.get(who, 0) + n
        return self.seen[who]


def build(nc, A, out):
    ctx = ExitStack()
    with ctx:
        def sb(name, shape, dt=F32):
            return ctx.enter_context(nc.sbuf_tensor(name, shape, dt))

        def sem(name):
            return ctx.enter_context(nc.semaphore(name))

        wring = sb("wring", [P, WSLOTS, WCOLS])
        X = sb("X", [P, DC, T])
        H = sb("H", [P, DC, T])
        H2 = sb("H2", [P, DC, T])
        SQ = sb("SQ", [P, DC, T])
        arena = sb("arena", [P, 18904])
        pcol = sb("pcol", [P, 4, P])
        ident = sb("ident", [P, P])
        ones = sb("ones", [P, P])
        upper = sb("upper", [P, TT, T])
        strict = sb("strict", [P, TT, T])
        neg_st = sb("neg_st", [P, TT, T])
        neg_qk = sb("neg_qk", [P, TT, T])
        alibi = sb("alibi", [P, TT, T])
        sel = sb("sel", [NE, NE, P])
        mods = sb("mods", [P, 112])
        cT = sb("cT", [P, DC])
        gmw = sb("gmw", [P, DEPTH, GMG, P])
        bsb = sb("bsb", [P, DEPTH, GMG, P])
        gainb = sb("gainb", [P, 2, DEPTH, QK])
        wr = sb("wr", [P, DC, NE])
        wif = sb("wif", [P, DIC, 2 * NH])
        bif = sb("bif", [NH, 2])
        brb = sb("brb", [P, NE])
        dtb = sb("dtb", [P, DEPTH, SH])
        alb = sb("alb", [P, DEPTH, SH])
        dsk = sb("dsk", [P, DEPTH, SI // P])
        posi = sb("posi", [P, TT], I32)
        posf = sb("posf", [P, TT])
        invf = sb("invf", [P, HR])
        trig = sb("trig", [P, 2, TT, HR])
        rank4 = sb("rank4", [P, NGRP])
        rank16 = sb("rank16", [P, NE])
        eps_ln = sb("eps_ln", [P, 1])
        eps_rms = sb("eps_rms", [P, 1])
        one_c = sb("one_c", [P, 1])
        nrm = sb("nrm", [P, 2, T])
        sm = sb("sm", [P, 540])

        bank = [ctx.enter_context(nc.psum_tensor(f"bank{i}", [P, 512], F32)) for i in range(4)]
        yacc = [ctx.enter_context(nc.psum_tensor(f"yacc{i}", [P, 512], F32)) for i in range(4)]

        def ysum(m):
            return yacc[m // 2][:, (m % 2) * T:(m % 2 + 1) * T]

        def view(off, *shape, parts=P):
            n = int(np.prod(shape))
            v = arena[0:parts, off:off + n]
            if len(shape) == 2:
                return v.rearrange("p (a b) -> p a b", a=shape[0])
            if len(shape) == 3:
                return v.rearrange("p (a b c) -> p a b c", a=shape[0], b=shape[1])
            return v

        col = {}
        for t, rows in enumerate(TABLE):
            r = 0
            for name, n in rows:
                col[name] = (t, r)
                r += n

        def vec(name, i):
            t, r = col[name]
            return pcol[:, t, r + i:r + i + 1]

        def mod(layer, s, which, k):
            i = ((layer * 2 + s) * 3 + which) * DC + k
            return mods[:, i:i + 1]

        def kvmod(which, k):
            i = DEPTH * 6 * DC + which * DC + k
            return mods[:, i:i + 1]

        w_landed = [sem(f"w_landed{i}") for i in range(WSLOTS)]
        bank_full = [sem(f"bank_full{i}") for i in range(4)]
        bank_drained = [sem(f"bank_drained{i}") for i in range(4)]
        consts_made = sem("consts_made")
        rows_landed = sem("rows_landed")
        small_landed = sem("small_landed")
        x_landed = sem("x_landed")
        out_landed = sem("out_landed")
        pool_steps = sem("pool_steps")
        act_steps = sem("act_steps")
        dve_steps = sem("dve_steps")
        consts_derived = sem("consts_derived")
        c_ready = sem("c_ready")
        ada_done = Signal(sem("ada_done"))
        h_ready = Signal(sem("h_ready"))
        h2_ready = Signal(sem("h2_ready"))
        x_ready = Signal(sem("x_ready"))
        sum_ready = Signal(sem("sum_ready"))
        centered = Signal(sem("centered"))
        squared = Signal(sem("squared"))
        conv_summed = Signal(sem("conv_summed"))
        conv_ready = Signal(sem("conv_ready"))
        pad_cleared = Signal(sem("pad_cleared"))
        exp_ready = Signal(sem("exp_ready"))
        plus_one = Signal(sem("plus_one"))
        ln_ready = Signal(sem("ln_ready"))
        rows_made = Signal(sem("rows_made"))
        stab_ready = Signal(sem("stab_ready"))
        emt_ready = Signal(sem("emt_ready"))
        dlog_ready = Signal(sem("dlog_ready"))
        wexp_ready = Signal(sem("wexp_ready"))
        head_ready = Signal(sem("head_ready"))
        hc_ready = Signal(sem("hc_ready"))
        hsq_ready = Signal(sem("hsq_ready"))
        router_exp = Signal(sem("router_exp"))
        route_ready = Signal(sem("route_ready"))
        silu_ready = Signal(sem("silu_ready"))
        scaled_ready = Signal(sem("scaled_ready"))
        down_done = Signal(sem("down_done"))
        score_ready = Signal(sem("score_ready"))
        prob_exp = Signal(sem("prob_exp"))
        prob_ready = Signal(sem("prob_ready"))
        rope_in = Signal(sem("rope_in"))
        rope_ready = Signal(sem("rope_ready"))
        vsq_ready = Signal(sem("vsq_ready"))
        vn_ready = Signal(sem("vn_ready"))
        sp_ready = Signal(sem("sp_ready"))
        qksq_ready = Signal(sem("qksq_ready"))
        qkss_ready = Signal(sem("qkss_ready"))
        qkstd_ready = Signal(sem("qkstd_ready"))
        qkrot_ready = Signal(sem("qkrot_ready"))
        lat_ready = Signal(sem("lat_ready"))
        abs_ready = Signal(sem("abs_ready"))
        aexp_ready = Signal(sem("aexp_ready"))
        decay_in = Signal(sem("decay_in"))
        decay_ready = Signal(sem("decay_ready"))
        sp_mm_ready = Signal(sem("sp_mm_ready"))
        yz_ready = Signal(sem("yz_ready"))
        yc_ready = Signal(sem("yc_ready"))
        merged_ready = Signal(sem("merged_ready"))
        ysilu_ready = Signal(sem("ysilu_ready"))

        N_CONST = 1
        N_SMALL = 15

        uses = {}
        freed = []
        tags = []

        def bank_of(name):
            return bank[uses[name] % 4]

        def full(name):
            k = uses[name]
            return bank_full[k % 4], k // 4 + 1

        def drained(name):
            k = uses[name]
            return bank_drained[k % 4], k // 4 + 1

        def drain_sem(name):
            return bank_drained[uses[name] % 4]

        prow = view(0, 4, P)
        xin = view(512, TT, D)
        xm = view(0, DIC, PAD + T)
        xc = view(4144, DIC, T)
        sz = view(8240, DIC, T)
        qm = view(12336, DHC, T)
        km = view(13360, DHC, T)
        Pm = [view(14384 + 512 * i, TT, T) for i in range(2)]
        Wm = [view(15408 + 512 * i, TT, T) for i in range(2)]
        lrow = [view(16432 + T * i, T, parts=NH) for i in range(8)]
        den_s = view(18480, T)

        def vm(h, i):
            c = 4 * (h % 2) + 2 * i
            return SQ[:, c:c + 2, :].rearrange("p a t -> p (a t)")

        hm = H2[:, 0:DHC, :]
        hsq = H2[:, DHC:2 * DHC, :]
        gbc = view(0, NE, T)
        sg = [view(4096 + 256 * i, T) for i in range(2)]
        sgw = [view(4608 + 256 * i, T) for i in range(2)]
        hid = [view(5120 + 256 * i, T) for i in range(2)]
        gT = view(5632, T, parts=NE)
        qa = view(0, DC, T)
        ka = view(2048, DC, T)
        va = view(4096, TT, D)
        oa = view(6144, DC, T)
        Es = [view(15832 + 512 * i, TT, T) for i in range(2)]
        Ss = [view(16856 + 512 * i, TT, T) for i in range(2)]
        PTs = [view(17880 + 512 * i, TT, T) for i in range(2)]
        yA, yB, yC = (view(1024 * i, 4, T) for i in range(3))
        zs = view(3072, 4, T)
        xb = view(4096, 8, PAD + T)
        xv = view(6168, 8, T)
        us = view(8216, 4, T)
        vn = view(9240, TT, GMW)
        cq = view(10264, 3, T)
        ckv = view(11032, 2, T)
        krs = view(11544, TT, ROPE)
        wT = view(11608, GMG, P)
        Vt = view(12120, TT, MH * MV)
        O2 = 12760 + 384
        Qt = view(O2, TT, MH, QK)
        Kt = view(O2 + 1536, TT, MH, QK)
        qksq = view(O2 + 3072, 1536)
        rt = [view(O2 + 4608 + T * i, TT, MH, HR) for i in range(4)]
        QT, KT = H2, SQ
        xdt = view(O2, TT, SI)
        Mh = [view(O2 + 1024 + 512 * i, TT, T) for i in range(2)]
        Eh = [view(O2 + 2048 + 512 * i, TT, T) for i in range(2)]
        Ph = [view(O2 + 3072 + 512 * i, TT, T) for i in range(2)]
        CB = [view(O2 + 4096 + 512 * i, TT, T) for i in range(SG)]
        sig = [view(O2 + 2048 * i, DC, T) for i in range(2)]
        xo = view(0, TT, D)

        block = ctx.enter_context(nc.Block())

        @block.tensor
        def _(pe):
            mm = nc.tensor.matmul

            def fill(name):
                k = len(uses)
                uses[name] = k
                if k >= 4:
                    pe.wait_ge(bank_drained[k % 4], k // 4)
                return bank[k % 4]

            def filled(name, ins):
                ins.then_inc(bank_full[uses[name] % 4], 1)

            def weights(tag):
                u = len(tags)
                tags.append(tag)
                freed.append(None)
                pe.wait_ge(w_landed[u % WSLOTS], 48 * (u // WSLOTS + 1))
                return wring[:, u % WSLOTS, :]

            def used_by(name):
                freed[-1] = full(name)

            def product(name, w, rhs, fresh=None, part=P):
                b = fill(name)
                n = w.shape[1]
                for k in range(n):
                    if fresh is not None:
                        pe.wait_ge(fresh.sem, fresh.upto("pe"))
                    last = mm(b[0:part, 0:T], w[:, k, :], rhs[:, k, :], start=(k == 0), stop=(k == n - 1))
                filled(name, last)

            def column_sums(name, src, n, fresh=None, moved=None):
                b = fill(name)
                for k in range(n):
                    if fresh is not None:
                        pe.wait_ge(fresh.sem, fresh.upto("pe"))
                    if moved is not None:
                        pe.wait_ge(*drained(f"{moved}{k}"))
                    last = mm(b[:, 0:T], ones[:, :], src[:, k, :], start=(k == 0), stop=(k == n - 1))
                filled(name, last)

            pe.wait_ge(consts_made, N_CONST)
            pe.wait_ge(rows_landed, 16 * sum(len(r) for r in TABLE))
            for t, rows in enumerate(TABLE):
                n = sum(m for _, m in rows)
                b = fill(f"table{t}")
                filled(f"table{t}", nc.tensor.transpose(b[:, 0:n], prow[0:n, t, :], ident[0:n, 0:n]))
            pe.wait_ge(x_landed, 16)
            for kk in range(DC // 2):
                b = fill(f"x{kk}")
                for k in range(2 * kk, 2 * kk + 2):
                    for i in range(TT):
                        o = (k % 2) * T + i * P
                        last = nc.tensor.transpose(b[:, o:o + P], xin[:, i, k * P:(k + 1) * P], ident[:, :])
                filled(f"x{kk}", last)

            def ada_unit(n):
                w = weights(f"ada{n}")[:, 0:DC * 512].rearrange("p (k n) -> p k n", k=DC)
                b = yacc[0] if n < ADA_FIRST else yacc[1]
                for m in range(4):
                    c = n * 4 + m
                    for k in range(DC):
                        last = mm(b[:, c:c + 1], w[:, k, m * P:(m + 1) * P], cT[:, k:k + 1],
                                  start=(k == 0), stop=(k == DC - 1))
                last.then_inc(ada_done.sem, 1)
                freed[-1] = (ada_done.sem, n + 1)

            pe.wait_ge(c_ready, 1)
            for n in range(ADA_FIRST):
                ada_unit(n)

            for n in range(2 * DI // 512):
                w = weights(f"a_w_in{n}")[:, 0:DC * 512].rearrange("p (k n) -> p k n", k=DC)
                for m in range(4):
                    product(f"w_in{4 * n + m}", w[:, :, m * P:(m + 1) * P], H, h_ready if n + m == 0 else None)
                used_by(f"w_in{4 * n + 3}")
                for a in ADA_IN[n]:
                    ada_unit(a)
            pe.wait_ge(small_landed, 16 * N_SMALL)
            pe.wait_ge(conv_ready.sem, conv_ready.upto("pe", DIC))
            for g in range(2):
                b = fill(f"gate{g}")
                for k in range(DIC):
                    last = mm(b[0:NH, 0:T], wif[:, k, g * NH:(g + 1) * NH], xc[:, k, :],
                              start=(k == 0), stop=(k == DIC - 1))
                filled(f"gate{g}", last)

            def mlstm_num(h):
                pe.wait_ge(*drained(f"mS{h}"))
                b = fill(f"den{h}")
                mm(b[:, 0:T], ones[:, :], Pm[h % 2][:, 0, :], start=True, stop=False)
                filled(f"den{h}", mm(b[:, P:T], ones[:, :], Pm[h % 2][:, 1, P:T], start=False, stop=True))
                pe.wait_ge(*drained(f"v{h}.0"))
                pe.wait_ge(*drained(f"v{h}.1"))
                for a in range(2):
                    b = fill(f"num{h}.{a}")
                    for m in range(2 * a, 2 * a + 2):
                        o = (m % 2) * T
                        mm(b[:, o:o + T], vm(h, 0)[:, m * P:(m + 1) * P], Pm[h % 2][:, 0, :], start=True, stop=False)
                        last = mm(b[:, o + P:o + T], vm(h, 1)[:, m * P:(m + 1) * P], Pm[h % 2][:, 1, P:T],
                                  start=False, stop=True)
                    filled(f"num{h}.{a}", last)

            def mlstm_mean(h):
                for a in range(2):
                    pe.wait_ge(*drained(f"num{h}.{a}"))
                column_sums(f"gmean{h}", hm, DHC)

            def mlstm_var(h):
                pe.wait_ge(hsq_ready.sem, hsq_ready.upto("pe"))
                column_sums(f"gvar{h}", hsq, DHC)

            for h in range(NH):
                c = DHC * h
                w = weights(f"qk{h}")[:, 0:2 * DHC * DH].rearrange("p (g k n) -> p g k n", g=2, k=DHC)
                for m in range(DHC):
                    product(f"q{h}.{m}", w[:, 0, :, m * P:(m + 1) * P], xc[:, c:c + DHC, :])
                if h > 0:
                    mlstm_num(h - 1)
                for m in range(DHC):
                    product(f"k{h}.{m}", w[:, 1, :, m * P:(m + 1) * P], xc[:, c:c + DHC, :])
                used_by(f"k{h}.{DHC - 1}")
                if h > 0:
                    mlstm_mean(h - 1)
                w = weights(f"v{h}")[:, 0:DHC * DH].rearrange("p (k n) -> p k n", k=DHC)
                for i in range(TT):
                    b = fill(f"v{h}.{i}")
                    for k in range(DHC):
                        last = mm(b[:, :], xm[:, c + k, PAD + i * P:PAD + (i + 1) * P], w[:, k, :],
                                  start=(k == 0), stop=(k == DHC - 1))
                    filled(f"v{h}.{i}", last)
                used_by(f"v{h}.{TT - 1}")
                if h == 0:
                    pe.wait_ge(stab_ready.sem, stab_ready.upto("pe"))
                    b = fill("ucol")
                    for i in range(TT):
                        last = nc.tensor.transpose(b[:, i * NH:(i + 1) * NH], lrow[3][:, i * P:(i + 1) * P],
                                                   ident[0:NH, 0:NH])
                    filled("ucol", last)
                else:
                    mlstm_var(h - 1)
                for a in ADA_QKV[h]:
                    ada_unit(a)
                for m in range(DHC):
                    pe.wait_ge(*drained(f"q{h}.{m}"))
                    pe.wait_ge(*drained(f"k{h}.{m}"))
                b = fill(f"mS{h}")
                for k in range(DHC):
                    mm(b[:, 0:T], km[:, k, 0:P], qm[:, k, :], start=(k == 0), stop=(k == DHC - 1))
                for k in range(DHC):
                    last = mm(b[:, T + P:2 * T], km[:, k, P:T], qm[:, k, P:T], start=(k == 0), stop=(k == DHC - 1))
                filled(f"mS{h}", last)
                if h == 0:
                    pe.wait_ge(emt_ready.sem, emt_ready.upto("pe"))
                b = fill(f"mbc{h}")
                mm(b[:, 0:T], sel[0:NH, h, :], lrow[5][:, :], start=True, stop=True)
                filled(f"mbc{h}", mm(b[:, T:2 * T], sel[0:NH, h, :], lrow[6][:, :], start=True, stop=True))
            mlstm_num(NH - 1)
            mlstm_mean(NH - 1)
            mlstm_var(NH - 1)
            for n in range(D // 256):
                w = weights(f"a_w_out{n}")[:, 0:DIC * 256].rearrange("p (k n) -> p k n", k=DIC)
                if n == 0:
                    pe.wait_ge(head_ready.sem, head_ready.upto("pe", NH))
                for m in range(2):
                    product(f"y0.{2 * n + m}", w[:, :, m * P:(m + 1) * P], xc)
                used_by(f"y0.{2 * n + 1}")

            def layer_norm(tag, y=None):
                column_sums(f"{tag}.mean", X, DC, None if y else sum_ready, y)
                column_sums(f"{tag}.var", SQ, DC, squared)

            def rms_norm(tag):
                column_sums(f"{tag}.ms", SQ, DC, squared)

            def swiglu(tag, steps, fresh=None):
                u0, k0, d0 = len(tags), len(uses), down_done.upto("base", 0)

                def up(i, j, fresh=None):
                    u, k = u0 + j, k0 + j
                    w = wring[:, u % WSLOTS, 0:2 * DC * HB].rearrange("p (g k n) -> p g k n", g=2, k=DC)
                    pe.wait_ge(w_landed[u % WSLOTS], i * 48 + 48 * (u // WSLOTS + 1))
                    pe.wait_ge(bank_drained[k % 4], i + k // 4)
                    b = bank[k % 4]
                    for g in range(2):
                        for c in range(DC):
                            if fresh is not None and g == 0:
                                pe.wait_ge(fresh.sem, fresh.upto("pe"))
                            last = mm(b[:, g * T:(g + 1) * T], w[:, g, c, :], H[:, c, :],
                                      start=(c == 0), stop=(c == DC - 1))
                    last.then_inc(bank_full[k % 4], 1)

                def down(i, j, first=False, final=False):
                    u, k = u0 + j, k0 + j
                    w = wring[:, u % WSLOTS, 2 * DC * HB:2 * DC * HB + D]
                    pe.wait_ge(bank_drained[k % 4], i + k // 4 + 1)
                    for m in range(DC):
                        last = mm(ysum(m), w[:, m * P:(m + 1) * P], hid[j % 2], start=first and m % 2 == 0,
                                  stop=final and m % 2 == 1, skip_group_check=True)
                    last.then_inc(down_done.sem, 1)

                up(0, 0, fresh)
                turns, rest = divmod(steps - 1, BODY)
                for j in range(BODY):
                    up(0, j + 1)
                    down(0, j, first=(j == 0))
                with pe.Fori(1, turns) as i:
                    for j in range(BODY):
                        up(i, j + 1)
                        down(i, j)
                for j in range(rest):
                    up(turns, j + 1)
                    down(turns, j)
                down(turns, rest, final=True)
                for s in range(steps):
                    uses[f"{tag}.{s}"] = k0 + s
                    tags.append(f"{tag}.{s}")
                    freed.append((down_done.sem, d0 + s + 1))
                down_done.upto("base", steps)

            def routing(l):
                b = fill(f"logits{l}")
                for i in range(TT):
                    for k in range(DC):
                        if i == 0:
                            pe.wait_ge(h_ready.sem, h_ready.upto("pe"))
                        last = mm(b[:, i * NE:(i + 1) * NE], H[:, k, i * P:(i + 1) * P], wr[:, k, :],
                                  start=(k == 0), stop=(k == DC - 1))
                filled(f"logits{l}", last)
                pe.wait_ge(route_ready.sem, route_ready.upto("pe"))
                b = fill(f"gT{l}")
                for i in range(TT):
                    last = nc.tensor.transpose(b[0:NE, i * P:(i + 1) * P], sm[:, i * NE:(i + 1) * NE], ident[:, :])
                filled(f"gT{l}", last)
                pe.wait_ge(*drained(f"gT{l}"))
                for e in range(0, NE, 2):
                    b = fill(f"gb{l}.{e}")
                    for o in range(2):
                        last = mm(b[:, o * T:(o + 1) * T], sel[:, e + o, :], gT, start=True, stop=True)
                    filled(f"gb{l}.{e}", last)

            def attention(tag, heads, q_of, k_of, v_of):
                def scores(h):
                    b = fill(f"{tag}.s{h}")
                    mm(b[:, 0:P], q_of(h)[:, 0:P], k_of(h)[:, 0:P], start=True, stop=True)
                    filled(f"{tag}.s{h}", mm(b[:, T:2 * T], q_of(h)[:, P:T], k_of(h), start=True, stop=True))

                def turn(h):
                    pe.wait_ge(prob_ready.sem, prob_ready.upto("pe"))
                    b = fill(f"{tag}.p{h}")
                    E = Es[h % 2]
                    nc.tensor.transpose(b[:, 0:P], E[:, 0, 0:P], ident[:, :])
                    nc.tensor.transpose(b[:, P:T], E[:, 1, 0:P], ident[:, :])
                    filled(f"{tag}.p{h}", nc.tensor.transpose(b[:, T + P:2 * T], E[:, 1, P:T], ident[:, :]))

                def values(h):
                    pe.wait_ge(*drained(f"{tag}.p{h}"))
                    b = fill(f"{tag}.o{h}") if h % 2 == 0 else bank_of(f"{tag}.o{h - 1}")
                    r = 64 * (h % 2)
                    mm(b[r:r + 64, 0:T], v_of(h, 0), PTs[h % 2][:, 0, :], start=True, stop=False)
                    last = mm(b[r:r + 64, P:T], v_of(h, 1), PTs[h % 2][:, 1, P:T], start=False, stop=True)
                    if h % 2:
                        filled(f"{tag}.o{h - 1}", last)

                for it in range(heads + 2):
                    if it < heads:
                        scores(it)
                    if 1 <= it <= heads:
                        turn(it - 1)
                    if it >= 2:
                        values(it - 2)

            layer_norm("ln00", "y0.")
            routing(0)
            swiglu("moe0", NE * FE // HB)
            layer_norm("ln01")

            for name, src, fresh in (("k", H2, h2_ready), ("v", H2, None), ("q", H, h_ready)):
                for n in range(2):
                    w = weights(f"b{name}{n}")[:, 0:DC * 512].rearrange("p (k n) -> p k n", k=DC)
                    if name == "v":
                        for i in range(TT):
                            b = fill(f"bv{n}.{i}")
                            for k in range(DC):
                                last = mm(b[:, :], H2[:, k, i * P:(i + 1) * P], w[:, k, :],
                                          start=(k == 0), stop=(k == DC - 1))
                            filled(f"bv{n}.{i}", last)
                        used_by(f"bv{n}.{TT - 1}")
                        continue
                    for m in range(4):
                        product(f"b{name}{4 * n + m}", w[:, :, m * P:(m + 1) * P], src, fresh if n + m == 0 else None)
                    used_by(f"b{name}{4 * n + 3}")
            for m in range(DC):
                pe.wait_ge(*drained(f"bk{m}"))
                pe.wait_ge(*drained(f"bq{m}"))
            for n in range(2):
                for i in range(TT):
                    pe.wait_ge(*drained(f"bv{n}.{i}"))
            attention("moba", AH, lambda h: qa[64 * (h % 2):64 * (h % 2) + 64, h // 2, :],
                      lambda h: ka[64 * (h % 2):64 * (h % 2) + 64, h // 2, :],
                      lambda h, i: va[:, i, h * AD:(h + 1) * AD])
            for n in range(2):
                w = weights(f"bo{n}")[:, 0:DC * 512].rearrange("p (k n) -> p k n", k=DC)
                if n == 0:
                    for h in range(0, AH, 2):
                        pe.wait_ge(*drained(f"moba.o{h}"))
                for m in range(4):
                    product(f"y1.{4 * n + m}", w[:, :, m * P:(m + 1) * P], oa)
                used_by(f"y1.{4 * n + 3}")
            layer_norm("ln10", "y1.")
            routing(1)
            swiglu("moe1", NE * FE // HB)
            layer_norm("ln11")

            for l in range(DEPTH):
                rms_norm(f"f1{l}")
                swiglu(f"f1{l}", FF // HB, h_ready)
                rms_norm(f"mx{l}")
                t = f"m{l}."

                def unit(tag, k, n):
                    return weights(t + tag)[:, 0:k * n].rearrange("p (k n) -> p k n", k=k)

                w = unit("u", DC, GMW)
                for m in range(4):
                    product(f"{t}u{m}", w[:, :, m * P:(m + 1) * P], H, h_ready if m == 0 else None)
                used_by(f"{t}u3")

                def token_major(name, i, w, src, n):
                    b = fill(name)
                    for k in range(w.shape[1]):
                        last = mm(b[:, 0:n], src[:, k, i * P:(i + 1) * P], w[:, k, :],
                                  start=(k == 0), stop=(k == w.shape[1] - 1))
                    filled(name, last)

                w = unit("v", DC, GMW)
                for i in range(TT):
                    token_major(f"{t}v{i}", i, w, H, GMW)
                used_by(f"{t}v1")
                w = unit("cq", DC, QR)
                for m in range(QR // P):
                    product(f"{t}cq{m}", w[:, :, m * P:(m + 1) * P], H)
                used_by(f"{t}cq2")
                w = unit("ckv", DC, KVR + ROPE)
                for m in range(KVR // P):
                    product(f"{t}ckv{m}", w[:, :, m * P:(m + 1) * P], H)
                for i in range(TT):
                    token_major(f"{t}kr{i}", i, w[:, :, KVR:KVR + ROPE], H, ROPE)
                used_by(f"{t}kr1")
                w = unit("z", DC, SI)
                for m in range(4):
                    product(f"{t}z{m}", w[:, :, m * P:(m + 1) * P], H)
                used_by(f"{t}z3")
                w = unit("xbc0", DC, 512)
                for m in range(4):
                    product(f"{t}xbc{m}", w[:, :, m * P:(m + 1) * P], H)
                used_by(f"{t}xbc3")
                w = unit("xbc1", DC, 512 + SH)
                for m in range(4):
                    product(f"{t}xbc{4 + m}", w[:, :, m * P:(m + 1) * P], H)
                b = fill(f"{t}dt")
                for i in range(TT):
                    for k in range(DC):
                        last = mm(b[:, i * SH:(i + 1) * SH], H[:, k, i * P:(i + 1) * P], w[:, k, 512:512 + SH],
                                  start=(k == 0), stop=(k == DC - 1))
                filled(f"{t}dt", last)
                used_by(f"{t}dt")
                for m in range(3):
                    pe.wait_ge(*drained(f"{t}cq{m}"))
                column_sums(f"{t}cqms", SQ, 3)
                for m in range(2):
                    pe.wait_ge(*drained(f"{t}ckv{m}"))
                column_sums(f"{t}ckvms", SQ[:, 3:5, :], 2)
                b = fill(f"{t}wT")
                for g in range(GMG):
                    last = nc.tensor.transpose(b[:, g * P:(g + 1) * P], gmw[:, l, g, :], ident[:, :])
                filled(f"{t}wT", last)
                pe.wait_ge(*drained(f"{t}wT"))
                pe.wait_ge(vn_ready.sem, vn_ready.upto("pe"))
                for g in range(GMG):
                    b = fill(f"{t}sp{g}")
                    for i in range(TT):
                        last = mm(b[:, i * P:(i + 1) * P], vn[:, i, g * P:(g + 1) * P], wT[:, g, :],
                                  start=True, stop=True)
                    filled(f"{t}sp{g}", last)
                w = unit("uq", QR // P, MH * QK)
                pe.wait_ge(lat_ready.sem, lat_ready.upto("pe"))
                for i in range(TT):
                    for g in range(2):
                        token_major(f"{t}q{i}.{g}", i, w[:, :, g * 4 * QK:(g + 1) * 4 * QK], cq, 4 * QK)
                used_by(f"{t}q1.1")
                w = unit("ukv", KVR // P, MH * (NOPE + MV))
                pe.wait_ge(lat_ready.sem, lat_ready.upto("pe"))
                for i in range(TT):
                    for g in range(2):
                        token_major(f"{t}kv{i}.{g}", i, w[:, :, g * 512:(g + 1) * 512], ckv, 512)
                used_by(f"{t}kv1.1")
                for name, src in (("qT", Qt), ("kT", Kt)):
                    pe.wait_ge(qkrot_ready.sem, qkrot_ready.upto("pe"))
                    for c in range(MH // 2):
                        b = fill(f"{t}{name}{c}")
                        for h in range(2):
                            for i in range(TT):
                                o = h * T + i * P
                                last = nc.tensor.transpose(b[0:QK, o:o + P], src[:, i, 2 * c + h, :], ident[:, :])
                        filled(f"{t}{name}{c}", last)
                for name in ("qT", "kT"):
                    for c in range(MH // 2):
                        pe.wait_ge(*drained(f"{t}{name}{c}"))
                attention(f"{t}mla", MH, lambda h: QT[0:QK, h, :], lambda h: KT[0:QK, h, :],
                          lambda h, i: Vt[:, i, h * MV:(h + 1) * MV])
                pe.wait_ge(conv_ready.sem, conv_ready.upto("pe", 8))
                for i in range(TT):
                    b = fill(f"{t}xs{i}")
                    for c in range(4):
                        last = nc.tensor.transpose(b[:, c * P:(c + 1) * P], xv[:, c, i * P:(i + 1) * P], ident[:, :])
                    filled(f"{t}xs{i}", last)
                for g in range(SG):
                    b = fill(f"{t}cb{g}")
                    mm(b[:, 0:T], xv[:, 4 + g, 0:P], xv[:, 6 + g, :], start=True, stop=True)
                    filled(f"{t}cb{g}", mm(b[:, T + P:2 * T], xv[:, 4 + g, P:T], xv[:, 6 + g, P:T],
                                           start=True, stop=True))

                def decays(h):
                    pe.wait_ge(decay_in.sem, decay_in.upto("pe"))
                    b = fill(f"{t}ss{h}")
                    M = Mh[h % 2]
                    mm(b[:, 0:T], M[:, 0, 0:P], upper[:, 0, :], start=True, stop=False)
                    mm(b[:, P:T], M[:, 1, 0:P], upper[:, 1, P:T], start=False, stop=True)
                    filled(f"{t}ss{h}", mm(b[:, T + P:2 * T], M[:, 1, P:T], upper[:, 1, P:T], start=True, stop=True))

                def outputs(h):
                    pe.wait_ge(sp_mm_ready.sem, sp_mm_ready.upto("pe"))
                    b = fill(f"{t}y{h}") if h % 2 == 0 else bank_of(f"{t}y{h - 1}")
                    r = SHD * (h % 2)
                    mm(b[r:r + SHD, 0:T], xdt[:, 0, h * SHD:(h + 1) * SHD], Ph[h % 2][:, 0, :], start=True, stop=False)
                    last = mm(b[r:r + SHD, P:T], xdt[:, 1, h * SHD:(h + 1) * SHD], Ph[h % 2][:, 1, P:T],
                              start=False, stop=True)
                    if h % 2:
                        filled(f"{t}y{h - 1}", last)

                for it in range(SH + 1):
                    if it < SH:
                        decays(it)
                    if it >= 1:
                        outputs(it - 1)
                for g in range(SG):
                    column_sums(f"{t}yms{g}", SQ[:, 2 * g:2 * g + 2, :], 2, ysilu_ready)
                for n in range(NB):
                    for hf in range(2):
                        w = unit(f"g{n}.{hf}", DC, 512)
                        for m in range(4):
                            product(f"{t}g{n}.{4 * hf + m}", w[:, :, m * P:(m + 1) * P], H)
                        used_by(f"{t}g{n}.{4 * hf + 3}")
                    w = unit(f"br{n}", 4, D)
                    if n == 0:
                        pe.wait_ge(sp_ready.sem, sp_ready.upto("pe"))
                    elif n == 1:
                        for h in range(0, MH, 2):
                            pe.wait_ge(*drained(f"{t}mla.o{h}"))
                    else:
                        pe.wait_ge(yc_ready.sem, yc_ready.upto("pe"))
                    for m in range(DC):
                        product(f"{t}br{n}.{m}", w[:, :, m * P:(m + 1) * P], (yA, yB, yC)[n])
                    used_by(f"{t}br{n}.{DC - 1}")
                for hf in range(2):
                    w = unit(f"o{hf}", DC, 512)
                    for m in range(4):
                        product(f"{t}o{4 * hf + m}", w[:, :, m * P:(m + 1) * P], H2, merged_ready if hf + m == 0 else None)
                    used_by(f"{t}o{4 * hf + 3}")
                rms_norm(f"f2{l}")
                swiglu(f"f2{l}", FF // HB, h_ready)

            pe.wait_ge(x_ready.sem, DC * (1 + 2 * DEPTH))
            for i in range(TT):
                for hf in range(2):
                    b = fill(f"out{i}.{hf}")
                    for m in range(4):
                        last = nc.tensor.transpose(b[:, m * P:(m + 1) * P], X[:, 4 * hf + m, i * P:(i + 1) * P], ident[:, :])
                    filled(f"out{i}.{hf}", last)

        def swiglu_turns(steps):
            return divmod(steps, BODY)

        @block.scalar
        def _(act):
            f = nc.scalar.activation

            def evac(name, dst, src=None, func=ACT.Copy, last=True, **kw):
                act.wait_ge(*full(name))
                ins = f(dst, bank_of(name)[0:dst.shape[0], 0:T] if src is None else src, func, **kw)
                if last:
                    ins.then_inc(drain_sem(name), 1)

            for t, rows in enumerate(TABLE):
                r = 0
                for name, n in rows:
                    act.dma_start(prow[r:r + n, t, :], A[SOURCES[name]].flatten().rearrange("(r p) -> r p", p=P)) \
                        .then_inc(rows_landed, 16)
                    r += n
            act.dma_start(xin, A["x"][0].rearrange("(i p) d -> p i d", p=P)).then_inc(x_landed, 16)
            with nc.allow_non_contiguous_dma(reason="small tables"):
                act.dma_start(wif[:, :, :], A["a_w_if"][0].rearrange("(k p) n -> p k n", p=P)).then_inc(small_landed, 16)
                act.dma_start(bif[:, :], A["a_b_if"].rearrange("o (g h) -> h (o g)", h=NH)).then_inc(small_landed, 16)
                act.dma_start(wr[:, :, :], A["moe_w_router"].rearrange("(k p) n -> p k n", p=P)).then_inc(small_landed, 16)
                act.dma_start(brb[:, :], A["moe_b_router"].partition_broadcast(P)).then_inc(small_landed, 16)
                act.dma_start(posi[:, :], A["positions_2"].rearrange("o (i p) -> p (o i)", p=P)).then_inc(small_landed, 16)
                act.dma_start(dtb[:, :, :], A["ssd_dt_bias_2"].partition_broadcast(P)).then_inc(small_landed, 16)
                act.dma_start(alb[:, :, :], A["ssd_a_log_2"].partition_broadcast(P)).then_inc(small_landed, 16)
                act.dma_start(gmw[:, :, :, :], A["gm_w_s_2"].rearrange("l g t s -> t l g s")).then_inc(small_landed, 16)
                act.dma_start(bsb[:, :, :, :], A["gm_b_s_2"].partition_broadcast(P)).then_inc(small_landed, 16)
                act.dma_start(gainb[:, 0, :, :], A["mla_q_gain_2"].partition_broadcast(P)).then_inc(small_landed, 16)
                act.dma_start(gainb[:, 1, :, :], A["mla_k_gain_2"].partition_broadcast(P)).then_inc(small_landed, 16)
                for l in range(DEPTH):
                    for o in range(2):
                        act.dma_start(dsk[o * SHD:(o + 1) * SHD, l, :],
                                      A["ssd_d_2"][l].rearrange("(c o) -> o c", o=2)[o].partition_broadcast(SHD)) \
                            .then_inc(small_landed, 16)
            act.wait_ge(*drained("table0"))
            t, r = col["c"]
            f(cT[:, :], pcol[:, t, r:r + DC], ACT.Silu).then_inc(c_ready, 1)
            act.wait_ge(consts_made, N_CONST)

            def conv_silu(m, dst, bias, n):
                act.wait_ge(conv_summed.sem, conv_summed.upto("act"))
                f(dst[:, m, :], dst[:, m, :], ACT.Silu, bias=vec(bias, n)).then_inc(conv_ready.sem, 1)

            act.wait_ge(pad_cleared.sem, pad_cleared.upto("act"))
            for n in range(DIC):
                evac(f"w_in{n}", xm[:, n, PAD:PAD + T])
                if n >= 2:
                    conv_silu(n - 2, xc, "conv_b", n - 2)
            for n in range(DIC):
                evac(f"w_in{DIC + n}", sz[:, n, :], func=ACT.Silu)
                if n < 2:
                    conv_silu(DIC - 2 + n, xc, "conv_b", DIC - 2 + n)
            act.wait_ge(small_landed, 16 * N_SMALL)
            f(alb[:, :, :], alb[:, :, :], ACT.Exp).then_inc(consts_derived, 1)
            for g in range(2):
                evac(f"gate{g}", lrow[g], func=ACT.Identity, bias=bif[:, g:g + 1])

            def softplus_tail(e, u):
                act.wait_ge(abs_ready.sem, abs_ready.upto("act"))
                f(e, e, ACT.Exp, scale=-1.0).then_inc(aexp_ready.sem, 1)
                act.wait_ge(plus_one.sem, plus_one.upto("act"))
                f(u, u, ACT.Ln).then_inc(ln_ready.sem, 1)

            ucol = sm[:, 0:TT * NH]
            for h in range(NH):
                for m in range(DHC):
                    evac(f"q{h}.{m}", qm[:, m, :])
                    if h == 0 and m == 1:
                        softplus_tail(lrow[7], lrow[2])
                for m in range(DHC):
                    evac(f"k{h}.{m}", km[:, m, :])
                if h == 0:
                    act.wait_ge(rows_made.sem, rows_made.upto("act"))
                    f(lrow[6], lrow[6], ACT.Exp, scale=-1.0).then_inc(emt_ready.sem, 1)
                    evac("ucol", ucol, bank_of("ucol")[:, 0:TT * NH])
                else:
                    mlstm_norm = h - 1
                    act.wait_ge(hc_ready.sem, hc_ready.upto("act"))
                    f(hsq, hm, ACT.Square).then_inc(hsq_ready.sem, 1)
                    evac(f"gvar{mlstm_norm}", nrm[:, 0, :], func=ACT.Sqrt, scale=1.0 / DH, bias=eps_ln[:, :])
                act.wait_ge(dlog_ready.sem, dlog_ready.upto("act"))
                if h == 0:
                    act.wait_ge(*drained("ucol"))
                W = Wm[h % 2]
                f(W[:, 0, :], W[:, 0, :], ACT.Exp, bias=ucol[:, h:h + 1])
                f(W[:, 1, P:T], W[:, 1, P:T], ACT.Exp, bias=ucol[:, NH + h:NH + h + 1]).then_inc(wexp_ready.sem, 1)
            act.wait_ge(hc_ready.sem, hc_ready.upto("act"))
            f(hsq, hm, ACT.Square).then_inc(hsq_ready.sem, 1)
            evac(f"gvar{NH - 1}", nrm[:, 0, :], func=ACT.Sqrt, scale=1.0 / DH, bias=eps_ln[:, :])

            def squares(fresh, moved=None):
                for k in range(DC):
                    if moved is None:
                        act.wait_ge(fresh.sem, fresh.upto("act"))
                    else:
                        act.wait_ge(*drained(f"{moved}{k}"))
                    f(SQ[:, k, :], X[:, k, :], ACT.Square).then_inc(squared.sem, 1)

            def layer_norm(tag):
                squares(centered)
                evac(f"{tag}.var", nrm[:, 0, :], func=ACT.Sqrt, scale=1.0 / D, bias=eps_ln[:, :])

            def rms_norm(tag, moved=None):
                squares(x_ready, moved)
                evac(f"{tag}.ms", nrm[:, 0, :], func=ACT.Sqrt, scale=1.0 / D, bias=eps_rms[:, :])

            def routing(l):
                act.wait_ge(*drained(f"logits{l}"))
                f(sm[:, 32:64], sm[:, 32:64], ACT.Exp).then_inc(router_exp.sem, 1)
                evac(f"gT{l}", gT)
                for e in range(0, NE, 2):
                    evac(f"gb{l}.{e}", gbc[:, e:e + 2, :], bank_of(f"gb{l}.{e}")[:, :].rearrange("p (a t) -> p a t", a=2))

            def swiglu(tag, steps):
                k0 = uses[f"{tag}.0"]

                def step(i, j):
                    k = k0 + j
                    act.wait_ge(bank_full[k % 4], i + k // 4 + 1)
                    f(sg[j % 2], bank[k % 4][:, 0:T], ACT.Silu).then_inc(silu_ready.sem, 1)

                turns, rest = swiglu_turns(steps)
                with act.Fori(0, turns) as i:
                    for j in range(BODY):
                        step(i, j)
                for j in range(rest):
                    step(turns, j)

            def attention(tag, heads, o):
                def exps(h):
                    act.wait_ge(score_ready.sem, score_ready.upto("act"))
                    S, E, c = Ss[h % 2], Es[h % 2], 64 + 8 * (h % 2)
                    f(E[:, 0, 0:P], S[:, 0, 0:P], ACT.Exp, bias=sm[:, c:c + 1], accum_out=sm[:, c + 2:c + 3])
                    f(E[:, 1, :], S[:, 1, :], ACT.Exp, bias=sm[:, c + 1:c + 2], accum_out=sm[:, c + 3:c + 4]) \
                        .then_inc(prob_exp.sem, 1)

                def turned(h):
                    name = f"{tag}.p{h}"
                    evac(name, PTs[h % 2][:, 0, :], last=False)
                    evac(name, PTs[h % 2][:, 1, P:T], bank_of(name)[:, T + P:2 * T])

                for it in range(heads + 2):
                    if it < heads:
                        exps(it)
                    if 1 <= it <= heads:
                        turned(it - 1)
                    if it >= 2 and it % 2:
                        evac(f"{tag}.o{it - 3}", o[:, (it - 3) // 2, :])

            layer_norm("ln00")
            routing(0)
            swiglu("moe0", NE * FE // HB)
            act.wait_ge(rope_in.sem, rope_in.upto("act"))
            for a in range(2):
                last = f(trig[:, a, :, :], trig[:, a, :, :], ACT.Sin)
            last.then_inc(rope_ready.sem, 1)
            layer_norm("ln01")

            for m in range(DC):
                evac(f"bk{m}", ka[:, m, :])
            for n in range(2):
                for i in range(TT):
                    evac(f"bv{n}.{i}", va[:, i, n * 512:(n + 1) * 512], bank_of(f"bv{n}.{i}")[:, :])
            for m in range(DC):
                evac(f"bq{m}", qa[:, m, :], scale=AD ** -0.5)
            attention("moba", AH, oa)
            layer_norm("ln10")
            routing(1)
            swiglu("moe1", NE * FE // HB)
            layer_norm("ln11")

            for l in range(DEPTH):
                rms_norm(f"f1{l}")
                swiglu(f"f1{l}", FF // HB)
                rms_norm(f"mx{l}")
                t = f"m{l}."
                for m in range(4):
                    evac(f"{t}u{m}", us[:, m, :], func=ACT.Gelu)
                for i in range(TT):
                    evac(f"{t}v{i}", vn[:, i, :], bank_of(f"{t}v{i}")[:, :], ACT.Gelu)
                for i in range(TT):
                    act.wait_ge(*drained(f"{t}v{i}"))
                    last = f(qksq[:, i * GMW:(i + 1) * GMW], vn[:, i, :], ACT.Square, accum_out=sm[:, 80 + i:81 + i])
                last.then_inc(vsq_ready.sem, 1)
                for m in range(3):
                    evac(f"{t}cq{m}", cq[:, m, :], last=False)
                    evac(f"{t}cq{m}", SQ[:, m, :], func=ACT.Square)
                for m in range(2):
                    evac(f"{t}ckv{m}", ckv[:, m, :], last=False)
                    evac(f"{t}ckv{m}", SQ[:, 3 + m, :], func=ACT.Square)
                for i in range(TT):
                    evac(f"{t}kr{i}", krs[:, i, :], bank_of(f"{t}kr{i}")[:, 0:ROPE])
                for m in range(4):
                    evac(f"{t}z{m}", zs[:, m, :], func=ACT.Silu)
                act.wait_ge(pad_cleared.sem, pad_cleared.upto("act"))
                for m in range(8):
                    evac(f"{t}xbc{m}", xb[:, m, PAD:PAD + T])
                act.wait_ge(vsq_ready.sem, vsq_ready.upto("act"))
                f(sm[:, 80:82], sm[:, 80:82], ACT.Sqrt, scale=1.0 / GMW, bias=eps_rms[:, :]).then_inc(vsq_ready.sem, 1)
                vsq_ready.upto("act")
                evac(f"{t}cqms", nrm[:, 0, :], func=ACT.Sqrt, scale=1.0 / QR, bias=eps_rms[:, :])
                evac(f"{t}ckvms", nrm[:, 1, :], func=ACT.Sqrt, scale=1.0 / KVR, bias=eps_rms[:, :])
                for i in range(TT):
                    for g in range(2):
                        evac(f"{t}q{i}.{g}", Qt[:, i, 4 * g:4 * g + 4, :].rearrange("p h d -> p (h d)"),
                             bank_of(f"{t}q{i}.{g}")[:, 0:4 * QK])
                qkb = [sm[:, 96:112], sm[:, 112:128]]
                for n, src in enumerate((Qt, Kt)):
                    if n:
                        for i in range(TT):
                            for g in range(2):
                                b = bank_of(f"{t}kv{i}.{g}")[:, :].rearrange("p (h d) -> p h d", h=4)
                                evac(f"{t}kv{i}.{g}", Kt[:, i, 4 * g:4 * g + 4, 0:NOPE], b[:, :, 0:NOPE], last=False)
                                evac(f"{t}kv{i}.{g}", Vt[:, i, 4 * g * MV:(4 * g + 4) * MV].rearrange("p (h d) -> p h d", h=4),
                                     b[:, :, NOPE:NOPE + MV])
                    if n:
                        act.wait_ge(qksq_ready.sem, qksq_ready.upto("act"))
                    for i in range(TT):
                        for g in range(2):
                            act.wait_ge(*drained(f"{t}{'kv' if n else 'q'}{i}.{g}"))
                    f(qksq, src.rearrange("p i h d -> p (i h d)"), ACT.Square).then_inc(qkss_ready.sem, 1)
                    act.wait_ge(qkstd_ready.sem, qkstd_ready.upto("act"))
                    f(qkb[n], qkb[n], ACT.Sqrt, scale=1.0 / QK, bias=eps_rms[:, :]).then_inc(qkstd_ready.sem, 1)
                    qkstd_ready.upto("act")
                for name, dst in (("qT", QT), ("kT", KT)):
                    for c in range(MH // 2):
                        evac(f"{t}{name}{c}", dst[0:QK, 2 * c:2 * c + 2, :],
                             bank_of(f"{t}{name}{c}")[0:QK, :].rearrange("p (h t) -> p h t", h=2))
                attention(f"{t}mla", MH, yB)
                for m in range(8):
                    conv_silu(m, xv, "conv_b2", 8 * l + m)
                softplus_tail(sm[:, 144:160], sm[:, 160:176])
                for h in range(SH):
                    act.wait_ge(*full(f"{t}ss{h}"))
                    b = bank_of(f"{t}ss{h}")
                    evac(f"{t}ss{h}", Eh[h % 2][:, 0, :], last=False, func=ACT.Exp)
                    evac(f"{t}ss{h}", Eh[h % 2][:, 1, P:T], b[:, T + P:2 * T], func=ACT.Exp)
                for c in range(4):
                    act.wait_ge(yz_ready.sem, yz_ready.upto("act"))
                    f(SQ[:, c, :], yC[:, c, :], ACT.Square).then_inc(ysilu_ready.sem, 1)
                for g in range(SG):
                    evac(f"{t}yms{g}", nrm[:, g, :], func=ACT.Sqrt, scale=1.0 / (SI // SG), bias=eps_rms[:, :])
                for n in range(NB):
                    for m in range(DC):
                        evac(f"{t}g{n}.{m}", sig[n % 2][:, m, :], func=ACT.Sigmoid)
                rms_norm(f"f2{l}", f"{t}o")
                swiglu(f"f2{l}", FF // HB)
            for i in range(TT):
                for hf in range(2):
                    evac(f"out{i}.{hf}", xo[:, i, hf * 512:(hf + 1) * 512], bank_of(f"out{i}.{hf}")[:, :])

        @block.vector
        def _(dve):
            v = nc.vector
            tt, ts, stt = v.tensor_tensor, v.tensor_scalar, v.scalar_tensor_tensor
            steps = [0]

            def link(ins):
                ins.then_inc(dve_steps, 1)
                steps[0] += 1
                dve.wait_ge(dve_steps, steps[0])

            def moved(name, ins):
                ins.then_inc(drain_sem(name), 1)

            def rows(ap, n):
                return ap.unsqueeze(1).broadcast_to([ap.shape[0], n, ap.shape[1]])

            def each(ap, n):
                return ap.unsqueeze(2).broadcast_to([ap.shape[0], ap.shape[1], n])

            for t, entries in enumerate(TABLE):
                n = sum(m for _, m in entries)
                dve.wait_ge(*full(f"table{t}"))
                moved(f"table{t}", v.tensor_copy(pcol[:, t, 0:n], bank_of(f"table{t}")[:, 0:n]))
            for kk in range(DC // 2):
                dve.wait_ge(*full(f"x{kk}"))
                moved(f"x{kk}", v.tensor_copy(X[:, 2 * kk:2 * kk + 2, :],
                                              bank_of(f"x{kk}")[:, :].rearrange("p (a t) -> p a t", a=2)))
            for t in range(len(TABLE)):
                dve.wait_ge(*drained(f"table{t}"))
            for kk in range(DC // 2):
                dve.wait_ge(*drained(f"x{kk}"))
            v.memset(xm[:, :, 0:PAD], 0.0).then_inc(pad_cleared.sem, 1)
            dve.wait_ge(pad_cleared.sem, pad_cleared.upto("dve"))

            def add_ada(b, c0, c1):
                t, r = col["b_ada"]
                link(tt(mods[:, c0:c1], b[:, c0:c1], pcol[:, t, r + c0:r + c1], ALU.add))
                for g in range(c0, c1, 3 * DC):
                    first, end = (g + DC, g + 3 * DC) if g < DEPTH * 6 * DC else (g + DC, g + 2 * DC)
                    last = ts(mods[:, first:end], mods[:, first:end], 1.0, None, ALU.add)
                link(last)

            def modulate(dst, layer, s, ready):
                for k in range(DC):
                    ts(dst[:, k, :], X[:, k, :], mod(layer, s, 1, k), mod(layer, s, 0, k), ALU.mult, ALU.add) \
                        .then_inc(ready.sem, 1)

            dve.wait_ge(ada_done.sem, ADA_FIRST)
            add_ada(yacc[0], 0, 4 * ADA_FIRST)
            def scale_residual():
                dve.wait_ge(h_ready.sem, h_ready.upto("dve", DC))
                link(ts(X[:, :, :], X[:, :, :], ALPHA, None, ALU.mult))

            modulate(H, 0, 0, h_ready)
            scale_residual()

            def conv(src, dst, m, taps):
                link(ts(dst[:, m, :], src[:, m, 0:T], taps[0], None, ALU.mult))
                for j in range(1, CONV):
                    ins = stt(dst[:, m, :], src[:, m, j:j + T], taps[j], dst[:, m, :], ALU.mult, ALU.add)
                    if j < CONV - 1:
                        link(ins)
                ins.then_inc(conv_summed.sem, 1)

            for m in range(DIC):
                dve.wait_ge(*drained(f"w_in{m}"))
                conv(xm, xc, m, [vec("conv_w", j * DIC + m) for j in range(CONV)])

            def log1p_exp(e, u, d, z):
                dve.wait_ge(aexp_ready.sem, aexp_ready.upto("dve"))
                link(ts(u, e, 1.0, None, ALU.add))
                link(ts(d, u, 1.0, None, ALU.subtract))
                ts(z, d, 0.0, None, ALU.is_equal).then_inc(plus_one.sem, 1)
                dve.wait_ge(plus_one.sem, plus_one.upto("dve"))
                link(tt(d, d, z, ALU.add))
                dve.wait_ge(ln_ready.sem, ln_ready.upto("dve"))
                link(tt(u, u, z, ALU.add))
                link(v.reciprocal(d, d))
                link(tt(u, u, d, ALU.mult))
                link(tt(u, u, e, ALU.mult))

            for g in range(2):
                dve.wait_ge(*drained(f"gate{g}"))
            v.memset(lrow[6], 1.0)
            stt(lrow[7], lrow[1], -1.0, lrow[1], ALU.mult, ALU.max).then_inc(abs_ready.sem, 1)
            dve.wait_ge(abs_ready.sem, abs_ready.upto("dve"))
            log1p_exp(lrow[7], lrow[2], lrow[3], lrow[4])
            link(stt(lrow[1], lrow[1], 0.0, lrow[2], ALU.min, ALU.subtract))
            link(v.tensor_tensor_scan(lrow[4], lrow[6], lrow[1], 0.0, ALU.mult, ALU.add))
            tt(lrow[3], lrow[0], lrow[4], ALU.subtract).then_inc(stab_ready.sem, 1)
            dve.wait_ge(stab_ready.sem, stab_ready.upto("dve"))
            link(v.tensor_tensor_scan(lrow[2], lrow[3], lrow[3], 0.0, ALU.max, ALU.max))
            ts(lrow[5], lrow[2], -1.0, None, ALU.mult)
            tt(lrow[6], lrow[4], lrow[2], ALU.add).then_inc(rows_made.sem, 1)

            def mlstm_num(h):
                dve.wait_ge(*full(f"den{h}"))
                moved(f"den{h}", v.tensor_copy(nrm[:, 1, :], bank_of(f"den{h}")[:, 0:T]))
                dve.wait_ge(*drained(f"den{h}"))
                dve.wait_ge(*drained(f"mbc{h}"))
                link(tt(den_s, den_s, nrm[:, 1, :], ALU.max))
                link(stt(den_s, nrm[:, 1, :], -1.0, den_s, ALU.mult, ALU.max))
                link(v.reciprocal(den_s, den_s))
                for a in range(2):
                    name = f"num{h}.{a}"
                    dve.wait_ge(*full(name))
                    moved(name, tt(hm[:, 2 * a:2 * a + 2, :], bank_of(name)[:, :].rearrange("p (a t) -> p a t", a=2),
                                   rows(den_s, 2), ALU.mult))
                dve.wait_ge(*full(f"gmean{h}"))
                moved(f"gmean{h}", ts(nrm[:, 1, :], bank_of(f"gmean{h}")[:, 0:T], -1.0 / DH, None, ALU.mult))
                dve.wait_ge(*drained(f"gmean{h}"))
                tt(hm, hm, rows(nrm[:, 1, :], DHC), ALU.add).then_inc(hc_ready.sem, 1)

            def mlstm_out(h):
                dve.wait_ge(*drained(f"gvar{h}"))
                link(v.reciprocal(nrm[:, 0, :], nrm[:, 0, :]))
                link(tt(hm, hm, rows(nrm[:, 0, :], DHC), ALU.mult))
                c = DHC * h
                for m in range(DHC):
                    last = ts(xc[:, c + m, :], xc[:, c + m, :], vec("skip", c + m), None, ALU.mult)
                link(last)
                for m in range(DHC):
                    last = stt(xc[:, c + m, :], hm[:, m, :], vec("gn_g", c + m), xc[:, c + m, :], ALU.mult, ALU.add)
                link(last)
                tt(xc[:, c:c + DHC, :], xc[:, c:c + DHC, :], sz[:, c:c + DHC, :], ALU.mult).then_inc(head_ready.sem, 1)

            for h in range(NH):
                if h > 0:
                    mlstm_num(h - 1)
                for i in range(TT):
                    dve.wait_ge(*full(f"v{h}.{i}"))
                    moved(f"v{h}.{i}", v.tensor_copy(vm(h, i), bank_of(f"v{h}.{i}")[:, :]))
                if h > 0:
                    mlstm_out(h - 1)
                dve.wait_ge(*full(f"mbc{h}"))
                b, W = bank_of(f"mbc{h}"), Wm[h % 2]
                tt(W[:, 0, :], b[:, 0:T], neg_st[:, 0, :], ALU.add)
                tt(W[:, 1, P:T], b[:, P:T], neg_st[:, 1, P:T], ALU.add).then_inc(dlog_ready.sem, 1)
                moved(f"mbc{h}", v.tensor_copy(den_s, b[:, T:2 * T]))
                dve.wait_ge(*full(f"mS{h}"))
                dve.wait_ge(wexp_ready.sem, wexp_ready.upto("dve"))
                b = bank_of(f"mS{h}")
                stt(Pm[h % 2][:, 0, :], b[:, 0:T], DH ** -0.5, W[:, 0, :], ALU.mult, ALU.mult)
                moved(f"mS{h}", stt(Pm[h % 2][:, 1, P:T], b[:, T + P:2 * T], DH ** -0.5, W[:, 1, P:T], ALU.mult, ALU.mult))
            mlstm_num(NH - 1)
            mlstm_out(NH - 1)
            dve.wait_ge(ada_done.sem, 28)
            add_ada(yacc[1], 4 * ADA_FIRST, 112)

            def layer_norm(tag, layer, s, y=None):
                for m in range(DC):
                    if y:
                        dve.wait_ge(*full(f"{y}{m}"))
                        moved(f"{y}{m}", stt(X[:, m, :], bank_of(f"{y}{m}")[:, 0:T], mod(layer, s, 2, m), X[:, m, :],
                                             ALU.mult, ALU.add))
                    else:
                        stt(X[:, m, :], ysum(m), mod(layer, s, 2, m), X[:, m, :], ALU.mult, ALU.add) \
                            .then_inc(sum_ready.sem, 1)
                dve.wait_ge(*full(f"{tag}.mean"))
                moved(f"{tag}.mean", ts(nrm[:, 1, :], bank_of(f"{tag}.mean")[:, 0:T], -1.0 / D, None, ALU.mult))
                dve.wait_ge(*drained(f"{tag}.mean"))
                for m in range(DC):
                    tt(X[:, m, :], X[:, m, :], nrm[:, 1, :], ALU.add).then_inc(centered.sem, 1)
                dve.wait_ge(*drained(f"{tag}.var"))
                link(v.reciprocal(nrm[:, 0, :], nrm[:, 0, :]))
                for m in range(DC):
                    last = tt(X[:, m, :], X[:, m, :], nrm[:, 0, :], ALU.mult)
                link(last)
                final = layer == DEPTH // 2 and s == 1
                for m in range(DC):
                    i = (layer * 2 + s) * DC + m
                    last = ts(X[:, m, :], X[:, m, :], vec("ln_g", i), vec("ln_b", i), ALU.mult, ALU.add)
                    if final:
                        last.then_inc(x_ready.sem, 1)
                if not final:
                    link(last)

            def rms_norm(tag, gain, l):
                dve.wait_ge(*drained(f"{tag}.ms"))
                link(v.reciprocal(nrm[:, 0, :], nrm[:, 0, :]))
                for k in range(DC):
                    stt(H[:, k, :], X[:, k, :], vec(gain, l * DC + k), nrm[:, 0, :], ALU.mult, ALU.mult) \
                        .then_inc(h_ready.sem, 1)
                dve.wait_ge(h_ready.sem, h_ready.upto("dve", DC))

            def routing(l):
                def s3(a, n, m):
                    return sm[:, a:a + n * m].rearrange("p (n m) -> p n m", n=n)

                gate, e, selp = s3(0, TT, NE), s3(32, TT, NE), s3(200, TT, NE)
                top, tot = sm[:, 192:194], sm[:, 194:196]
                dve.wait_ge(*full(f"logits{l}"))
                b = bank_of(f"logits{l}")[:, 0:TT * NE].rearrange("p (n m) -> p n m", n=TT)
                link(v.tensor_reduce(top, b, AX.X, ALU.max))
                moved(f"logits{l}", tt(e, b, each(top, NE), ALU.subtract))
                dve.wait_ge(router_exp.sem, router_exp.upto("dve"))
                link(v.tensor_reduce(tot, e, AX.X, ALU.add))
                link(v.reciprocal(tot, tot))
                link(tt(e, e, each(tot, NE), ALU.mult))
                link(tt(selp, e, rows(brb[:, :], TT), ALU.add))
                s4 = s3(200, TT * NGRP, EPG)
                pairs = s3(232, 6, TT * NGRP)
                for n, (i, j) in enumerate([(i, j) for i in range(EPG) for j in range(i + 1, EPG)]):
                    last = tt(pairs[:, n, :], s4[:, :, i], s4[:, :, j], ALU.add)
                link(last)
                gs, gm, g1 = sm[:, 280:288], sm[:, 288:290], sm[:, 290:298]
                link(v.tensor_reduce(gs, pairs.rearrange("p s n -> p n s"), AX.X, ALU.max))

                def first_best(score, best, onehot, rank, n):
                    link(v.tensor_reduce(best, score, AX.X, ALU.max))
                    link(tt(onehot, score, each(best, n), ALU.is_equal))
                    link(tt(onehot, onehot, rows(rank, TT), ALU.mult))
                    link(v.tensor_reduce(best, onehot, AX.X, ALU.max))
                    link(tt(onehot, onehot, each(best, n), ALU.is_equal))

                first_best(s3(280, TT, NGRP), gm, s3(290, TT, NGRP), rank4[:, :], NGRP)
                link(ts(g1, g1, -NEG, NEG, ALU.mult, ALU.add))
                link(tt(s4, s4, each(g1, EPG), ALU.add))
                o1, o2 = s3(304, TT, NE), s3(336, TT, NE)
                first_best(selp, top, o1, rank16[:, :], NE)
                link(stt(sm[:, 200:232], sm[:, 304:336], 2 * NEG, sm[:, 200:232], ALU.mult, ALU.add))
                first_best(selp, top, o2, rank16[:, :], NE)
                link(tt(sm[:, 304:336], sm[:, 304:336], sm[:, 336:368], ALU.add))
                link(tt(gate, e, o1, ALU.mult))
                link(v.tensor_reduce(tot, gate, AX.X, ALU.add))
                link(v.reciprocal(tot, tot))
                tt(gate, gate, each(tot, NE), ALU.mult).then_inc(route_ready.sem, 1)

            def swiglu(tag, n_steps, gated):
                k0 = uses[f"{tag}.0"]
                s0, g0 = silu_ready.upto("dve", 0), scaled_ready.upto("dve", 0)

                def step(i, j, gate):
                    k = k0 + j
                    dve.wait_ge(silu_ready.sem, i * BODY + s0 + j + 1)
                    src = sg[j % 2]
                    if gated:
                        tt(sgw[j % 2], src, gate, ALU.mult).then_inc(scaled_ready.sem, 1)
                        dve.wait_ge(scaled_ready.sem, i * BODY + g0 + j + 1)
                        src = sgw[j % 2]
                    tt(hid[j % 2], src, bank[k % 4][:, T:2 * T], ALU.mult).then_inc(bank_drained[k % 4], 1)

                turns, rest = swiglu_turns(n_steps)
                if gated:
                    assert BODY * HB == FE and rest == 0
                    for e in range(0, NE, 2):
                        dve.wait_ge(*drained(f"gb{tag[-1]}.{e}"))
                with dve.Fori(0, turns) as i:
                    for j in range(BODY):
                        step(i, j, gbc[:, bass.ds(i, 1), :].rearrange("p a t -> p (a t)") if gated else None)
                for j in range(rest):
                    step(turns, j, None)
                silu_ready.upto("dve", n_steps)
                if gated:
                    scaled_ready.upto("dve", n_steps)

            def attention(tag, heads, score):
                for i in range(2):
                    last = v.memset(Ss[i][:, 0, P:T], NEG)
                link(last)

                def scores(h):
                    name, c, S = f"{tag}.s{h}", 64 + 8 * (h % 2), Ss[h % 2]
                    dve.wait_ge(*full(name))
                    b = bank_of(name)
                    score(h, S[:, 0, 0:P], b[:, 0:P], 0, P)
                    moved(name, score(h, S[:, 1, :], b[:, T:2 * T], 1, T))
                    dve.wait_ge(*drained(name))
                    link(v.tensor_reduce(sm[:, c + 4:c + 6], S, AX.X, ALU.max))
                    ts(sm[:, c:c + 2], sm[:, c + 4:c + 6], -1.0, None, ALU.mult).then_inc(score_ready.sem, 1)

                def normed(h):
                    c, E = 64 + 8 * (h % 2), Es[h % 2]
                    dve.wait_ge(prob_exp.sem, prob_exp.upto("dve"))
                    link(v.reciprocal(sm[:, c + 6:c + 8], sm[:, c + 2:c + 4]))
                    ts(E[:, 0, 0:P], E[:, 0, 0:P], sm[:, c + 6:c + 7], None, ALU.mult)
                    ts(E[:, 1, :], E[:, 1, :], sm[:, c + 7:c + 8], None, ALU.mult).then_inc(prob_ready.sem, 1)

                for it in range(heads + 1):
                    if it < heads:
                        scores(it)
                    if it >= 1:
                        normed(it - 1)

            def rotary_angles():
                two_pi = 2 * np.pi
                c1 = 6.28125
                c2 = float(np.float32(np.round((two_pi - c1) * 2.0 ** 22) / 2.0 ** 22))
                c3 = float(np.float32(two_pi - c1 - c2))
                magic = 1.5 * 2.0 ** 23
                dve.wait_ge(small_landed, 16 * N_SMALL)
                link(v.tensor_copy(posf[:, :], posi[:, :]))
                ang, sn, cs = sm[:, 500:532], trig[:, 1, :, :].rearrange("p i d -> p (i d)"), trig[:, 0, :, :].rearrange("p i d -> p (i d)")
                for i in range(TT):
                    last = ts(ang[:, i * HR:(i + 1) * HR], invf[:, :], posf[:, i:i + 1], None, ALU.mult)
                link(last)
                link(ts(cs, ang, 1.0 / two_pi, magic, ALU.mult, ALU.add))
                link(ts(cs, cs, magic, None, ALU.subtract))
                for c in (c1, c2, c3):
                    link(stt(ang, cs, -c, ang, ALU.mult, ALU.add))
                lim = 3.1415925
                link(ts(sn, ang, lim, -lim, ALU.min, ALU.max))
                link(ts(cs, ang, np.pi / 2, None, ALU.add))
                link(ts(ang, cs, np.pi, None, ALU.is_gt))
                link(stt(cs, ang, -two_pi, cs, ALU.mult, ALU.add))
                ts(cs, cs, lim, -lim, ALU.min, ALU.max).then_inc(rope_in.sem, 1)

            layer_norm("ln00", 0, 0, "y0.")
            modulate(H, 0, 1, h_ready)
            scale_residual()
            routing(0)
            rotary_angles()
            swiglu("moe0", NE * FE // HB, True)
            dve.wait_ge(down_done.sem, NE * FE // HB)
            layer_norm("ln01", 0, 1)
            for k in range(DC):
                ts(H2[:, k, :], X[:, k, :], kvmod(1, k), kvmod(0, k), ALU.mult, ALU.add).then_inc(h2_ready.sem, 1)
            modulate(H, 1, 0, h_ready)
            scale_residual()
            attention("moba", AH, lambda h, dst, b, i, n: stt(dst, alibi[:, i, 0:n], 2.0 ** (-8.0 * (h + 1) / AH), b,
                                                              ALU.mult, ALU.add))
            layer_norm("ln10", 1, 0, "y1.")
            modulate(H, 1, 1, h_ready)
            scale_residual()
            routing(1)
            swiglu("moe1", NE * FE // HB, True)
            dve.wait_ge(down_done.sem, 2 * NE * FE // HB)
            layer_norm("ln11", 1, 1)

            done = [2 * NE * FE // HB]

            def half_step(tag):
                swiglu(tag, FF // HB, False)
                done[0] += FF // HB
                dve.wait_ge(down_done.sem, done[0])
                for m in range(DC):
                    stt(X[:, m, :], ysum(m), 0.5, X[:, m, :], ALU.mult, ALU.add).then_inc(x_ready.sem, 1)

            for l in range(DEPTH):
                rms_norm(f"f1{l}", "ffn1", l)
                half_step(f"f1{l}")
                rms_norm(f"mx{l}", "mix", l)
                t = f"m{l}."
                v.memset(xb[:, :, 0:PAD], 0.0).then_inc(pad_cleared.sem, 1)
                dve.wait_ge(pad_cleared.sem, pad_cleared.upto("dve"))
                dve.wait_ge(vsq_ready.sem, vsq_ready.upto("dve", 2))
                link(v.reciprocal(sm[:, 80:82], sm[:, 80:82]))
                for i in range(TT):
                    last = ts(vn[:, i, :], vn[:, i, :], sm[:, 80 + i:81 + i], None, ALU.mult)
                last.then_inc(vn_ready.sem, 1)
                x8, a8, u8 = sm[:, 128:144], sm[:, 144:160], sm[:, 160:176]
                dtv, da = sm[:, 416:432].rearrange("p (i h) -> p i h", i=TT), sm[:, 432:448].rearrange("p (i h) -> p i h", i=TT)
                dve.wait_ge(*full(f"{t}dt"))
                moved(f"{t}dt", tt(x8.rearrange("p (i h) -> p i h", i=TT),
                                   bank_of(f"{t}dt")[:, 0:TT * SH].rearrange("p (i h) -> p i h", i=TT),
                                   rows(dtb[:, l, :], TT), ALU.add))
                dve.wait_ge(*drained(f"{t}dt"))
                stt(a8, x8, -1.0, x8, ALU.mult, ALU.max).then_inc(abs_ready.sem, 1)
                for name, src, n, gain, r in (("cq", cq, 3, "qn", 0), ("ckv", ckv, 2, "kvn", 1)):
                    dve.wait_ge(*drained(f"{t}{name}ms"))
                    link(v.reciprocal(nrm[:, r, :], nrm[:, r, :]))
                    for m in range(n):
                        last = stt(src[:, m, :], src[:, m, :], vec(gain, l * n + m), nrm[:, r, :], ALU.mult, ALU.mult)
                    last.then_inc(lat_ready.sem, 1)
                dve.wait_ge(*full(f"{t}wT"))
                moved(f"{t}wT", tt(wT, bank_of(f"{t}wT")[:, :].rearrange("p (g t) -> p g t", g=GMG),
                                   rows(upper[:, 0, 0:P], GMG), ALU.mult))
                for g in range(GMG):
                    dve.wait_ge(*full(f"{t}sp{g}"))
                    moved(f"{t}sp{g}", stt(yA[:, g, :].rearrange("p (i t) -> p i t", i=TT),
                                           bank_of(f"{t}sp{g}")[:, 0:T].rearrange("p (i t) -> p i t", i=TT),
                                           vec("gmv", l * GMG + g), rows(bsb[:, l, g, :], TT), ALU.mult, ALU.add))
                    dve.wait_ge(*drained(f"{t}sp{g}"))
                    last = tt(yA[:, g, :], yA[:, g, :], us[:, g, :], ALU.mult)
                last.then_inc(sp_ready.sem, 1)
                for i in range(TT):
                    dve.wait_ge(*drained(f"{t}kr{i}"))
                    last = v.tensor_copy(Kt[:, i, :, NOPE:QK], rows(krs[:, i, :], MH))
                last.then_inc(qksq_ready.sem, 1)
                for m in range(8):
                    dve.wait_ge(*drained(f"{t}xbc{m}"))
                    conv(xb, xv, m, [vec("conv_w2", (l * CONV + j) * 8 + m) for j in range(CONV)])
                if l == 0:
                    dve.wait_ge(rope_ready.sem, rope_ready.upto("dve"))
                for n, src in enumerate((Qt, Kt)):
                    ss = sm[:, 96 + 16 * n:112 + 16 * n]
                    dve.wait_ge(qkss_ready.sem, qkss_ready.upto("dve"))
                    v.tensor_reduce(ss, qksq.rearrange("p (h d) -> p h d", d=QK), AX.X, ALU.add).then_inc(qkstd_ready.sem, 1)
                    dve.wait_ge(qkstd_ready.sem, qkstd_ready.upto("dve", 2))
                    link(v.reciprocal(ss, ss))
                    flat = src.rearrange("p i h d -> p (i h) d")
                    link(tt(flat, flat, each(ss, QK), ALU.mult))
                    link(tt(flat, flat, rows(gainb[:, n, l, :], TT * MH), ALU.mult))
                    for i in range(TT):
                        x1, x2 = src[:, i, :, NOPE:NOPE + HR], src[:, i, :, NOPE + HR:QK]
                        cs, sn = rows(trig[:, 0, i, :], MH), rows(trig[:, 1, i, :], MH)
                        for a, (x, c) in enumerate(((x1, cs), (x2, sn), (x2, cs), (x1, sn))):
                            last = tt(rt[a][:, i, :, :], x, c, ALU.mult)
                    link(last)
                    x1, x2 = src[:, :, :, NOPE:NOPE + HR], src[:, :, :, NOPE + HR:QK]
                    tt(x1, rt[0], rt[1], ALU.subtract)
                    tt(x2, rt[2], rt[3], ALU.add).then_inc(qkrot_ready.sem, 1)
                dve.wait_ge(qkrot_ready.sem, qkrot_ready.upto("dve", 2))
                attention(f"{t}mla", MH, lambda h, dst, b, i, n: stt(dst, b, QK ** -0.5, neg_qk[:, i, 0:n], ALU.mult, ALU.add))
                dve.wait_ge(abs_ready.sem, abs_ready.upto("dve"))
                log1p_exp(a8, u8, sm[:, 176:192], sm[:, 400:416])
                link(stt(sm[:, 416:432], x8, 0.0, u8, ALU.max, ALU.add))
                dve.wait_ge(consts_derived, 1)
                link(stt(da, dtv, -1.0, rows(alb[:, l, :], TT), ALU.mult, ALU.mult))
                for i in range(TT):
                    dve.wait_ge(*full(f"{t}xs{i}"))
                    moved(f"{t}xs{i}", tt(xdt[:, i, :].rearrange("p (h d) -> p h d", h=SH),
                                          bank_of(f"{t}xs{i}")[:, :].rearrange("p (h d) -> p h d", h=SH),
                                          each(dtv[:, i, :], SHD), ALU.mult))
                for g in range(SG):
                    dve.wait_ge(*full(f"{t}cb{g}"))
                    b = bank_of(f"{t}cb{g}")
                    tt(CB[g][:, 0, :], b[:, 0:T], upper[:, 0, :], ALU.mult)
                    moved(f"{t}cb{g}", tt(CB[g][:, 1, P:T], b[:, T + P:2 * T], upper[:, 1, P:T], ALU.mult))
                for g in range(SG):
                    dve.wait_ge(*drained(f"{t}cb{g}"))

                def decay_terms(h):
                    ts(Mh[h % 2][:, 0, 0:P], strict[:, 0, 0:P], da[:, 0, h:h + 1], None, ALU.mult)
                    ts(Mh[h % 2][:, 1, :], strict[:, 1, :], da[:, 1, h:h + 1], None, ALU.mult).then_inc(decay_in.sem, 1)

                def output(c):
                    name = f"{t}y{2 * c}"
                    dve.wait_ge(*full(name))
                    moved(name, stt(yC[:, c, :], xv[:, c, :], dsk[:, l, c:c + 1], bank_of(name)[:, 0:T], ALU.mult, ALU.add))
                    dve.wait_ge(*drained(name))
                    tt(yC[:, c, :], yC[:, c, :], zs[:, c, :], ALU.mult).then_inc(yz_ready.sem, 1)

                decay_terms(0)
                decay_terms(1)
                for h in range(SH):
                    dve.wait_ge(*drained(f"{t}ss{h}"))
                    g = h // (SH // SG)
                    tt(Ph[h % 2][:, 0, :], Eh[h % 2][:, 0, :], CB[g][:, 0, :], ALU.mult)
                    tt(Ph[h % 2][:, 1, P:T], Eh[h % 2][:, 1, P:T], CB[g][:, 1, P:T], ALU.mult).then_inc(sp_mm_ready.sem, 1)
                    if h + 2 < SH:
                        decay_terms(h + 2)
                    if h % 2:
                        output(h // 2)
                for g in range(SG):
                    dve.wait_ge(*drained(f"{t}yms{g}"))
                    link(v.reciprocal(nrm[:, g, :], nrm[:, g, :]))
                    for c in range(2 * g, 2 * g + 2):
                        last = stt(yC[:, c, :], yC[:, c, :], vec("ssdn", l * 4 + c), nrm[:, g, :], ALU.mult, ALU.mult)
                last.then_inc(yc_ready.sem, 1)
                for n in range(NB):
                    for m in range(DC):
                        name, gate = f"{t}br{n}.{m}", sig[n % 2][:, m, :]
                        dve.wait_ge(*full(name))
                        dve.wait_ge(*drained(f"{t}g{n}.{m}"))
                        moved(name, tt(H2[:, m, :] if n == 0 else gate, bank_of(name)[:, 0:T], gate, ALU.mult))
                        dve.wait_ge(*drained(name))
                        if n:
                            last = tt(H2[:, m, :], H2[:, m, :], gate, ALU.add)
                            if n == NB - 1:
                                last.then_inc(merged_ready.sem, 1)
                            else:
                                link(last)
                for m in range(DC):
                    dve.wait_ge(*full(f"{t}o{m}"))
                    moved(f"{t}o{m}", tt(X[:, m, :], bank_of(f"{t}o{m}")[:, 0:T], X[:, m, :], ALU.add))
                rms_norm(f"f2{l}", "ffn2", l)
                half_step(f"f2{l}")

        @block.sync
        def _(sp):
            nxt = [0]

            def slot_free(u):
                if u >= WSLOTS:
                    sp.wait_ge(*freed[u - WSLOTS])

            def load(tag, *pieces):
                u = nxt[0]
                nxt[0] += 1
                assert tags[u] == tag, (tags[u], tag)
                slot_free(u)
                o = 0
                for n, (src, k) in enumerate(pieces):
                    cols = src.shape[1]
                    inc = 48 - 16 * (len(pieces) - 1) if n == 0 else 16
                    sp.dma_start(wring[:, u % WSLOTS, o:o + k * cols].rearrange("p (k n) -> p k n", k=k),
                                 src.rearrange("(k p) n -> p k n", p=P)).then_inc(w_landed[u % WSLOTS], inc)
                    o += k * cols

            def ada(n):
                load(f"ada{n}", (A["w_ada"][:, n * 512:(n + 1) * 512], DC))

            def swiglu(tag, steps, sources):
                u0, d0 = nxt[0], freed[nxt[0]][1] - 1
                assert tags[u0] == f"{tag}.0"

                def step(i, j):
                    u = (u0 + j) % WSLOTS
                    wg, wu, wd = sources(i, j)
                    o = DC * HB
                    for n, src in enumerate((wg, wu)):
                        sp.dma_start(wring[:, u, n * o:(n + 1) * o].rearrange("p (k n) -> p k n", k=DC), src) \
                            .then_inc(w_landed[u], 16)
                    sp.dma_start(wring[:, u, 2 * o:2 * o + D], wd).then_inc(w_landed[u], 16)

                turns, rest = swiglu_turns(steps)
                for j in range(BODY):
                    slot_free(u0 + j)
                    step(0, j)
                with sp.Fori(1, turns) as i:
                    for j in range(BODY):
                        sp.wait_ge(down_done.sem, i * BODY + (d0 + j + 1 - BODY))
                        step(i, j)
                for j in range(rest):
                    sp.wait_ge(down_done.sem, turns * BODY + d0 + j + 1 - BODY)
                    step(turns, j)
                nxt[0] += steps

            def experts(l):
                def sources(i, j):
                    one = bass.ds(i, 1) if not isinstance(i, int) else slice(i, i + 1)
                    return (A["moe_w_gate"][l, one, :, j * HB:(j + 1) * HB].rearrange("e (k p) n -> p (e k) n", p=P),
                            A["moe_w_up"][l, one, :, j * HB:(j + 1) * HB].rearrange("e (k p) n -> p (e k) n", p=P),
                            A["moe_w_down"][l, one, j * HB:(j + 1) * HB, :].rearrange("e p n -> (e p) n"))
                return sources

            def ffn(w_in, w_out):
                def sources(i, j):
                    def cols(o):
                        return bass.ds(i * (BODY * HB) + (o + j * HB), HB)
                    return (w_in[:, cols(0)].rearrange("(k p) n -> p k n", p=P),
                            w_in[:, cols(FF)].rearrange("(k p) n -> p k n", p=P), w_out[cols(0), :])
                return sources

            for n in range(ADA_FIRST):
                ada(n)
            for n in range(2 * DI // 512):
                load(f"a_w_in{n}", (A["a_w_in"][0][:, n * 512:(n + 1) * 512], DC))
                for a in ADA_IN[n]:
                    ada(a)
            for h in range(NH):
                load(f"qk{h}", (A["a_wq"][0, h], DHC), (A["a_wk"][0, h], DHC))
                load(f"v{h}", (A["a_wv"][0, h], DHC))
                for a in ADA_QKV[h]:
                    ada(a)
            for n in range(D // 256):
                load(f"a_w_out{n}", (A["a_w_out"][0][:, n * 256:(n + 1) * 256], DIC))
            swiglu("moe0", NE * FE // HB, experts(0))
            for name, src, o in (("k", A["b_w_kv"], 0), ("v", A["b_w_kv"], D), ("q", A["b_wq"][0], 0)):
                for n in range(2):
                    load(f"b{name}{n}", (src[:, o + n * 512:o + (n + 1) * 512], DC))
            for n in range(2):
                load(f"bo{n}", (A["b_wo"][0][:, n * 512:(n + 1) * 512], DC))
            swiglu("moe1", NE * FE // HB, experts(1))
            for l in range(DEPTH):
                swiglu(f"f1{l}", FF // HB, ffn(A["ffn1_w_in_2"][l], A["ffn1_w_out_2"][l]))
                t, w = f"m{l}.", A["w_in_2"][l]
                for tag, o, n in (("u", O_U, GMW), ("v", O_V, GMW), ("cq", O_CQ, QR), ("ckv", O_CKV, KVR + ROPE),
                                  ("z", O_Z, SI), ("xbc0", O_XBC, 512), ("xbc1", O_XBC + 512, 512 + SH)):
                    load(t + tag, (w[:, o:o + n], DC))
                load(t + "uq", (A["mla_w_uq_2"][l], QR // P))
                load(t + "ukv", (A["mla_w_ukv_2"][l], KVR // P))
                for n in range(NB):
                    for hf in range(2):
                        o = O_G + n * D + hf * 512
                        load(f"{t}g{n}.{hf}", (w[:, o:o + 512], DC))
                    load(f"{t}br{n}", (A["w_branch_2"][l, n], 4))
                for hf in range(2):
                    load(f"{t}o{hf}", (A["w_out_2"][l][:, hf * 512:(hf + 1) * 512], DC))
                swiglu(f"f2{l}", FF // HB, ffn(A["ffn2_w_in_2"][l], A["ffn2_w_out_2"][l]))
            assert nxt[0] == len(tags)
            for i in range(TT):
                for hf in range(2):
                    sp.wait_ge(*drained(f"out{i}.{hf}"))
            sp.dma_start(out[0].rearrange("(i p) d -> p i d", p=P), xo).then_inc(out_landed, 16)
            sp.wait_ge(out_landed, 16)

        @block.gpsimd
        def _(pool):
            g = nc.gpsimd
            n_steps = [0]

            def link(ins):
                ins.then_inc(pool_steps, 1)
                n_steps[0] += 1
                pool.wait_ge(pool_steps, n_steps[0])

            g.memset(ident[:, :], 0.0)
            g.memset(ones[:, :], 1.0)
            g.memset(upper[:, :, :], 1.0)
            g.memset(strict[:, :, :], 1.0)
            g.memset(neg_st[:, :, :], 0.0)
            g.memset(neg_qk[:, :, :], 0.0)
            g.memset(sel[:, :, :], 0.0)
            g.memset(eps_ln[:, :], LN_EPS)
            g.memset(eps_rms[:, :], RMS_EPS)
            inv = 1.0 / (np.float32(10000.0) ** (np.arange(0, ROPE, 2, dtype=np.float32) / np.float32(ROPE)))
            for d in range(HR):
                g.memset(invf[:, d:d + 1], float(np.float32(inv[d])))
            for n in range(NGRP):
                g.memset(rank4[:, n:n + 1], float(NGRP - n))
            for n in range(NE):
                g.memset(rank16[:, n:n + 1], float(NE - n))
            link(g.iota(alibi[:, :, :], pattern=[[-P, TT], [1, T]], base=0, channel_multiplier=-1,
                        allow_small_or_imprecise_dtypes=True))
            r_less_c = dict(pattern=[[P, TT], [-1, T]], base=0, channel_multiplier=1)
            c_less_r = dict(pattern=[[-P, TT], [1, T]], base=0, channel_multiplier=-1)
            g.affine_select(out=ident[:, :], in_=ident[:, :], compare_op=ALU.not_equal, fill=1.0, base=0,
                            pattern=[[-1, P]], channel_multiplier=1)
            g.affine_select(out=upper[:, :, :], in_=upper[:, :, :], compare_op=ALU.is_ge, fill=0.0, **c_less_r)
            g.affine_select(out=strict[:, :, :], in_=strict[:, :, :], compare_op=ALU.is_gt, fill=0.0, **r_less_c)
            g.affine_select(out=neg_st[:, :, :], in_=neg_st[:, :, :], compare_op=ALU.is_ge, fill=NEG, **c_less_r)
            g.affine_select(out=neg_qk[:, :, :], in_=neg_qk[:, :, :], compare_op=ALU.is_ge, fill=NEG, **r_less_c)
            g.affine_select(out=alibi[:, :, :], in_=alibi[:, :, :], compare_op=ALU.is_ge, fill=NEG, **r_less_c)
            g.affine_select(out=sel[:, :, :], in_=sel[:, :, :], compare_op=ALU.not_equal, fill=1.0, base=0,
                            pattern=[[-1, NE], [0, P]], channel_multiplier=1).then_inc(consts_made, 1)


_INS = ['x', 'c', 'w_ada', 'b_ada', 'ln_g', 'ln_b', 'a_w_in', 'a_conv_w', 'a_conv_b', 'a_wq', 'a_wk', 'a_wv', 'a_w_if',
        'a_b_if', 'a_gn_g', 'a_skip', 'a_w_out', 'b_w_kv', 'b_wq', 'b_wo', 'moe_w_router', 'moe_b_router',
        'moe_w_gate', 'moe_w_up', 'moe_w_down', 'positions_2', 'ffn1_norm_2', 'ffn1_w_in_2', 'ffn1_w_out_2',
        'mix_norm_2', 'w_in_2', 'gm_v_norm_2', 'gm_w_s_2', 'gm_b_s_2', 'mla_q_norm_2', 'mla_kv_norm_2', 'mla_w_uq_2',
        'mla_w_ukv_2', 'mla_q_gain_2', 'mla_k_gain_2', 'ssd_conv_w_2', 'ssd_conv_b_2', 'ssd_dt_bias_2', 'ssd_a_log_2',
        'ssd_d_2', 'ssd_norm_2', 'w_branch_2', 'w_out_2', 'ffn2_norm_2', 'ffn2_w_in_2', 'ffn2_w_out_2']


def kernel(**inputs):
    import numpy as _np
    import concourse.bacc as _bacc
    from concourse import mybir as _mybir
    from concourse.bass_utils import run_bass_kernel_spmd as _run

    nc = _bacc.Bacc("TRN2", target_bir_lowering=False, num_devices=1)
    arrays, aps = {}, {}
    for name in _INS:
        a = _np.ascontiguousarray(inputs[name])
        arrays[f"in_{name}"] = a
        aps[name] = nc.dram_tensor(f"in_{name}", a.shape, _mybir.dt.from_np(a.dtype), kind="ExternalInput").ap()
    out = nc.dram_tensor("out", (1, T, D), _mybir.dt.float32, kind="ExternalOutput").ap()
    build(nc, aps, out)
    r = _run(nc, [arrays], core_ids=[0])
    return r.results[0]["out"]
```

```python
from contextlib import ExitStack

import numpy as np

import concourse.bass as bass
from concourse import mybir

F32 = mybir.dt.float32
I32 = mybir.dt.int32
ALU = mybir.AluOpType
ACT = mybir.ActivationFunctionType
AX = mybir.AxisListType

P = 128
T = 256
TT = T // P
D = 1024
DC = D // P
DEPTH = 2
ALPHA = float(np.float32((2.0 * DEPTH) ** 0.25))
LN_EPS = 1e-5
RMS_EPS = 1e-6
NEG = -1e30

NH = 4
DI = 2 * D
DIC = DI // P
DH = DI // NH
DHC = DH // P
CONV = 4
PAD = CONV - 1
AH = 16
AD = D // AH
NE = 16
NGRP = 4
EPG = NE // NGRP
FE = 512
FF = 2816
GMW = 512
GMG = 4
QR = 384
KVR = 256
MH = 8
NOPE = 64
ROPE = 32
HR = ROPE // 2
QK = NOPE + ROPE
MV = 64
SH = 8
SHD = 64
SI = SH * SHD
SG = 2
XBC = SI + 2 * SG * P
O_U, O_V, O_CQ, O_CKV, O_KR = 0, GMW, 2 * GMW, 2 * GMW + QR, 2 * GMW + QR + KVR
O_Z = O_KR + ROPE
O_XBC = O_Z + SI
O_DT = O_XBC + XBC
O_G = O_DT + SH
NB = 3

WSLOTS = 4
WCOLS = DC * (512 + SH)
ADA_FIRST = 6
ADA_UNITS = (DEPTH * 6 + 2) * D // 512
ADA_IN = [[n for n in range(ADA_FIRST, ADA_UNITS) if (n - ADA_FIRST) * 8 // (ADA_UNITS - ADA_FIRST) == i]
          for i in range(8)]
HB = 128
SLOTS = 64
PAIRS = NE // 2
PAIR_UNITS = 6
PAIR_LOOP = (1, PAIRS // 2 - 1)
PAIR_STEPS = ("g", "u", "xg0", "xg1", "hT", "S", "d0", "d1")
LAST_STEPS = ("g", "u", "hT", "S", "d0", "d1")
BODY = 4

TABLE = [
    [("b_ada", 112), ("c", 8), ("kvn", 4)],
    [("ln_g", 32), ("ln_b", 32), ("conv_w", 64)],
    [("conv_b", 16), ("gn_g", 16), ("skip", 16), ("ffn1", 16), ("mix", 16), ("ffn2", 16), ("gmv", 8), ("ssdn", 8),
     ("qn", 6)],
    [("conv_w2", 64), ("conv_b2", 16)],
]

SOURCES = {"b_ada": "b_ada", "c": "c", "kvn": "mla_kv_norm_2", "ln_g": "ln_g", "ln_b": "ln_b", "conv_w": "a_conv_w",
           "conv_b": "a_conv_b", "gn_g": "a_gn_g", "skip": "a_skip", "ffn1": "ffn1_norm_2", "mix": "mix_norm_2",
           "ffn2": "ffn2_norm_2", "gmv": "gm_v_norm_2", "ssdn": "ssd_norm_2", "qn": "mla_q_norm_2",
           "conv_w2": "ssd_conv_w_2", "conv_b2": "ssd_conv_b_2"}


class Signal:

    def __init__(self, sem):
        self.sem, self.seen = sem, {}

    def upto(self, who, n=1):
        self.seen[who] = self.seen.get(who, 0) + n
        return self.seen[who]


def build(nc, A, out):
    ctx = ExitStack()
    with ctx:
        def sb(name, shape, dt=F32):
            return ctx.enter_context(nc.sbuf_tensor(name, shape, dt))

        def sem(name):
            return ctx.enter_context(nc.semaphore(name))

        wring = sb("wring", [P, WSLOTS, WCOLS])
        X = sb("X", [P, DC, T])
        H = sb("H", [P, DC, T])
        H2 = sb("H2", [P, DC, T])
        SQ = sb("SQ", [P, DC, T])
        arena = sb("arena", [P, 18904])
        pcol = sb("pcol", [P, 4, P])
        ident = sb("ident", [P, P])
        ones = sb("ones", [P, P])
        upper = sb("upper", [P, TT, T])
        strict = sb("strict", [P, TT, T])
        neg_st = sb("neg_st", [P, TT, T])
        neg_qk = sb("neg_qk", [P, TT, T])
        alibi = sb("alibi", [P, TT, T])
        slot_no = sb("slot_no", [P, SLOTS])
        over_flag = sb("over_flag", [1, DEPTH], I32)
        mods = sb("mods", [P, 112])
        gmw = sb("gmw", [P, DEPTH, GMG, P])
        bsb = sb("bsb", [P, DEPTH, GMG, P])
        gainb = sb("gainb", [P, 2, DEPTH, QK])
        wr = sb("wr", [P, DC, NE])
        wif = sb("wif", [P, DIC, 2 * NH])
        bif = sb("bif", [NH, 2])
        brb = sb("brb", [P, NE])
        dtb = sb("dtb", [P, DEPTH, SH])
        alb = sb("alb", [P, DEPTH, SH])
        dsk = sb("dsk", [P, DEPTH, SI // P])
        posi = sb("posi", [P, TT], I32)
        posf = sb("posf", [P, TT])
        invf = sb("invf", [P, HR])
        trig = sb("trig", [P, 2, TT, HR])
        rank4 = sb("rank4", [P, NGRP])
        rank16 = sb("rank16", [P, NE])
        eps_ln = sb("eps_ln", [P, 1])
        eps_rms = sb("eps_rms", [P, 1])
        one_c = sb("one_c", [P, 1])
        nrm = sb("nrm", [P, 2, T])
        sm = sb("sm", [P, 540])

        bank = [ctx.enter_context(nc.psum_tensor(f"bank{i}", [P, 512], F32)) for i in range(4)]
        yacc = [ctx.enter_context(nc.psum_tensor(f"yacc{i}", [P, 512], F32)) for i in range(4)]

        def ysum(m):
            return yacc[m // 2][:, (m % 2) * T:(m % 2 + 1) * T]

        def view(off, *shape, parts=P):
            n = int(np.prod(shape))
            v = arena[0:parts, off:off + n]
            if len(shape) == 2:
                return v.rearrange("p (a b) -> p a b", a=shape[0])
            if len(shape) == 3:
                return v.rearrange("p (a b c) -> p a b c", a=shape[0], b=shape[1])
            return v

        col = {}
        for t, rows in enumerate(TABLE):
            r = 0
            for name, n in rows:
                col[name] = (t, r)
                r += n

        def vec(name, i):
            t, r = col[name]
            return pcol[:, t, r + i:r + i + 1]

        def mod(layer, s, which, k):
            i = ((layer * 2 + s) * 3 + which) * DC + k
            return mods[:, i:i + 1]

        def kvmod(which, k):
            i = DEPTH * 6 * DC + which * DC + k
            return mods[:, i:i + 1]

        w_landed = [sem(f"w_landed{i}") for i in range(WSLOTS)]
        bank_full = [sem(f"bank_full{i}") for i in range(4)]
        bank_drained = [sem(f"bank_drained{i}") for i in range(4)]
        consts_made = sem("consts_made")
        rows_landed = sem("rows_landed")
        small_landed = sem("small_landed")
        x_landed = sem("x_landed")
        out_landed = sem("out_landed")
        pool_steps = sem("pool_steps")
        act_steps = sem("act_steps")
        dve_steps = sem("dve_steps")
        consts_derived = sem("consts_derived")
        c_ready = sem("c_ready")
        h_ready = Signal(sem("h_ready"))
        h2_ready = Signal(sem("h2_ready"))
        x_ready = Signal(sem("x_ready"))
        sum_ready = Signal(sem("sum_ready"))
        centered = Signal(sem("centered"))
        squared = Signal(sem("squared"))
        conv_summed = Signal(sem("conv_summed"))
        conv_ready = Signal(sem("conv_ready"))
        pad_cleared = Signal(sem("pad_cleared"))
        exp_ready = Signal(sem("exp_ready"))
        plus_one = Signal(sem("plus_one"))
        ln_ready = Signal(sem("ln_ready"))
        rows_made = Signal(sem("rows_made"))
        stab_ready = Signal(sem("stab_ready"))
        emt_ready = Signal(sem("emt_ready"))
        dlog_ready = Signal(sem("dlog_ready"))
        wexp_ready = Signal(sem("wexp_ready"))
        head_ready = Signal(sem("head_ready"))
        hc_ready = Signal(sem("hc_ready"))
        hsq_ready = Signal(sem("hsq_ready"))
        router_exp = Signal(sem("router_exp"))
        route_ready = Signal(sem("route_ready"))
        silu_ready = Signal(sem("silu_ready"))
        slots_ready = sem("slots_ready")
        gated_ready = sem("gated_ready")
        over_summed = sem("over_summed")
        flagged = sem("flagged")
        scattered = sem("scattered")
        over_landed, over_filled, over_moved, over_up, over_silu, over_scaled, over_hid, over_down = (
            [sem(f"over_{what}{l}") for l in range(DEPTH)]
            for what in ("landed", "filled", "moved", "up", "silu", "scaled", "hid", "down"))
        down_done = Signal(sem("down_done"))
        score_ready = Signal(sem("score_ready"))
        prob_exp = Signal(sem("prob_exp"))
        prob_ready = Signal(sem("prob_ready"))
        rope_in = Signal(sem("rope_in"))
        rope_ready = Signal(sem("rope_ready"))
        vsq_ready = Signal(sem("vsq_ready"))
        vn_ready = Signal(sem("vn_ready"))
        sp_ready = Signal(sem("sp_ready"))
        qksq_ready = Signal(sem("qksq_ready"))
        qkss_ready = Signal(sem("qkss_ready"))
        qkstd_ready = Signal(sem("qkstd_ready"))
        qkrot_ready = Signal(sem("qkrot_ready"))
        lat_ready = Signal(sem("lat_ready"))
        abs_ready = Signal(sem("abs_ready"))
        aexp_ready = Signal(sem("aexp_ready"))
        decay_in = Signal(sem("decay_in"))
        decay_ready = Signal(sem("decay_ready"))
        sp_mm_ready = Signal(sem("sp_mm_ready"))
        yz_ready = Signal(sem("yz_ready"))
        yc_ready = Signal(sem("yc_ready"))
        merged_ready = Signal(sem("merged_ready"))
        ysilu_ready = Signal(sem("ysilu_ready"))

        N_CONST = 1
        N_SMALL = 15

        uses = {}
        freed = []
        tags = []

        def bank_of(name):
            return bank[uses[name] % 4]

        def full(name):
            k = uses[name]
            return bank_full[k % 4], k // 4 + 1

        def drained(name):
            k = uses[name]
            return bank_drained[k % 4], k // 4 + 1

        def drain_sem(name):
            return bank_drained[uses[name] % 4]

        def pair_use(l, i, odd, step):
            steps = LAST_STEPS if isinstance(i, int) and 2 * i + odd == PAIRS - 1 else PAIR_STEPS
            k = uses[f"moe{l}.g0"] + len(PAIR_STEPS) * odd + steps.index(step)
            return k % 4, i * (2 * len(PAIR_STEPS) // 4) + k // 4

        def pair_full(l, i, odd, step):
            b, n = pair_use(l, i, odd, step)
            return bank_full[b], n + 1

        def pair_drained(l, i, odd, step):
            b, n = pair_use(l, i, odd, step)
            return bank_drained[b], n + 1

        def pair_bank(l, i, odd, step):
            return bank[pair_use(l, i, odd, step)[0]]

        def pair_drain_sem(l, i, odd, step):
            return bank_drained[pair_use(l, i, odd, step)[0]]

        def all_pairs(eng, pair):
            for odd in range(2):
                pair(0, odd)
            with eng.Fori(*PAIR_LOOP) as turn:
                for odd in range(2):
                    pair(turn, odd)
            for odd in range(2):
                pair(PAIRS // 2 - 1, odd)

        prow = view(0, 4, P)
        xin = view(512, TT, D)
        xm = view(0, DIC, PAD + T)
        xc = view(4144, DIC, T)
        sz = view(8240, DIC, T)
        qm = view(12336, DHC, T)
        km = view(13360, DHC, T)
        Pm = [view(14384 + 512 * i, TT, T) for i in range(2)]
        Wm = [view(15408 + 512 * i, TT, T) for i in range(2)]
        lrow = [view(16432 + T * i, T, parts=NH) for i in range(8)]
        den_s = view(18480, T)

        def vm(h, i):
            c = 4 * (h % 2) + 2 * i
            return SQ[:, c:c + 2, :].rearrange("p a t -> p (a t)")

        cT = H2[:, 0, :].rearrange("p (k n) -> p k n", k=DC)
        adar = [SQ[:, 2 * i:2 * i + 2, :].rearrange("p a t -> p (a t)") for i in range(2)]
        hm = H2[:, 0:DHC, :]
        hsq = H2[:, DHC:2 * DHC, :]
        Htok = view(0, TT, D)
        XG = view(2048, DC, P)
        slot = view(3072, TT, 2, SLOTS)
        slot_g = view(3328, TT, 2, SLOTS)
        sge = view(3584, FE)
        hide = view(4096, FE)
        hidT = view(4608, FE // P, P)
        ye = view(5120, D)
        S_e = view(6144, T)
        gbc = view(8192, NE, T)
        gT = view(12288, T, parts=NE)
        sg_o, sgw_o, hid_o = (view(12544 + 256 * i, T) for i in range(3))
        sg = [view(4096 + 256 * i, T) for i in range(2)]
        hid = [view(5120 + 256 * i, T) for i in range(2)]
        gate_t, mask_t, number_t, gate_o = (
            sm[:, a:a + TT * NE].rearrange("p (n m) -> p n m", n=TT) for a in (0, 304, 336, 200))
        qa = view(0, DC, T)
        ka = view(2048, DC, T)
        va = view(4096, TT, D)
        oa = view(6144, DC, T)
        Es = [view(15832 + 512 * i, TT, T) for i in range(2)]
        Ss = [view(16856 + 512 * i, TT, T) for i in range(2)]
        PTs = [view(17880 + 512 * i, TT, T) for i in range(2)]
        yA, yB, yC = (view(1024 * i, 4, T) for i in range(3))
        zs = view(3072, 4, T)
        xb = view(4096, 8, PAD + T)
        xv = view(6168, 8, T)
        us = view(8216, 4, T)
        vn = view(9240, TT, GMW)
        cq = view(10264, 3, T)
        ckv = view(11032, 2, T)
        krs = view(11544, TT, ROPE)
        wT = view(11608, GMG, P)
        Vt = view(12120, TT, MH * MV)
        O2 = 12760 + 384
        Qt = view(O2, TT, MH, QK)
        Kt = view(O2 + 1536, TT, MH, QK)
        qksq = view(O2 + 3072, 1536)
        rt = [view(O2 + 4608 + T * i, TT, MH, HR) for i in range(4)]
        QT, KT = H2, SQ
        xdt = view(O2, TT, SI)
        Mh = [view(O2 + 1024 + 512 * i, TT, T) for i in range(2)]
        Eh = [view(O2 + 2048 + 512 * i, TT, T) for i in range(2)]
        Ph = [view(O2 + 3072 + 512 * i, TT, T) for i in range(2)]
        CB = [view(O2 + 4096 + 512 * i, TT, T) for i in range(SG)]
        sig = [view(O2 + 2048 * i, DC, T) for i in range(2)]
        xo = view(0, TT, D)

        block = ctx.enter_context(nc.Block())

        @block.tensor
        def _(pe):
            mm = nc.tensor.matmul

            def fill(name):
                k = len(uses)
                uses[name] = k
                if k >= 4:
                    pe.wait_ge(bank_drained[k % 4], k // 4)
                return bank[k % 4]

            def filled(name, ins):
                ins.then_inc(bank_full[uses[name] % 4], 1)

            def weights(tag):
                u = len(tags)
                tags.append(tag)
                freed.append(None)
                pe.wait_ge(w_landed[u % WSLOTS], 48 * (u // WSLOTS + 1))
                return wring[:, u % WSLOTS, :]

            def used_by(name):
                freed[-1] = full(name)

            def product(name, w, rhs, fresh=None, part=P):
                b = fill(name)
                n = w.shape[1]
                for k in range(n):
                    if fresh is not None:
                        pe.wait_ge(fresh.sem, fresh.upto("pe"))
                    last = mm(b[0:part, 0:T], w[:, k, :], rhs[:, k, :], start=(k == 0), stop=(k == n - 1))
                filled(name, last)

            def column_sums(name, src, n, fresh=None, moved=None):
                b = fill(name)
                for k in range(n):
                    if fresh is not None:
                        pe.wait_ge(fresh.sem, fresh.upto("pe"))
                    if moved is not None:
                        pe.wait_ge(*drained(f"{moved}{k}"))
                    last = mm(b[:, 0:T], ones[:, :], src[:, k, :], start=(k == 0), stop=(k == n - 1))
                filled(name, last)

            pe.wait_ge(consts_made, N_CONST)
            pe.wait_ge(rows_landed, 16 * sum(len(r) for r in TABLE))
            for t, rows in enumerate(TABLE):
                n = sum(m for _, m in rows)
                b = fill(f"table{t}")
                filled(f"table{t}", nc.tensor.transpose(b[:, 0:n], prow[0:n, t, :], ident[0:n, 0:n]))
            pe.wait_ge(x_landed, 16)
            for kk in range(DC // 2):
                b = fill(f"x{kk}")
                for k in range(2 * kk, 2 * kk + 2):
                    for i in range(TT):
                        o = (k % 2) * T + i * P
                        last = nc.tensor.transpose(b[:, o:o + P], xin[:, i, k * P:(k + 1) * P], ident[:, :])
                filled(f"x{kk}", last)

            def ada_unit(n):
                w = weights(f"ada{n}")[:, 0:DC * 512].rearrange("p (k n) -> p k n", k=DC)
                b = fill(f"ada{n}")
                for k in range(DC):
                    g = 32 * (k % 4)
                    last = mm(b[g:g + 32, :], cT[:, k, :], w[:, k, :], start=(k < 4), stop=(k >= DC - 4),
                              skip_group_check=True)
                filled(f"ada{n}", last)
                used_by(f"ada{n}")

            def ada_turn(n):
                pe.wait_ge(*drained(f"ada{n}"))
                b = fill(f"adaT{n}")
                for m in range(4):
                    last = nc.tensor.transpose(b[:, m * P:(m + 1) * P], adar[n % 2][:, m * P:(m + 1) * P], ident[:, :])
                filled(f"adaT{n}", last)

            pe.wait_ge(c_ready, 1)
            for n in range(ADA_FIRST):
                ada_unit(n)
                if n > 0:
                    ada_turn(n - 1)
            ada_turn(ADA_FIRST - 1)

            for n in range(2 * DI // 512):
                w = weights(f"a_w_in{n}")[:, 0:DC * 512].rearrange("p (k n) -> p k n", k=DC)
                for m in range(4):
                    product(f"w_in{4 * n + m}", w[:, :, m * P:(m + 1) * P], H, h_ready if n + m == 0 else None)
                used_by(f"w_in{4 * n + 3}")
                for a in ADA_IN[n]:
                    ada_unit(a)
                    if a > ADA_FIRST:
                        ada_turn(a - 1)
            ada_turn(ADA_UNITS - 1)
            pe.wait_ge(small_landed, 16 * N_SMALL)
            pe.wait_ge(conv_ready.sem, conv_ready.upto("pe", DIC))
            for g in range(2):
                b = fill(f"gate{g}")
                for k in range(DIC):
                    last = mm(b[0:NH, 0:T], wif[:, k, g * NH:(g + 1) * NH], xc[:, k, :],
                              start=(k == 0), stop=(k == DIC - 1))
                filled(f"gate{g}", last)

            def mlstm_num(h):
                pe.wait_ge(*drained(f"mS{h}"))
                b = fill(f"den{h}")
                mm(b[:, 0:T], ones[:, :], Pm[h % 2][:, 0, :], start=True, stop=False)
                filled(f"den{h}", mm(b[:, P:T], ones[:, :], Pm[h % 2][:, 1, P:T], start=False, stop=True))
                pe.wait_ge(*drained(f"v{h}.0"))
                pe.wait_ge(*drained(f"v{h}.1"))
                for a in range(2):
                    b = fill(f"num{h}.{a}")
                    for m in range(2 * a, 2 * a + 2):
                        o = (m % 2) * T
                        mm(b[:, o:o + T], vm(h, 0)[:, m * P:(m + 1) * P], Pm[h % 2][:, 0, :], start=True, stop=False)
                        last = mm(b[:, o + P:o + T], vm(h, 1)[:, m * P:(m + 1) * P], Pm[h % 2][:, 1, P:T],
                                  start=False, stop=True)
                    filled(f"num{h}.{a}", last)

            def mlstm_mean(h):
                for a in range(2):
                    pe.wait_ge(*drained(f"num{h}.{a}"))
                column_sums(f"gmean{h}", hm, DHC)

            def mlstm_var(h):
                pe.wait_ge(hsq_ready.sem, hsq_ready.upto("pe"))
                column_sums(f"gvar{h}", hsq, DHC)

            for h in range(NH):
                c = DHC * h
                w = weights(f"qk{h}")[:, 0:2 * DHC * DH].rearrange("p (g k n) -> p g k n", g=2, k=DHC)
                for m in range(DHC):
                    product(f"q{h}.{m}", w[:, 0, :, m * P:(m + 1) * P], xc[:, c:c + DHC, :])
                if h > 0:
                    mlstm_num(h - 1)
                for m in range(DHC):
                    product(f"k{h}.{m}", w[:, 1, :, m * P:(m + 1) * P], xc[:, c:c + DHC, :])
                used_by(f"k{h}.{DHC - 1}")
                if h > 0:
                    mlstm_mean(h - 1)
                w = weights(f"v{h}")[:, 0:DHC * DH].rearrange("p (k n) -> p k n", k=DHC)
                for i in range(TT):
                    b = fill(f"v{h}.{i}")
                    for k in range(DHC):
                        last = mm(b[:, :], xm[:, c + k, PAD + i * P:PAD + (i + 1) * P], w[:, k, :],
                                  start=(k == 0), stop=(k == DHC - 1))
                    filled(f"v{h}.{i}", last)
                used_by(f"v{h}.{TT - 1}")
                if h == 0:
                    pe.wait_ge(stab_ready.sem, stab_ready.upto("pe"))
                    b = fill("ucol")
                    for i in range(TT):
                        last = nc.tensor.transpose(b[:, i * NH:(i + 1) * NH], lrow[3][:, i * P:(i + 1) * P],
                                                   ident[0:NH, 0:NH])
                    filled("ucol", last)
                else:
                    mlstm_var(h - 1)
                for m in range(DHC):
                    pe.wait_ge(*drained(f"q{h}.{m}"))
                    pe.wait_ge(*drained(f"k{h}.{m}"))
                b = fill(f"mS{h}")
                for k in range(DHC):
                    mm(b[:, 0:T], km[:, k, 0:P], qm[:, k, :], start=(k == 0), stop=(k == DHC - 1))
                for k in range(DHC):
                    last = mm(b[:, T + P:2 * T], km[:, k, P:T], qm[:, k, P:T], start=(k == 0), stop=(k == DHC - 1))
                filled(f"mS{h}", last)
                if h == 0:
                    pe.wait_ge(emt_ready.sem, emt_ready.upto("pe"))
                b = fill(f"mbc{h}")
                mm(b[:, 0:T], ident[0:NH, h:h + 1].broadcast_to([NH, P]), lrow[5][:, :], start=True, stop=True)
                filled(f"mbc{h}", mm(b[:, T:2 * T], ident[0:NH, h:h + 1].broadcast_to([NH, P]), lrow[6][:, :], start=True, stop=True))
            mlstm_num(NH - 1)
            mlstm_mean(NH - 1)
            mlstm_var(NH - 1)
            for n in range(D // 256):
                w = weights(f"a_w_out{n}")[:, 0:DIC * 256].rearrange("p (k n) -> p k n", k=DIC)
                if n == 0:
                    pe.wait_ge(head_ready.sem, head_ready.upto("pe", NH))
                for m in range(2):
                    product(f"y0.{2 * n + m}", w[:, :, m * P:(m + 1) * P], xc)
                used_by(f"y0.{2 * n + 1}")

            def layer_norm(tag, y=None):
                column_sums(f"{tag}.mean", X, DC, None if y else sum_ready, y)
                column_sums(f"{tag}.var", SQ, DC, squared)

            def rms_norm(tag):
                column_sums(f"{tag}.ms", SQ, DC, squared)

            def swiglu(tag, steps, fresh=None):
                u0, k0, d0 = len(tags), len(uses), down_done.upto("base", 0)

                def up(i, j, fresh=None):
                    u, k = u0 + j, k0 + j
                    w = wring[:, u % WSLOTS, 0:2 * DC * HB].rearrange("p (g k n) -> p g k n", g=2, k=DC)
                    pe.wait_ge(w_landed[u % WSLOTS], i * 48 + 48 * (u // WSLOTS + 1))
                    pe.wait_ge(bank_drained[k % 4], i + k // 4)
                    b = bank[k % 4]
                    for g in range(2):
                        for c in range(DC):
                            if fresh is not None and g == 0:
                                pe.wait_ge(fresh.sem, fresh.upto("pe"))
                            last = mm(b[:, g * T:(g + 1) * T], w[:, g, c, :], H[:, c, :],
                                      start=(c == 0), stop=(c == DC - 1))
                    last.then_inc(bank_full[k % 4], 1)

                def down(i, j, first=False, final=False):
                    u, k = u0 + j, k0 + j
                    w = wring[:, u % WSLOTS, 2 * DC * HB:2 * DC * HB + D]
                    pe.wait_ge(bank_drained[k % 4], i + k // 4 + 1)
                    for m in range(DC):
                        last = mm(ysum(m), w[:, m * P:(m + 1) * P], hid[j % 2], start=first and m % 2 == 0,
                                  stop=final and m % 2 == 1, skip_group_check=True)
                    last.then_inc(down_done.sem, 1)

                up(0, 0, fresh)
                turns, rest = divmod(steps - 1, BODY)
                for j in range(BODY):
                    up(0, j + 1)
                    down(0, j, first=(j == 0))
                with pe.Fori(1, turns) as i:
                    for j in range(BODY):
                        up(i, j + 1)
                        down(i, j)
                for j in range(rest):
                    up(turns, j + 1)
                    down(turns, j)
                down(turns, rest, final=True)
                for s in range(steps):
                    uses[f"{tag}.{s}"] = k0 + s
                    tags.append(f"{tag}.{s}")
                    freed.append((down_done.sem, d0 + s + 1))
                down_done.upto("base", steps)

            def routing(l):
                b = fill(f"logits{l}")
                for i in range(TT):
                    for k in range(DC):
                        if i == 0:
                            pe.wait_ge(h_ready.sem, h_ready.upto("pe"))
                        last = mm(b[:, i * NE:(i + 1) * NE], H[:, k, i * P:(i + 1) * P], wr[:, k, :],
                                  start=(k == 0), stop=(k == DC - 1))
                filled(f"logits{l}", last)
                for n in range(2 * TT):
                    i, half = divmod(n, 2)
                    b = fill(f"ht{l}.{n}")
                    for c in range(4):
                        last = nc.tensor.transpose(b[:, c * P:(c + 1) * P], H[:, 4 * half + c, i * P:(i + 1) * P],
                                                   ident[:, :])
                    filled(f"ht{l}.{n}", last)
                pe.wait_ge(route_ready.sem, route_ready.upto("pe"))
                b = fill(f"rank{l}")
                for i in range(TT):
                    for j in range(i + 1):
                        last = mm(b[:, i * NE:(i + 1) * NE], upper[:, j, i * P:(i + 1) * P], mask_t[:, j, :],
                                  start=(j == 0), stop=(j == i))
                filled(f"rank{l}", last)

            def gather(banks):
                for k in range(DC):
                    for i in range(TT):
                        last = mm(banks[k // 4][:, (k % 4) * P:(k % 4 + 1) * P], Htok[:, i, k * P:(k + 1) * P],
                                  slot[:, i, :, :].rearrange("p e s -> p (e s)"), start=(i == 0), stop=(i == TT - 1))
                    if k % 4 == 3:
                        yield last

            def moe(l):
                for n in range(2 * TT):
                    pe.wait_ge(*drained(f"ht{l}.{n}"))
                pe.wait_ge(slots_ready, PAIRS * l + 1)
                names = [f"xg{l}.{n}" for n in range(2)]
                for name, ins in zip(names, gather([fill(name) for name in names])):
                    filled(name, ins)
                pe.wait_ge(over_summed, l + 1)
                b = fill(f"over{l}")
                filled(f"over{l}", mm(b[0:1, 0:1], sm[:, 264:265], ones[:, 0:1], start=True, stop=True))

                u0, k0 = len(tags), len(uses)
                uses[f"moe{l}.g0"] = k0

                def unit(i, odd, n, k, cols):
                    u = u0 + PAIR_UNITS * odd + n
                    pe.wait_ge(w_landed[u % WSLOTS], i * (48 * 2 * PAIR_UNITS // WSLOTS) + 48 * (u // WSLOTS + 1))
                    return wring[:, u % WSLOTS, 0:k * cols].rearrange("p (k n) -> p k n", k=k)

                def take(i, odd, step):
                    b, n = pair_use(l, i, odd, step)
                    pe.wait_ge(bank_drained[b], n)
                    return bank[b]

                def done(i, odd, step, ins):
                    ins.then_inc(bank_full[pair_use(l, i, odd, step)[0]], 1)

                def halves(b, x, n, w, cols):
                    for k in range(n):
                        for e in range(2):
                            last = mm(b[e * SLOTS:(e + 1) * SLOTS, :], x[:, k, e * SLOTS:(e + 1) * SLOTS], w[e][:, k, cols],
                                      start=(k == 0), stop=(k == n - 1), skip_group_check=True)
                    return last

                def pair(i, odd):
                    first, last_pair = (isinstance(i, int) and 2 * i + odd == p for p in (0, PAIRS - 1))
                    for n in range(2):
                        pe.wait_ge(*(drained(names[n]) if first else pair_drained(l, i, odd - 1, f"xg{n}")))
                    for n, step in enumerate(("g", "u")):
                        w = [unit(i, odd, 2 * n + e, DC, FE) for e in range(2)]
                        done(i, odd, step, halves(take(i, odd, step), XG, DC, w, slice(0, FE)))
                    if not last_pair:
                        pe.wait_ge(slots_ready, i * 2 + (PAIRS * l + odd + 2))
                        for n, ins in enumerate(gather([take(i, odd, f"xg{n}") for n in range(2)])):
                            done(i, odd, f"xg{n}", ins)
                    pe.wait_ge(*pair_drained(l, i, odd, "u"))
                    b = take(i, odd, "hT")
                    for c in range(FE // P):
                        last = nc.tensor.transpose(b[:, c * P:(c + 1) * P], hide[:, c * P:(c + 1) * P], ident[:, :])
                    done(i, odd, "hT", last)
                    pe.wait_ge(gated_ready, i * 2 + (PAIRS * l + odd + 1))
                    b = take(i, odd, "S")
                    for j in range(TT):
                        last = nc.tensor.transpose(b[:, j * P:(j + 1) * P],
                                                   slot_g[:, j, :, :].rearrange("p e s -> p (e s)"), ident[:, :])
                    done(i, odd, "S", last)
                    w = [unit(i, odd, 4 + e, FE // P, D) for e in range(2)]
                    pe.wait_ge(*pair_drained(l, i, odd, "hT"))
                    for n in range(2):
                        done(i, odd, f"d{n}", halves(take(i, odd, f"d{n}"), hidT, FE // P, w, slice(n * 512, (n + 1) * 512)))
                    for step in ("S", "d0", "d1"):
                        pe.wait_ge(*pair_drained(l, i, odd, step))
                    for m in range(DC):
                        last = mm(ysum(m), ye[:, m * P:(m + 1) * P], S_e, start=first and m % 2 == 0,
                                  stop=last_pair and m % 2 == 1, skip_group_check=True)
                    last.then_inc(scattered, 1)

                all_pairs(pe, pair)
                for p in range(PAIRS):
                    i, odd = divmod(p, 2)
                    for step in LAST_STEPS if p == PAIRS - 1 else PAIR_STEPS:
                        uses[f"moe{l}.{step}{p}"] = len(uses) if (step, p) != ("g", 0) else k0
                    for n in range(PAIR_UNITS):
                        tags.append(f"moe{l}.{p}.{n}")
                        freed.append(pair_full(l, i, odd, ("g", "u", "d1")[n // 2]))
                last_uses = sorted(uses.values())[-4:]
                pe.wait_ge(flagged, l + 1)
                flag = pe.value_load(over_flag[0:1, l:l + 1], min_val=0, max_val=1)
                with pe.If(flag > 0):
                    general(l, last_uses)

            def general(l, last_uses):
                for k in last_uses:
                    pe.wait_ge(bank_drained[k % 4], k // 4 + 1)
                for i in range(TT):
                    last = nc.tensor.transpose(bank[0][0:NE, i * P:(i + 1) * P],
                                               gate_o[:, i, :], ident[:, :])
                last.then_inc(over_filled[l], 1)
                for e in range(0, NE, 2):
                    pe.wait_ge(over_moved[l], e // 2 + 1)
                    for o in range(2):
                        last = mm(bank[0][:, o * T:(o + 1) * T], ident[0:NE, e + o:e + o + 1].broadcast_to([NE, P]), gT,
                                  start=True, stop=True)
                    last.then_inc(over_filled[l], 1)
                w = [wring[:, n, 0:DC * FE].rearrange("p (k n) -> p k n", k=DC) for n in range(2)]
                wd = wring[:, 2, 0:FE * D // P].rearrange("p (k n) -> p k n", k=FE // P)
                blocks = FE // HB
                with pe.Fori(0, NE) as e:
                    pe.wait_ge(over_landed[l], e * 48 + 48)
                    for n in range(blocks):
                        for g in range(2):
                            for k in range(DC):
                                last = mm(bank[1][:, g * T:(g + 1) * T], w[g][:, k, n * HB:(n + 1) * HB], H[:, k, :],
                                          start=(k == 0), stop=(k == DC - 1))
                        last.then_inc(over_up[l], 1)
                        pe.wait_ge(over_hid[l], e * blocks + n + 1)
                        for m in range(DC):
                            last = mm(ysum(m), wd[:, n, m * P:(m + 1) * P], hid_o, start=False, stop=False,
                                      skip_group_check=True)
                        last.then_inc(over_down[l], 1)

            def attention(tag, heads, q_of, k_of, v_of):
                def scores(h):
                    b = fill(f"{tag}.s{h}")
                    mm(b[:, 0:P], q_of(h)[:, 0:P], k_of(h)[:, 0:P], start=True, stop=True)
                    filled(f"{tag}.s{h}", mm(b[:, T:2 * T], q_of(h)[:, P:T], k_of(h), start=True, stop=True))

                def turn(h):
                    pe.wait_ge(prob_ready.sem, prob_ready.upto("pe"))
                    b = fill(f"{tag}.p{h}")
                    E = Es[h % 2]
                    nc.tensor.transpose(b[:, 0:P], E[:, 0, 0:P], ident[:, :])
                    nc.tensor.transpose(b[:, P:T], E[:, 1, 0:P], ident[:, :])
                    filled(f"{tag}.p{h}", nc.tensor.transpose(b[:, T + P:2 * T], E[:, 1, P:T], ident[:, :]))

                def values(h):
                    pe.wait_ge(*drained(f"{tag}.p{h}"))
                    b = fill(f"{tag}.o{h}") if h % 2 == 0 else bank_of(f"{tag}.o{h - 1}")
                    r = 64 * (h % 2)
                    mm(b[r:r + 64, 0:T], v_of(h, 0), PTs[h % 2][:, 0, :], start=True, stop=False)
                    last = mm(b[r:r + 64, P:T], v_of(h, 1), PTs[h % 2][:, 1, P:T], start=False, stop=True)
                    if h % 2:
                        filled(f"{tag}.o{h - 1}", last)

                for it in range(heads + 2):
                    if it < heads:
                        scores(it)
                    if 1 <= it <= heads:
                        turn(it - 1)
                    if it >= 2:
                        values(it - 2)

            layer_norm("ln00", "y0.")
            routing(0)
            moe(0)
            layer_norm("ln01")

            for name, src, fresh in (("k", H2, h2_ready), ("v", H2, None), ("q", H, h_ready)):
                for n in range(2):
                    w = weights(f"b{name}{n}")[:, 0:DC * 512].rearrange("p (k n) -> p k n", k=DC)
                    if name == "v":
                        for i in range(TT):
                            b = fill(f"bv{n}.{i}")
                            for k in range(DC):
                                last = mm(b[:, :], H2[:, k, i * P:(i + 1) * P], w[:, k, :],
                                          start=(k == 0), stop=(k == DC - 1))
                            filled(f"bv{n}.{i}", last)
                        used_by(f"bv{n}.{TT - 1}")
                        continue
                    for m in range(4):
                        product(f"b{name}{4 * n + m}", w[:, :, m * P:(m + 1) * P], src, fresh if n + m == 0 else None)
                    used_by(f"b{name}{4 * n + 3}")
            for m in range(DC):
                pe.wait_ge(*drained(f"bk{m}"))
                pe.wait_ge(*drained(f"bq{m}"))
            for n in range(2):
                for i in range(TT):
                    pe.wait_ge(*drained(f"bv{n}.{i}"))
            attention("moba", AH, lambda h: qa[64 * (h % 2):64 * (h % 2) + 64, h // 2, :],
                      lambda h: ka[64 * (h % 2):64 * (h % 2) + 64, h // 2, :],
                      lambda h, i: va[:, i, h * AD:(h + 1) * AD])
            for n in range(2):
                w = weights(f"bo{n}")[:, 0:DC * 512].rearrange("p (k n) -> p k n", k=DC)
                if n == 0:
                    for h in range(0, AH, 2):
                        pe.wait_ge(*drained(f"moba.o{h}"))
                for m in range(4):
                    product(f"y1.{4 * n + m}", w[:, :, m * P:(m + 1) * P], oa)
                used_by(f"y1.{4 * n + 3}")
            layer_norm("ln10", "y1.")
            routing(1)
            moe(1)
            layer_norm("ln11")

            for l in range(DEPTH):
                rms_norm(f"f1{l}")
                swiglu(f"f1{l}", FF // HB, h_ready)
                rms_norm(f"mx{l}")
                t = f"m{l}."

                def unit(tag, k, n):
                    return weights(t + tag)[:, 0:k * n].rearrange("p (k n) -> p k n", k=k)

                w = unit("u", DC, GMW)
                for m in range(4):
                    product(f"{t}u{m}", w[:, :, m * P:(m + 1) * P], H, h_ready if m == 0 else None)
                used_by(f"{t}u3")

                def token_major(name, i, w, src, n):
                    b = fill(name)
                    for k in range(w.shape[1]):
                        last = mm(b[:, 0:n], src[:, k, i * P:(i + 1) * P], w[:, k, :],
                                  start=(k == 0), stop=(k == w.shape[1] - 1))
                    filled(name, last)

                w = unit("v", DC, GMW)
                for i in range(TT):
                    token_major(f"{t}v{i}", i, w, H, GMW)
                used_by(f"{t}v1")
                w = unit("cq", DC, QR)
                for m in range(QR // P):
                    product(f"{t}cq{m}", w[:, :, m * P:(m + 1) * P], H)
                used_by(f"{t}cq2")
                w = unit("ckv", DC, KVR + ROPE)
                for m in range(KVR // P):
                    product(f"{t}ckv{m}", w[:, :, m * P:(m + 1) * P], H)
                for i in range(TT):
                    token_major(f"{t}kr{i}", i, w[:, :, KVR:KVR + ROPE], H, ROPE)
                used_by(f"{t}kr1")
                w = unit("z", DC, SI)
                for m in range(4):
                    product(f"{t}z{m}", w[:, :, m * P:(m + 1) * P], H)
                used_by(f"{t}z3")
                w = unit("xbc0", DC, 512)
                for m in range(4):
                    product(f"{t}xbc{m}", w[:, :, m * P:(m + 1) * P], H)
                used_by(f"{t}xbc3")
                w = unit("xbc1", DC, 512 + SH)
                for m in range(4):
                    product(f"{t}xbc{4 + m}", w[:, :, m * P:(m + 1) * P], H)
                b = fill(f"{t}dt")
                for i in range(TT):
                    for k in range(DC):
                        last = mm(b[:, i * SH:(i + 1) * SH], H[:, k, i * P:(i + 1) * P], w[:, k, 512:512 + SH],
                                  start=(k == 0), stop=(k == DC - 1))
                filled(f"{t}dt", last)
                used_by(f"{t}dt")
                for m in range(3):
                    pe.wait_ge(*drained(f"{t}cq{m}"))
                column_sums(f"{t}cqms", SQ, 3)
                for m in range(2):
                    pe.wait_ge(*drained(f"{t}ckv{m}"))
                column_sums(f"{t}ckvms", SQ[:, 3:5, :], 2)
                b = fill(f"{t}wT")
                for g in range(GMG):
                    last = nc.tensor.transpose(b[:, g * P:(g + 1) * P], gmw[:, l, g, :], ident[:, :])
                filled(f"{t}wT", last)
                pe.wait_ge(*drained(f"{t}wT"))
                pe.wait_ge(vn_ready.sem, vn_ready.upto("pe"))
                for g in range(GMG):
                    b = fill(f"{t}sp{g}")
                    for i in range(TT):
                        last = mm(b[:, i * P:(i + 1) * P], vn[:, i, g * P:(g + 1) * P], wT[:, g, :],
                                  start=True, stop=True)
                    filled(f"{t}sp{g}", last)
                w = unit("uq", QR // P, MH * QK)
                pe.wait_ge(lat_ready.sem, lat_ready.upto("pe"))
                for i in range(TT):
                    for g in range(2):
                        token_major(f"{t}q{i}.{g}", i, w[:, :, g * 4 * QK:(g + 1) * 4 * QK], cq, 4 * QK)
                used_by(f"{t}q1.1")
                w = unit("ukv", KVR // P, MH * (NOPE + MV))
                pe.wait_ge(lat_ready.sem, lat_ready.upto("pe"))
                for i in range(TT):
                    for g in range(2):
                        token_major(f"{t}kv{i}.{g}", i, w[:, :, g * 512:(g + 1) * 512], ckv, 512)
                used_by(f"{t}kv1.1")
                for name, src in (("qT", Qt), ("kT", Kt)):
                    pe.wait_ge(qkrot_ready.sem, qkrot_ready.upto("pe"))
                    for c in range(MH // 2):
                        b = fill(f"{t}{name}{c}")
                        for h in range(2):
                            for i in range(TT):
                                o = h * T + i * P
                                last = nc.tensor.transpose(b[0:QK, o:o + P], src[:, i, 2 * c + h, :], ident[:, :])
                        filled(f"{t}{name}{c}", last)
                for name in ("qT", "kT"):
                    for c in range(MH // 2):
                        pe.wait_ge(*drained(f"{t}{name}{c}"))
                attention(f"{t}mla", MH, lambda h: QT[0:QK, h, :], lambda h: KT[0:QK, h, :],
                          lambda h, i: Vt[:, i, h * MV:(h + 1) * MV])
                pe.wait_ge(conv_ready.sem, conv_ready.upto("pe", 8))
                for i in range(TT):
                    b = fill(f"{t}xs{i}")
                    for c in range(4):
                        last = nc.tensor.transpose(b[:, c * P:(c + 1) * P], xv[:, c, i * P:(i + 1) * P], ident[:, :])
                    filled(f"{t}xs{i}", last)
                for g in range(SG):
                    b = fill(f"{t}cb{g}")
                    mm(b[:, 0:T], xv[:, 4 + g, 0:P], xv[:, 6 + g, :], start=True, stop=True)
                    filled(f"{t}cb{g}", mm(b[:, T + P:2 * T], xv[:, 4 + g, P:T], xv[:, 6 + g, P:T],
                                           start=True, stop=True))

                def decays(h):
                    pe.wait_ge(decay_in.sem, decay_in.upto("pe"))
                    b = fill(f"{t}ss{h}")
                    M = Mh[h % 2]
                    mm(b[:, 0:T], M[:, 0, 0:P], upper[:, 0, :], start=True, stop=False)
                    mm(b[:, P:T], M[:, 1, 0:P], upper[:, 1, P:T], start=False, stop=True)
                    filled(f"{t}ss{h}", mm(b[:, T + P:2 * T], M[:, 1, P:T], upper[:, 1, P:T], start=True, stop=True))

                def outputs(h):
                    pe.wait_ge(sp_mm_ready.sem, sp_mm_ready.upto("pe"))
                    b = fill(f"{t}y{h}") if h % 2 == 0 else bank_of(f"{t}y{h - 1}")
                    r = SHD * (h % 2)
                    mm(b[r:r + SHD, 0:T], xdt[:, 0, h * SHD:(h + 1) * SHD], Ph[h % 2][:, 0, :], start=True, stop=False)
                    last = mm(b[r:r + SHD, P:T], xdt[:, 1, h * SHD:(h + 1) * SHD], Ph[h % 2][:, 1, P:T],
                              start=False, stop=True)
                    if h % 2:
                        filled(f"{t}y{h - 1}", last)

                for it in range(SH + 1):
                    if it < SH:
                        decays(it)
                    if it >= 1:
                        outputs(it - 1)
                for g in range(SG):
                    column_sums(f"{t}yms{g}", SQ[:, 2 * g:2 * g + 2, :], 2, ysilu_ready)
                for n in range(NB):
                    for hf in range(2):
                        w = unit(f"g{n}.{hf}", DC, 512)
                        for m in range(4):
                            product(f"{t}g{n}.{4 * hf + m}", w[:, :, m * P:(m + 1) * P], H)
                        used_by(f"{t}g{n}.{4 * hf + 3}")
                    w = unit(f"br{n}", 4, D)
                    if n == 0:
                        pe.wait_ge(sp_ready.sem, sp_ready.upto("pe"))
                    elif n == 1:
                        for h in range(0, MH, 2):
                            pe.wait_ge(*drained(f"{t}mla.o{h}"))
                    else:
                        pe.wait_ge(yc_ready.sem, yc_ready.upto("pe"))
                    for m in range(DC):
                        product(f"{t}br{n}.{m}", w[:, :, m * P:(m + 1) * P], (yA, yB, yC)[n])
                    used_by(f"{t}br{n}.{DC - 1}")
                for hf in range(2):
                    w = unit(f"o{hf}", DC, 512)
                    for m in range(4):
                        product(f"{t}o{4 * hf + m}", w[:, :, m * P:(m + 1) * P], H2, merged_ready if hf + m == 0 else None)
                    used_by(f"{t}o{4 * hf + 3}")
                rms_norm(f"f2{l}")
                swiglu(f"f2{l}", FF // HB, h_ready)

            pe.wait_ge(x_ready.sem, DC * (1 + 2 * DEPTH))
            for i in range(TT):
                for hf in range(2):
                    b = fill(f"out{i}.{hf}")
                    for m in range(4):
                        last = nc.tensor.transpose(b[:, m * P:(m + 1) * P], X[:, 4 * hf + m, i * P:(i + 1) * P], ident[:, :])
                    filled(f"out{i}.{hf}", last)

        def swiglu_turns(steps):
            return divmod(steps, BODY)

        @block.scalar
        def _(act):
            f = nc.scalar.activation

            def evac(name, dst, src=None, func=ACT.Copy, last=True, **kw):
                act.wait_ge(*full(name))
                ins = f(dst, bank_of(name)[0:dst.shape[0], 0:T] if src is None else src, func, **kw)
                if last:
                    ins.then_inc(drain_sem(name), 1)

            for t, rows in enumerate(TABLE):
                r = 0
                for name, n in rows:
                    act.dma_start(prow[r:r + n, t, :], A[SOURCES[name]].flatten().rearrange("(r p) -> r p", p=P)) \
                        .then_inc(rows_landed, 16)
                    r += n
            act.dma_start(xin, A["x"][0].rearrange("(i p) d -> p i d", p=P)).then_inc(x_landed, 16)
            with nc.allow_non_contiguous_dma(reason="small tables"):
                act.dma_start(wif[:, :, :], A["a_w_if"][0].rearrange("(k p) n -> p k n", p=P)).then_inc(small_landed, 16)
                act.dma_start(bif[:, :], A["a_b_if"].rearrange("o (g h) -> h (o g)", h=NH)).then_inc(small_landed, 16)
                act.dma_start(wr[:, :, :], A["moe_w_router"].rearrange("(k p) n -> p k n", p=P)).then_inc(small_landed, 16)
                act.dma_start(brb[:, :], A["moe_b_router"].partition_broadcast(P)).then_inc(small_landed, 16)
                act.dma_start(posi[:, :], A["positions_2"].rearrange("o (i p) -> p (o i)", p=P)).then_inc(small_landed, 16)
                act.dma_start(dtb[:, :, :], A["ssd_dt_bias_2"].partition_broadcast(P)).then_inc(small_landed, 16)
                act.dma_start(alb[:, :, :], A["ssd_a_log_2"].partition_broadcast(P)).then_inc(small_landed, 16)
                act.dma_start(gmw[:, :, :, :], A["gm_w_s_2"].rearrange("l g t s -> t l g s")).then_inc(small_landed, 16)
                act.dma_start(bsb[:, :, :, :], A["gm_b_s_2"].partition_broadcast(P)).then_inc(small_landed, 16)
                act.dma_start(gainb[:, 0, :, :], A["mla_q_gain_2"].partition_broadcast(P)).then_inc(small_landed, 16)
                act.dma_start(gainb[:, 1, :, :], A["mla_k_gain_2"].partition_broadcast(P)).then_inc(small_landed, 16)
                for l in range(DEPTH):
                    for o in range(2):
                        act.dma_start(dsk[o * SHD:(o + 1) * SHD, l, :],
                                      A["ssd_d_2"][l].rearrange("(c o) -> o c", o=2)[o].partition_broadcast(SHD)) \
                            .then_inc(small_landed, 16)
            act.wait_ge(*drained("table0"))
            t, r = col["c"]
            f(cT[:, :, :], pcol[:, t, r:r + DC].unsqueeze(2).broadcast_to([P, DC, 32]), ACT.Silu).then_inc(c_ready, 1)
            act.wait_ge(consts_made, N_CONST)

            def ada(n):
                evac(f"ada{n}", adar[n % 2], bank_of(f"ada{n}")[:, :])

            for n in range(ADA_FIRST):
                ada(n)

            def conv_silu(m, dst, bias, n):
                act.wait_ge(conv_summed.sem, conv_summed.upto("act"))
                f(dst[:, m, :], dst[:, m, :], ACT.Silu, bias=vec(bias, n)).then_inc(conv_ready.sem, 1)

            act.wait_ge(pad_cleared.sem, pad_cleared.upto("act"))
            for n in range(2 * DIC):
                if n < DIC:
                    evac(f"w_in{n}", xm[:, n, PAD:PAD + T])
                else:
                    evac(f"w_in{n}", sz[:, n - DIC, :], func=ACT.Silu)
                if 2 <= n < DIC + 2:
                    conv_silu(n - 2, xc, "conv_b", n - 2)
                if n % 4 == 3:
                    for a in ADA_IN[n // 4]:
                        ada(a)
            act.wait_ge(small_landed, 16 * N_SMALL)
            f(alb[:, :, :], alb[:, :, :], ACT.Exp).then_inc(consts_derived, 1)
            for g in range(2):
                evac(f"gate{g}", lrow[g], func=ACT.Identity, bias=bif[:, g:g + 1])

            def softplus_tail(e, u):
                act.wait_ge(abs_ready.sem, abs_ready.upto("act"))
                f(e, e, ACT.Exp, scale=-1.0).then_inc(aexp_ready.sem, 1)
                act.wait_ge(plus_one.sem, plus_one.upto("act"))
                f(u, u, ACT.Ln).then_inc(ln_ready.sem, 1)

            ucol = sm[:, 0:TT * NH]
            for h in range(NH):
                for m in range(DHC):
                    evac(f"q{h}.{m}", qm[:, m, :])
                    if h == 0 and m == 1:
                        softplus_tail(lrow[7], lrow[2])
                for m in range(DHC):
                    evac(f"k{h}.{m}", km[:, m, :])
                if h == 0:
                    act.wait_ge(rows_made.sem, rows_made.upto("act"))
                    f(lrow[6], lrow[6], ACT.Exp, scale=-1.0).then_inc(emt_ready.sem, 1)
                    evac("ucol", ucol, bank_of("ucol")[:, 0:TT * NH])
                else:
                    mlstm_norm = h - 1
                    act.wait_ge(hc_ready.sem, hc_ready.upto("act"))
                    f(hsq, hm, ACT.Square).then_inc(hsq_ready.sem, 1)
                    evac(f"gvar{mlstm_norm}", nrm[:, 0, :], func=ACT.Sqrt, scale=1.0 / DH, bias=eps_ln[:, :])
                act.wait_ge(dlog_ready.sem, dlog_ready.upto("act"))
                if h == 0:
                    act.wait_ge(*drained("ucol"))
                W = Wm[h % 2]
                f(W[:, 0, :], W[:, 0, :], ACT.Exp, bias=ucol[:, h:h + 1])
                f(W[:, 1, P:T], W[:, 1, P:T], ACT.Exp, bias=ucol[:, NH + h:NH + h + 1]).then_inc(wexp_ready.sem, 1)
            act.wait_ge(hc_ready.sem, hc_ready.upto("act"))
            f(hsq, hm, ACT.Square).then_inc(hsq_ready.sem, 1)
            evac(f"gvar{NH - 1}", nrm[:, 0, :], func=ACT.Sqrt, scale=1.0 / DH, bias=eps_ln[:, :])

            def squares(fresh, moved=None):
                for k in range(DC):
                    if moved is None:
                        act.wait_ge(fresh.sem, fresh.upto("act"))
                    else:
                        act.wait_ge(*drained(f"{moved}{k}"))
                    f(SQ[:, k, :], X[:, k, :], ACT.Square).then_inc(squared.sem, 1)

            def layer_norm(tag):
                squares(centered)
                evac(f"{tag}.var", nrm[:, 0, :], func=ACT.Sqrt, scale=1.0 / D, bias=eps_ln[:, :])

            def rms_norm(tag, moved=None):
                squares(x_ready, moved)
                evac(f"{tag}.ms", nrm[:, 0, :], func=ACT.Sqrt, scale=1.0 / D, bias=eps_rms[:, :])

            def routing(l):
                act.wait_ge(*drained(f"logits{l}"))
                f(sm[:, 32:64], sm[:, 32:64], ACT.Exp).then_inc(router_exp.sem, 1)
                for n in range(2 * TT):
                    i, half = divmod(n, 2)
                    evac(f"ht{l}.{n}", Htok[:, i, half * 512:(half + 1) * 512], bank_of(f"ht{l}.{n}")[:, :])

            def moe(l):
                for n in range(2):
                    evac(f"xg{l}.{n}", XG[:, 4 * n:4 * n + 4, :].rearrange("p k s -> p (k s)"), bank_of(f"xg{l}.{n}")[:, :])

                def move(i, odd, step, dst, func=ACT.Copy):
                    act.wait_ge(*pair_full(l, i, odd, step))
                    f(dst, pair_bank(l, i, odd, step)[:, :], func).then_inc(pair_drain_sem(l, i, odd, step), 1)

                def pair(i, odd):
                    move(i, odd, "g", sge, ACT.Silu)
                    if not (isinstance(i, int) and 2 * i + odd == PAIRS - 1):
                        for n in range(2):
                            move(i, odd, f"xg{n}", XG[:, 4 * n:4 * n + 4, :].rearrange("p k s -> p (k s)"))
                    move(i, odd, "hT", hidT.rearrange("p k s -> p (k s)"))
                    move(i, odd, "d1", ye[:, 512:D])

                all_pairs(act, pair)
                act.wait_ge(flagged, l + 1)
                flag = act.value_load(over_flag[0:1, l:l + 1], min_val=0, max_val=1)
                with act.If(flag > 0):
                    act.wait_ge(over_filled[l], 1)
                    f(gT, bank[0][0:NE, 0:T], ACT.Copy).then_inc(over_moved[l], 1)
                    for e in range(0, NE, 2):
                        act.wait_ge(over_filled[l], e // 2 + 2)
                        f(gbc[:, e:e + 2, :].rearrange("p a t -> p (a t)"), bank[0][:, :], ACT.Copy) \
                            .then_inc(over_moved[l], 1)
                    with act.Fori(0, NE) as e:
                        for n in range(FE // HB):
                            act.wait_ge(over_up[l], e * (FE // HB) + n + 1)
                            f(sg_o, bank[1][:, 0:T], ACT.Silu).then_inc(over_silu[l], 1)

            def swiglu(tag, steps):
                k0 = uses[f"{tag}.0"]

                def step(i, j):
                    k = k0 + j
                    act.wait_ge(bank_full[k % 4], i + k // 4 + 1)
                    f(sg[j % 2], bank[k % 4][:, 0:T], ACT.Silu).then_inc(silu_ready.sem, 1)

                turns, rest = swiglu_turns(steps)
                with act.Fori(0, turns) as i:
                    for j in range(BODY):
                        step(i, j)
                for j in range(rest):
                    step(turns, j)

            def attention(tag, heads, o):
                def exps(h):
                    act.wait_ge(score_ready.sem, score_ready.upto("act"))
                    S, E, c = Ss[h % 2], Es[h % 2], 64 + 8 * (h % 2)
                    f(E[:, 0, 0:P], S[:, 0, 0:P], ACT.Exp, bias=sm[:, c:c + 1], accum_out=sm[:, c + 2:c + 3])
                    f(E[:, 1, :], S[:, 1, :], ACT.Exp, bias=sm[:, c + 1:c + 2], accum_out=sm[:, c + 3:c + 4]) \
                        .then_inc(prob_exp.sem, 1)

                def turned(h):
                    name = f"{tag}.p{h}"
                    evac(name, PTs[h % 2][:, 0, :], last=False)
                    evac(name, PTs[h % 2][:, 1, P:T], bank_of(name)[:, T + P:2 * T])

                for it in range(heads + 2):
                    if it < heads:
                        exps(it)
                    if 1 <= it <= heads:
                        turned(it - 1)
                    if it >= 2 and it % 2:
                        evac(f"{tag}.o{it - 3}", o[:, (it - 3) // 2, :])

            layer_norm("ln00")
            routing(0)
            moe(0)
            act.wait_ge(rope_in.sem, rope_in.upto("act"))
            for a in range(2):
                last = f(trig[:, a, :, :], trig[:, a, :, :], ACT.Sin)
            last.then_inc(rope_ready.sem, 1)
            layer_norm("ln01")

            for m in range(DC):
                evac(f"bk{m}", ka[:, m, :])
            for n in range(2):
                for i in range(TT):
                    evac(f"bv{n}.{i}", va[:, i, n * 512:(n + 1) * 512], bank_of(f"bv{n}.{i}")[:, :])
            for m in range(DC):
                evac(f"bq{m}", qa[:, m, :], scale=AD ** -0.5)
            attention("moba", AH, oa)
            layer_norm("ln10")
            routing(1)
            moe(1)
            layer_norm("ln11")

            for l in range(DEPTH):
                rms_norm(f"f1{l}")
                swiglu(f"f1{l}", FF // HB)
                rms_norm(f"mx{l}")
                t = f"m{l}."
                for m in range(4):
                    evac(f"{t}u{m}", us[:, m, :], func=ACT.Gelu)
                for i in range(TT):
                    evac(f"{t}v{i}", vn[:, i, :], bank_of(f"{t}v{i}")[:, :], ACT.Gelu)
                for i in range(TT):
                    act.wait_ge(*drained(f"{t}v{i}"))
                    last = f(qksq[:, i * GMW:(i + 1) * GMW], vn[:, i, :], ACT.Square, accum_out=sm[:, 80 + i:81 + i])
                last.then_inc(vsq_ready.sem, 1)
                for m in range(3):
                    evac(f"{t}cq{m}", cq[:, m, :], last=False)
                    evac(f"{t}cq{m}", SQ[:, m, :], func=ACT.Square)
                for m in range(2):
                    evac(f"{t}ckv{m}", ckv[:, m, :], last=False)
                    evac(f"{t}ckv{m}", SQ[:, 3 + m, :], func=ACT.Square)
                for i in range(TT):
                    evac(f"{t}kr{i}", krs[:, i, :], bank_of(f"{t}kr{i}")[:, 0:ROPE])
                for m in range(4):
                    evac(f"{t}z{m}", zs[:, m, :], func=ACT.Silu)
                act.wait_ge(pad_cleared.sem, pad_cleared.upto("act"))
                for m in range(8):
                    evac(f"{t}xbc{m}", xb[:, m, PAD:PAD + T])
                act.wait_ge(vsq_ready.sem, vsq_ready.upto("act"))
                f(sm[:, 80:82], sm[:, 80:82], ACT.Sqrt, scale=1.0 / GMW, bias=eps_rms[:, :]).then_inc(vsq_ready.sem, 1)
                vsq_ready.upto("act")
                evac(f"{t}cqms", nrm[:, 0, :], func=ACT.Sqrt, scale=1.0 / QR, bias=eps_rms[:, :])
                evac(f"{t}ckvms", nrm[:, 1, :], func=ACT.Sqrt, scale=1.0 / KVR, bias=eps_rms[:, :])
                for i in range(TT):
                    for g in range(2):
                        evac(f"{t}q{i}.{g}", Qt[:, i, 4 * g:4 * g + 4, :].rearrange("p h d -> p (h d)"),
                             bank_of(f"{t}q{i}.{g}")[:, 0:4 * QK])
                qkb = [sm[:, 96:112], sm[:, 112:128]]
                for n, src in enumerate((Qt, Kt)):
                    if n:
                        for i in range(TT):
                            for g in range(2):
                                b = bank_of(f"{t}kv{i}.{g}")[:, :].rearrange("p (h d) -> p h d", h=4)
                                evac(f"{t}kv{i}.{g}", Kt[:, i, 4 * g:4 * g + 4, 0:NOPE], b[:, :, 0:NOPE], last=False)
                                evac(f"{t}kv{i}.{g}", Vt[:, i, 4 * g * MV:(4 * g + 4) * MV].rearrange("p (h d) -> p h d", h=4),
                                     b[:, :, NOPE:NOPE + MV])
                    if n:
                        act.wait_ge(qksq_ready.sem, qksq_ready.upto("act"))
                    for i in range(TT):
                        for g in range(2):
                            act.wait_ge(*drained(f"{t}{'kv' if n else 'q'}{i}.{g}"))
                    f(qksq, src.rearrange("p i h d -> p (i h d)"), ACT.Square).then_inc(qkss_ready.sem, 1)
                    act.wait_ge(qkstd_ready.sem, qkstd_ready.upto("act"))
                    f(qkb[n], qkb[n], ACT.Sqrt, scale=1.0 / QK, bias=eps_rms[:, :]).then_inc(qkstd_ready.sem, 1)
                    qkstd_ready.upto("act")
                for name, dst in (("qT", QT), ("kT", KT)):
                    for c in range(MH // 2):
                        evac(f"{t}{name}{c}", dst[0:QK, 2 * c:2 * c + 2, :],
                             bank_of(f"{t}{name}{c}")[0:QK, :].rearrange("p (h t) -> p h t", h=2))
                attention(f"{t}mla", MH, yB)
                for m in range(8):
                    conv_silu(m, xv, "conv_b2", 8 * l + m)
                softplus_tail(sm[:, 144:160], sm[:, 160:176])
                for h in range(SH):
                    act.wait_ge(*full(f"{t}ss{h}"))
                    b = bank_of(f"{t}ss{h}")
                    evac(f"{t}ss{h}", Eh[h % 2][:, 0, :], last=False, func=ACT.Exp)
                    evac(f"{t}ss{h}", Eh[h % 2][:, 1, P:T], b[:, T + P:2 * T], func=ACT.Exp)
                for c in range(4):
                    act.wait_ge(yz_ready.sem, yz_ready.upto("act"))
                    f(SQ[:, c, :], yC[:, c, :], ACT.Square).then_inc(ysilu_ready.sem, 1)
                for g in range(SG):
                    evac(f"{t}yms{g}", nrm[:, g, :], func=ACT.Sqrt, scale=1.0 / (SI // SG), bias=eps_rms[:, :])
                for n in range(NB):
                    for m in range(DC):
                        evac(f"{t}g{n}.{m}", sig[n % 2][:, m, :], func=ACT.Sigmoid)
                rms_norm(f"f2{l}", f"{t}o")
                swiglu(f"f2{l}", FF // HB)
            for i in range(TT):
                for hf in range(2):
                    evac(f"out{i}.{hf}", xo[:, i, hf * 512:(hf + 1) * 512], bank_of(f"out{i}.{hf}")[:, :])

        @block.vector
        def _(dve):
            v = nc.vector
            tt, ts, stt = v.tensor_tensor, v.tensor_scalar, v.scalar_tensor_tensor
            steps = [0]

            def link(ins):
                ins.then_inc(dve_steps, 1)
                steps[0] += 1
                dve.wait_ge(dve_steps, steps[0])

            def moved(name, ins):
                ins.then_inc(drain_sem(name), 1)

            def rows(ap, n):
                return ap.unsqueeze(1).broadcast_to([ap.shape[0], n, ap.shape[1]])

            def each(ap, n):
                return ap.unsqueeze(2).broadcast_to([ap.shape[0], ap.shape[1], n])

            for t, entries in enumerate(TABLE):
                n = sum(m for _, m in entries)
                dve.wait_ge(*full(f"table{t}"))
                moved(f"table{t}", v.tensor_copy(pcol[:, t, 0:n], bank_of(f"table{t}")[:, 0:n]))
            for kk in range(DC // 2):
                dve.wait_ge(*full(f"x{kk}"))
                moved(f"x{kk}", v.tensor_copy(X[:, 2 * kk:2 * kk + 2, :],
                                              bank_of(f"x{kk}")[:, :].rearrange("p (a t) -> p a t", a=2)))
            for t in range(len(TABLE)):
                dve.wait_ge(*drained(f"table{t}"))
            for kk in range(DC // 2):
                dve.wait_ge(*drained(f"x{kk}"))
            v.memset(xm[:, :, 0:PAD], 0.0).then_inc(pad_cleared.sem, 1)
            dve.wait_ge(pad_cleared.sem, pad_cleared.upto("dve"))

            def ada(n):
                dve.wait_ge(*full(f"adaT{n}"))
                src = bank_of(f"adaT{n}")[:, :].rearrange("p (m g c) -> p m g c", m=4, g=4)[:, :, :, 0]
                moved(f"adaT{n}", v.tensor_reduce(mods[:, 4 * n:4 * n + 4], src, AX.X, ALU.add))

            def finish_ada(n0, n1):
                for n in range(n0, n1):
                    dve.wait_ge(*drained(f"adaT{n}"))
                t, r = col["b_ada"]
                c0, c1 = 4 * n0, 4 * n1
                link(tt(mods[:, c0:c1], mods[:, c0:c1], pcol[:, t, r + c0:r + c1], ALU.add))
                for g in range(c0, c1, 3 * DC):
                    first, end = (g + DC, g + 3 * DC) if g < DEPTH * 6 * DC else (g + DC, g + 2 * DC)
                    last = ts(mods[:, first:end], mods[:, first:end], 1.0, None, ALU.add)
                link(last)

            def modulate(dst, layer, s, ready):
                for k in range(DC):
                    ts(dst[:, k, :], X[:, k, :], mod(layer, s, 1, k), mod(layer, s, 0, k), ALU.mult, ALU.add) \
                        .then_inc(ready.sem, 1)

            for n in range(ADA_FIRST):
                ada(n)
            finish_ada(0, ADA_FIRST)
            def scale_residual():
                dve.wait_ge(h_ready.sem, h_ready.upto("dve", DC))
                link(ts(X[:, :, :], X[:, :, :], ALPHA, None, ALU.mult))

            modulate(H, 0, 0, h_ready)
            scale_residual()

            def conv(src, dst, m, taps):
                link(ts(dst[:, m, :], src[:, m, 0:T], taps[0], None, ALU.mult))
                for j in range(1, CONV):
                    ins = stt(dst[:, m, :], src[:, m, j:j + T], taps[j], dst[:, m, :], ALU.mult, ALU.add)
                    if j < CONV - 1:
                        link(ins)
                ins.then_inc(conv_summed.sem, 1)

            for n in range(2 * DIC // 4):
                for m in range(4 * n, 4 * n + 4):
                    if m < DIC:
                        dve.wait_ge(*drained(f"w_in{m}"))
                        conv(xm, xc, m, [vec("conv_w", j * DIC + m) for j in range(CONV)])
                for a in ADA_IN[n]:
                    if a > ADA_FIRST:
                        ada(a - 1)
            ada(ADA_UNITS - 1)
            finish_ada(ADA_FIRST, ADA_UNITS)

            def log1p_exp(e, u, d, z):
                dve.wait_ge(aexp_ready.sem, aexp_ready.upto("dve"))
                link(ts(u, e, 1.0, None, ALU.add))
                link(ts(d, u, 1.0, None, ALU.subtract))
                ts(z, d, 0.0, None, ALU.is_equal).then_inc(plus_one.sem, 1)
                dve.wait_ge(plus_one.sem, plus_one.upto("dve"))
                link(tt(d, d, z, ALU.add))
                dve.wait_ge(ln_ready.sem, ln_ready.upto("dve"))
                link(tt(u, u, z, ALU.add))
                link(v.reciprocal(d, d))
                link(tt(u, u, d, ALU.mult))
                link(tt(u, u, e, ALU.mult))

            for g in range(2):
                dve.wait_ge(*drained(f"gate{g}"))
            v.memset(lrow[6], 1.0)
            stt(lrow[7], lrow[1], -1.0, lrow[1], ALU.mult, ALU.max).then_inc(abs_ready.sem, 1)
            dve.wait_ge(abs_ready.sem, abs_ready.upto("dve"))
            log1p_exp(lrow[7], lrow[2], lrow[3], lrow[4])
            link(stt(lrow[1], lrow[1], 0.0, lrow[2], ALU.min, ALU.subtract))
            link(v.tensor_tensor_scan(lrow[4], lrow[6], lrow[1], 0.0, ALU.mult, ALU.add))
            tt(lrow[3], lrow[0], lrow[4], ALU.subtract).then_inc(stab_ready.sem, 1)
            dve.wait_ge(stab_ready.sem, stab_ready.upto("dve"))
            link(v.tensor_tensor_scan(lrow[2], lrow[3], lrow[3], 0.0, ALU.max, ALU.max))
            ts(lrow[5], lrow[2], -1.0, None, ALU.mult)
            tt(lrow[6], lrow[4], lrow[2], ALU.add).then_inc(rows_made.sem, 1)

            def mlstm_num(h):
                dve.wait_ge(*full(f"den{h}"))
                moved(f"den{h}", v.tensor_copy(nrm[:, 1, :], bank_of(f"den{h}")[:, 0:T]))
                dve.wait_ge(*drained(f"den{h}"))
                dve.wait_ge(*drained(f"mbc{h}"))
                link(tt(den_s, den_s, nrm[:, 1, :], ALU.max))
                link(stt(den_s, nrm[:, 1, :], -1.0, den_s, ALU.mult, ALU.max))
                link(v.reciprocal(den_s, den_s))
                for a in range(2):
                    name = f"num{h}.{a}"
                    dve.wait_ge(*full(name))
                    moved(name, tt(hm[:, 2 * a:2 * a + 2, :], bank_of(name)[:, :].rearrange("p (a t) -> p a t", a=2),
                                   rows(den_s, 2), ALU.mult))
                dve.wait_ge(*full(f"gmean{h}"))
                moved(f"gmean{h}", ts(nrm[:, 1, :], bank_of(f"gmean{h}")[:, 0:T], -1.0 / DH, None, ALU.mult))
                dve.wait_ge(*drained(f"gmean{h}"))
                tt(hm, hm, rows(nrm[:, 1, :], DHC), ALU.add).then_inc(hc_ready.sem, 1)

            def mlstm_out(h):
                dve.wait_ge(*drained(f"gvar{h}"))
                link(v.reciprocal(nrm[:, 0, :], nrm[:, 0, :]))
                link(tt(hm, hm, rows(nrm[:, 0, :], DHC), ALU.mult))
                c = DHC * h
                for m in range(DHC):
                    last = ts(xc[:, c + m, :], xc[:, c + m, :], vec("skip", c + m), None, ALU.mult)
                link(last)
                for m in range(DHC):
                    last = stt(xc[:, c + m, :], hm[:, m, :], vec("gn_g", c + m), xc[:, c + m, :], ALU.mult, ALU.add)
                link(last)
                tt(xc[:, c:c + DHC, :], xc[:, c:c + DHC, :], sz[:, c:c + DHC, :], ALU.mult).then_inc(head_ready.sem, 1)

            for h in range(NH):
                if h > 0:
                    mlstm_num(h - 1)
                for i in range(TT):
                    dve.wait_ge(*full(f"v{h}.{i}"))
                    moved(f"v{h}.{i}", v.tensor_copy(vm(h, i), bank_of(f"v{h}.{i}")[:, :]))
                if h > 0:
                    mlstm_out(h - 1)
                dve.wait_ge(*full(f"mbc{h}"))
                b, W = bank_of(f"mbc{h}"), Wm[h % 2]
                tt(W[:, 0, :], b[:, 0:T], neg_st[:, 0, :], ALU.add)
                tt(W[:, 1, P:T], b[:, P:T], neg_st[:, 1, P:T], ALU.add).then_inc(dlog_ready.sem, 1)
                moved(f"mbc{h}", v.tensor_copy(den_s, b[:, T:2 * T]))
                dve.wait_ge(*full(f"mS{h}"))
                dve.wait_ge(wexp_ready.sem, wexp_ready.upto("dve"))
                b = bank_of(f"mS{h}")
                stt(Pm[h % 2][:, 0, :], b[:, 0:T], DH ** -0.5, W[:, 0, :], ALU.mult, ALU.mult)
                moved(f"mS{h}", stt(Pm[h % 2][:, 1, P:T], b[:, T + P:2 * T], DH ** -0.5, W[:, 1, P:T], ALU.mult, ALU.mult))
            mlstm_num(NH - 1)
            mlstm_out(NH - 1)

            def layer_norm(tag, layer, s, y=None):
                for m in range(DC):
                    if y:
                        dve.wait_ge(*full(f"{y}{m}"))
                        moved(f"{y}{m}", stt(X[:, m, :], bank_of(f"{y}{m}")[:, 0:T], mod(layer, s, 2, m), X[:, m, :],
                                             ALU.mult, ALU.add))
                    else:
                        stt(X[:, m, :], ysum(m), mod(layer, s, 2, m), X[:, m, :], ALU.mult, ALU.add) \
                            .then_inc(sum_ready.sem, 1)
                dve.wait_ge(*full(f"{tag}.mean"))
                moved(f"{tag}.mean", ts(nrm[:, 1, :], bank_of(f"{tag}.mean")[:, 0:T], -1.0 / D, None, ALU.mult))
                dve.wait_ge(*drained(f"{tag}.mean"))
                for m in range(DC):
                    tt(X[:, m, :], X[:, m, :], nrm[:, 1, :], ALU.add).then_inc(centered.sem, 1)
                dve.wait_ge(*drained(f"{tag}.var"))
                link(v.reciprocal(nrm[:, 0, :], nrm[:, 0, :]))
                for m in range(DC):
                    last = tt(X[:, m, :], X[:, m, :], nrm[:, 0, :], ALU.mult)
                link(last)
                final = layer == DEPTH // 2 and s == 1
                for m in range(DC):
                    i = (layer * 2 + s) * DC + m
                    last = ts(X[:, m, :], X[:, m, :], vec("ln_g", i), vec("ln_b", i), ALU.mult, ALU.add)
                    if final:
                        last.then_inc(x_ready.sem, 1)
                if not final:
                    link(last)

            def rms_norm(tag, gain, l):
                dve.wait_ge(*drained(f"{tag}.ms"))
                link(v.reciprocal(nrm[:, 0, :], nrm[:, 0, :]))
                for k in range(DC):
                    stt(H[:, k, :], X[:, k, :], vec(gain, l * DC + k), nrm[:, 0, :], ALU.mult, ALU.mult) \
                        .then_inc(h_ready.sem, 1)
                dve.wait_ge(h_ready.sem, h_ready.upto("dve", DC))

            def routing(l):
                def s3(a, n, m):
                    return sm[:, a:a + n * m].rearrange("p (n m) -> p n m", n=n)

                gate, e, selp = s3(0, TT, NE), s3(32, TT, NE), s3(200, TT, NE)
                top, tot = sm[:, 192:194], sm[:, 194:196]
                dve.wait_ge(*full(f"logits{l}"))
                b = bank_of(f"logits{l}")[:, 0:TT * NE].rearrange("p (n m) -> p n m", n=TT)
                link(v.tensor_reduce(top, b, AX.X, ALU.max))
                moved(f"logits{l}", tt(e, b, each(top, NE), ALU.subtract))
                dve.wait_ge(router_exp.sem, router_exp.upto("dve"))
                link(v.tensor_reduce(tot, e, AX.X, ALU.add))
                link(v.reciprocal(tot, tot))
                link(tt(e, e, each(tot, NE), ALU.mult))
                link(tt(selp, e, rows(brb[:, :], TT), ALU.add))
                s4 = s3(200, TT * NGRP, EPG)
                pairs = s3(232, 6, TT * NGRP)
                for n, (i, j) in enumerate([(i, j) for i in range(EPG) for j in range(i + 1, EPG)]):
                    last = tt(pairs[:, n, :], s4[:, :, i], s4[:, :, j], ALU.add)
                link(last)
                gs, gm, g1 = sm[:, 280:288], sm[:, 288:290], sm[:, 290:298]
                link(v.tensor_reduce(gs, pairs.rearrange("p s n -> p n s"), AX.X, ALU.max))

                def first_best(score, best, onehot, rank, n):
                    link(v.tensor_reduce(best, score, AX.X, ALU.max))
                    link(tt(onehot, score, each(best, n), ALU.is_equal))
                    link(tt(onehot, onehot, rows(rank, TT), ALU.mult))
                    link(v.tensor_reduce(best, onehot, AX.X, ALU.max))
                    link(tt(onehot, onehot, each(best, n), ALU.is_equal))

                first_best(s3(280, TT, NGRP), gm, s3(290, TT, NGRP), rank4[:, :], NGRP)
                link(ts(g1, g1, -NEG, NEG, ALU.mult, ALU.add))
                link(tt(s4, s4, each(g1, EPG), ALU.add))
                o1, o2 = s3(304, TT, NE), s3(336, TT, NE)
                first_best(selp, top, o1, rank16[:, :], NE)
                link(stt(sm[:, 200:232], sm[:, 304:336], 2 * NEG, sm[:, 200:232], ALU.mult, ALU.add))
                first_best(selp, top, o2, rank16[:, :], NE)
                tt(sm[:, 304:336], sm[:, 304:336], sm[:, 336:368], ALU.add).then_inc(route_ready.sem, 1)
                dve.wait_ge(route_ready.sem, route_ready.upto("dve"))
                link(tt(gate, e, o1, ALU.mult))
                link(v.tensor_reduce(tot, gate, AX.X, ALU.add))
                link(v.reciprocal(tot, tot))
                link(tt(gate, gate, each(tot, NE), ALU.mult))
                dve.wait_ge(*full(f"rank{l}"))
                b = bank_of(f"rank{l}")[:, 0:TT * NE].rearrange("p (n m) -> p n m", n=TT)
                moved(f"rank{l}", tt(number_t, mask_t, b, ALU.mult))
                dve.wait_ge(*drained(f"rank{l}"))

            def by_slots(table, i, odd):
                cols = bass.ds(i * 4 + 2 * odd, 2) if not isinstance(i, int) else slice(4 * i + 2 * odd, 4 * i + 2 * odd + 2)
                return table[:, :, cols].unsqueeze(3).broadcast_to([P, TT, 2, SLOTS])

            def fill_slots(l, i, odd):
                numbers = slot_no[:, :].unsqueeze(1).unsqueeze(1).broadcast_to([P, TT, 2, SLOTS])
                tt(slot, numbers, by_slots(number_t, i, odd), ALU.is_equal).then_inc(slots_ready, 1)

            def weigh_slots(l, i, odd):
                dve.wait_ge(slots_ready, i * 2 + (PAIRS * l + odd + 1))
                tt(slot_g, slot, by_slots(gate_t, i, odd), ALU.mult).then_inc(gated_ready, 1)

            def moe(l):
                fill_slots(l, 0, 0)
                weigh_slots(l, 0, 0)
                over = sm[:, 232:264].rearrange("p (n m) -> p n m", n=TT)
                link(ts(over, number_t, SLOTS + 0.5, None, ALU.is_gt))
                tt(gate_o, gate_t, over, ALU.mult)
                v.tensor_reduce(sm[:, 264:265], sm[:, 232:264], AX.X, ALU.add).then_inc(over_summed, 1)
                dve.wait_ge(*full(f"over{l}"))
                moved(f"over{l}", v.tensor_copy(sm[0:1, 265:266], bank_of(f"over{l}")[0:1, 0:1]))
                dve.wait_ge(*drained(f"over{l}"))
                ts(over_flag[0:1, l:l + 1], sm[0:1, 265:266], 0.5, None, ALU.is_gt).then_inc(flagged, 1)

                def pair(i, odd):
                    last_pair = isinstance(i, int) and 2 * i + odd == PAIRS - 1
                    if not last_pair:
                        first = isinstance(i, int) and 2 * i + odd == 0
                        dve.wait_ge(*(full(f"xg{l}.1") if first else pair_full(l, i, odd - 1, "xg1")))
                        dve.wait_ge(gated_ready, i * 2 + (PAIRS * l + odd + 1))
                        fill_slots(l, i, odd + 1)
                    dve.wait_ge(*pair_drained(l, i, odd, "g"))
                    dve.wait_ge(*pair_full(l, i, odd, "u"))
                    tt(hide, sge, pair_bank(l, i, odd, "u")[:, :], ALU.mult).then_inc(pair_drain_sem(l, i, odd, "u"), 1)
                    dve.wait_ge(*pair_full(l, i, odd, "S"))
                    v.tensor_copy(S_e, pair_bank(l, i, odd, "S")[:, 0:T]).then_inc(pair_drain_sem(l, i, odd, "S"), 1)
                    if not last_pair:
                        weigh_slots(l, i, odd + 1)
                    dve.wait_ge(*pair_full(l, i, odd, "d0"))
                    v.tensor_copy(ye[:, 0:512], pair_bank(l, i, odd, "d0")[:, :]) \
                        .then_inc(pair_drain_sem(l, i, odd, "d0"), 1)

                all_pairs(dve, pair)
                dve.wait_ge(scattered, PAIRS * (l + 1))
                dve.wait_ge(flagged, l + 1)
                flag = dve.value_load(over_flag[0:1, l:l + 1], min_val=0, max_val=1)
                with dve.If(flag > 0):
                    blocks = FE // HB
                    dve.wait_ge(over_moved[l], NE // 2 + 1)
                    with dve.Fori(0, NE) as e:
                        for n in range(blocks):
                            dve.wait_ge(over_silu[l], e * blocks + n + 1)
                            tt(sgw_o, sg_o, gbc[:, bass.ds(e, 1), :].rearrange("p a t -> p (a t)"), ALU.mult) \
                                .then_inc(over_scaled[l], 1)
                            dve.wait_ge(over_scaled[l], e * blocks + n + 1)
                            tt(hid_o, sgw_o, bank[1][:, T:2 * T], ALU.mult).then_inc(over_hid[l], 1)
                    dve.wait_ge(over_down[l], NE * blocks)

            def swiglu(tag, n_steps):
                k0 = uses[f"{tag}.0"]
                s0 = silu_ready.upto("dve", 0)

                def step(i, j):
                    k = k0 + j
                    dve.wait_ge(silu_ready.sem, i * BODY + s0 + j + 1)
                    tt(hid[j % 2], sg[j % 2], bank[k % 4][:, T:2 * T], ALU.mult).then_inc(bank_drained[k % 4], 1)

                turns, rest = swiglu_turns(n_steps)
                with dve.Fori(0, turns) as i:
                    for j in range(BODY):
                        step(i, j)
                for j in range(rest):
                    step(turns, j)
                silu_ready.upto("dve", n_steps)

            def attention(tag, heads, score):
                for i in range(2):
                    last = v.memset(Ss[i][:, 0, P:T], NEG)
                link(last)

                def scores(h):
                    name, c, S = f"{tag}.s{h}", 64 + 8 * (h % 2), Ss[h % 2]
                    dve.wait_ge(*full(name))
                    b = bank_of(name)
                    score(h, S[:, 0, 0:P], b[:, 0:P], 0, P)
                    moved(name, score(h, S[:, 1, :], b[:, T:2 * T], 1, T))
                    dve.wait_ge(*drained(name))
                    link(v.tensor_reduce(sm[:, c + 4:c + 6], S, AX.X, ALU.max))
                    ts(sm[:, c:c + 2], sm[:, c + 4:c + 6], -1.0, None, ALU.mult).then_inc(score_ready.sem, 1)

                def normed(h):
                    c, E = 64 + 8 * (h % 2), Es[h % 2]
                    dve.wait_ge(prob_exp.sem, prob_exp.upto("dve"))
                    link(v.reciprocal(sm[:, c + 6:c + 8], sm[:, c + 2:c + 4]))
                    ts(E[:, 0, 0:P], E[:, 0, 0:P], sm[:, c + 6:c + 7], None, ALU.mult)
                    ts(E[:, 1, :], E[:, 1, :], sm[:, c + 7:c + 8], None, ALU.mult).then_inc(prob_ready.sem, 1)

                for it in range(heads + 1):
                    if it < heads:
                        scores(it)
                    if it >= 1:
                        normed(it - 1)

            def rotary_angles():
                two_pi = 2 * np.pi
                c1 = 6.28125
                c2 = float(np.float32(np.round((two_pi - c1) * 2.0 ** 22) / 2.0 ** 22))
                c3 = float(np.float32(two_pi - c1 - c2))
                magic = 1.5 * 2.0 ** 23
                dve.wait_ge(small_landed, 16 * N_SMALL)
                link(v.tensor_copy(posf[:, :], posi[:, :]))
                ang, sn, cs = sm[:, 500:532], trig[:, 1, :, :].rearrange("p i d -> p (i d)"), trig[:, 0, :, :].rearrange("p i d -> p (i d)")
                for i in range(TT):
                    last = ts(ang[:, i * HR:(i + 1) * HR], invf[:, :], posf[:, i:i + 1], None, ALU.mult)
                link(last)
                link(ts(cs, ang, 1.0 / two_pi, magic, ALU.mult, ALU.add))
                link(ts(cs, cs, magic, None, ALU.subtract))
                for c in (c1, c2, c3):
                    link(stt(ang, cs, -c, ang, ALU.mult, ALU.add))
                lim = 3.1415925
                link(ts(sn, ang, lim, -lim, ALU.min, ALU.max))
                link(ts(cs, ang, np.pi / 2, None, ALU.add))
                link(ts(ang, cs, np.pi, None, ALU.is_gt))
                link(stt(cs, ang, -two_pi, cs, ALU.mult, ALU.add))
                ts(cs, cs, lim, -lim, ALU.min, ALU.max).then_inc(rope_in.sem, 1)

            layer_norm("ln00", 0, 0, "y0.")
            modulate(H, 0, 1, h_ready)
            scale_residual()
            routing(0)
            rotary_angles()
            moe(0)
            layer_norm("ln01", 0, 1)
            for k in range(DC):
                ts(H2[:, k, :], X[:, k, :], kvmod(1, k), kvmod(0, k), ALU.mult, ALU.add).then_inc(h2_ready.sem, 1)
            modulate(H, 1, 0, h_ready)
            scale_residual()
            attention("moba", AH, lambda h, dst, b, i, n: stt(dst, alibi[:, i, 0:n], 2.0 ** (-8.0 * (h + 1) / AH), b,
                                                              ALU.mult, ALU.add))
            layer_norm("ln10", 1, 0, "y1.")
            modulate(H, 1, 1, h_ready)
            scale_residual()
            routing(1)
            moe(1)
            layer_norm("ln11", 1, 1)

            done = [0]

            def half_step(tag):
                swiglu(tag, FF // HB)
                done[0] += FF // HB
                dve.wait_ge(down_done.sem, done[0])
                for m in range(DC):
                    stt(X[:, m, :], ysum(m), 0.5, X[:, m, :], ALU.mult, ALU.add).then_inc(x_ready.sem, 1)

            for l in range(DEPTH):
                rms_norm(f"f1{l}", "ffn1", l)
                half_step(f"f1{l}")
                rms_norm(f"mx{l}", "mix", l)
                t = f"m{l}."
                v.memset(xb[:, :, 0:PAD], 0.0).then_inc(pad_cleared.sem, 1)
                dve.wait_ge(pad_cleared.sem, pad_cleared.upto("dve"))
                dve.wait_ge(vsq_ready.sem, vsq_ready.upto("dve", 2))
                link(v.reciprocal(sm[:, 80:82], sm[:, 80:82]))
                for i in range(TT):
                    last = ts(vn[:, i, :], vn[:, i, :], sm[:, 80 + i:81 + i], None, ALU.mult)
                last.then_inc(vn_ready.sem, 1)
                x8, a8, u8 = sm[:, 128:144], sm[:, 144:160], sm[:, 160:176]
                dtv, da = sm[:, 416:432].rearrange("p (i h) -> p i h", i=TT), sm[:, 432:448].rearrange("p (i h) -> p i h", i=TT)
                dve.wait_ge(*full(f"{t}dt"))
                moved(f"{t}dt", tt(x8.rearrange("p (i h) -> p i h", i=TT),
                                   bank_of(f"{t}dt")[:, 0:TT * SH].rearrange("p (i h) -> p i h", i=TT),
                                   rows(dtb[:, l, :], TT), ALU.add))
                dve.wait_ge(*drained(f"{t}dt"))
                stt(a8, x8, -1.0, x8, ALU.mult, ALU.max).then_inc(abs_ready.sem, 1)
                for name, src, n, gain, r in (("cq", cq, 3, "qn", 0), ("ckv", ckv, 2, "kvn", 1)):
                    dve.wait_ge(*drained(f"{t}{name}ms"))
                    link(v.reciprocal(nrm[:, r, :], nrm[:, r, :]))
                    for m in range(n):
                        last = stt(src[:, m, :], src[:, m, :], vec(gain, l * n + m), nrm[:, r, :], ALU.mult, ALU.mult)
                    last.then_inc(lat_ready.sem, 1)
                dve.wait_ge(*full(f"{t}wT"))
                moved(f"{t}wT", tt(wT, bank_of(f"{t}wT")[:, :].rearrange("p (g t) -> p g t", g=GMG),
                                   rows(upper[:, 0, 0:P], GMG), ALU.mult))
                for g in range(GMG):
                    dve.wait_ge(*full(f"{t}sp{g}"))
                    moved(f"{t}sp{g}", stt(yA[:, g, :].rearrange("p (i t) -> p i t", i=TT),
                                           bank_of(f"{t}sp{g}")[:, 0:T].rearrange("p (i t) -> p i t", i=TT),
                                           vec("gmv", l * GMG + g), rows(bsb[:, l, g, :], TT), ALU.mult, ALU.add))
                    dve.wait_ge(*drained(f"{t}sp{g}"))
                    last = tt(yA[:, g, :], yA[:, g, :], us[:, g, :], ALU.mult)
                last.then_inc(sp_ready.sem, 1)
                for i in range(TT):
                    dve.wait_ge(*drained(f"{t}kr{i}"))
                    last = v.tensor_copy(Kt[:, i, :, NOPE:QK], rows(krs[:, i, :], MH))
                last.then_inc(qksq_ready.sem, 1)
                for m in range(8):
                    dve.wait_ge(*drained(f"{t}xbc{m}"))
                    conv(xb, xv, m, [vec("conv_w2", (l * CONV + j) * 8 + m) for j in range(CONV)])
                if l == 0:
                    dve.wait_ge(rope_ready.sem, rope_ready.upto("dve"))
                for n, src in enumerate((Qt, Kt)):
                    ss = sm[:, 96 + 16 * n:112 + 16 * n]
                    dve.wait_ge(qkss_ready.sem, qkss_ready.upto("dve"))
                    v.tensor_reduce(ss, qksq.rearrange("p (h d) -> p h d", d=QK), AX.X, ALU.add).then_inc(qkstd_ready.sem, 1)
                    dve.wait_ge(qkstd_ready.sem, qkstd_ready.upto("dve", 2))
                    link(v.reciprocal(ss, ss))
                    flat = src.rearrange("p i h d -> p (i h) d")
                    link(tt(flat, flat, each(ss, QK), ALU.mult))
                    link(tt(flat, flat, rows(gainb[:, n, l, :], TT * MH), ALU.mult))
                    for i in range(TT):
                        x1, x2 = src[:, i, :, NOPE:NOPE + HR], src[:, i, :, NOPE + HR:QK]
                        cs, sn = rows(trig[:, 0, i, :], MH), rows(trig[:, 1, i, :], MH)
                        for a, (x, c) in enumerate(((x1, cs), (x2, sn), (x2, cs), (x1, sn))):
                            last = tt(rt[a][:, i, :, :], x, c, ALU.mult)
                    link(last)
                    x1, x2 = src[:, :, :, NOPE:NOPE + HR], src[:, :, :, NOPE + HR:QK]
                    tt(x1, rt[0], rt[1], ALU.subtract)
                    tt(x2, rt[2], rt[3], ALU.add).then_inc(qkrot_ready.sem, 1)
                dve.wait_ge(qkrot_ready.sem, qkrot_ready.upto("dve", 2))
                attention(f"{t}mla", MH, lambda h, dst, b, i, n: stt(dst, b, QK ** -0.5, neg_qk[:, i, 0:n], ALU.mult, ALU.add))
                dve.wait_ge(abs_ready.sem, abs_ready.upto("dve"))
                log1p_exp(a8, u8, sm[:, 176:192], sm[:, 400:416])
                link(stt(sm[:, 416:432], x8, 0.0, u8, ALU.max, ALU.add))
                dve.wait_ge(consts_derived, 1)
                link(stt(da, dtv, -1.0, rows(alb[:, l, :], TT), ALU.mult, ALU.mult))
                for i in range(TT):
                    dve.wait_ge(*full(f"{t}xs{i}"))
                    moved(f"{t}xs{i}", tt(xdt[:, i, :].rearrange("p (h d) -> p h d", h=SH),
                                          bank_of(f"{t}xs{i}")[:, :].rearrange("p (h d) -> p h d", h=SH),
                                          each(dtv[:, i, :], SHD), ALU.mult))
                for g in range(SG):
                    dve.wait_ge(*full(f"{t}cb{g}"))
                    b = bank_of(f"{t}cb{g}")
                    tt(CB[g][:, 0, :], b[:, 0:T], upper[:, 0, :], ALU.mult)
                    moved(f"{t}cb{g}", tt(CB[g][:, 1, P:T], b[:, T + P:2 * T], upper[:, 1, P:T], ALU.mult))
                for g in range(SG):
                    dve.wait_ge(*drained(f"{t}cb{g}"))

                def decay_terms(h):
                    ts(Mh[h % 2][:, 0, 0:P], strict[:, 0, 0:P], da[:, 0, h:h + 1], None, ALU.mult)
                    ts(Mh[h % 2][:, 1, :], strict[:, 1, :], da[:, 1, h:h + 1], None, ALU.mult).then_inc(decay_in.sem, 1)

                def output(c):
                    name = f"{t}y{2 * c}"
                    dve.wait_ge(*full(name))
                    moved(name, stt(yC[:, c, :], xv[:, c, :], dsk[:, l, c:c + 1], bank_of(name)[:, 0:T], ALU.mult, ALU.add))
                    dve.wait_ge(*drained(name))
                    tt(yC[:, c, :], yC[:, c, :], zs[:, c, :], ALU.mult).then_inc(yz_ready.sem, 1)

                decay_terms(0)
                decay_terms(1)
                for h in range(SH):
                    dve.wait_ge(*drained(f"{t}ss{h}"))
                    g = h // (SH // SG)
                    tt(Ph[h % 2][:, 0, :], Eh[h % 2][:, 0, :], CB[g][:, 0, :], ALU.mult)
                    tt(Ph[h % 2][:, 1, P:T], Eh[h % 2][:, 1, P:T], CB[g][:, 1, P:T], ALU.mult).then_inc(sp_mm_ready.sem, 1)
                    if h + 2 < SH:
                        decay_terms(h + 2)
                    if h % 2:
                        output(h // 2)
                for g in range(SG):
                    dve.wait_ge(*drained(f"{t}yms{g}"))
                    link(v.reciprocal(nrm[:, g, :], nrm[:, g, :]))
                    for c in range(2 * g, 2 * g + 2):
                        last = stt(yC[:, c, :], yC[:, c, :], vec("ssdn", l * 4 + c), nrm[:, g, :], ALU.mult, ALU.mult)
                last.then_inc(yc_ready.sem, 1)
                for n in range(NB):
                    for m in range(DC):
                        name, gate = f"{t}br{n}.{m}", sig[n % 2][:, m, :]
                        dve.wait_ge(*full(name))
                        dve.wait_ge(*drained(f"{t}g{n}.{m}"))
                        moved(name, tt(H2[:, m, :] if n == 0 else gate, bank_of(name)[:, 0:T], gate, ALU.mult))
                        dve.wait_ge(*drained(name))
                        if n:
                            last = tt(H2[:, m, :], H2[:, m, :], gate, ALU.add)
                            if n == NB - 1:
                                last.then_inc(merged_ready.sem, 1)
                            else:
                                link(last)
                for m in range(DC):
                    dve.wait_ge(*full(f"{t}o{m}"))
                    moved(f"{t}o{m}", tt(X[:, m, :], bank_of(f"{t}o{m}")[:, 0:T], X[:, m, :], ALU.add))
                rms_norm(f"f2{l}", "ffn2", l)
                half_step(f"f2{l}")

        @block.sync
        def _(sp):
            nxt = [0]

            def slot_free(u):
                if u >= WSLOTS:
                    sp.wait_ge(*freed[u - WSLOTS])

            def load(tag, *pieces):
                u = nxt[0]
                nxt[0] += 1
                assert tags[u] == tag, (tags[u], tag)
                slot_free(u)
                o = 0
                for n, (src, k) in enumerate(pieces):
                    cols = src.shape[1]
                    inc = 48 - 16 * (len(pieces) - 1) if n == 0 else 16
                    sp.dma_start(wring[:, u % WSLOTS, o:o + k * cols].rearrange("p (k n) -> p k n", k=k),
                                 src.rearrange("(k p) n -> p k n", p=P)).then_inc(w_landed[u % WSLOTS], inc)
                    o += k * cols

            def ada(n):
                load(f"ada{n}", (A["w_ada"][:, n * 512:(n + 1) * 512], DC))

            def swiglu(tag, steps, sources):
                u0, d0 = nxt[0], freed[nxt[0]][1] - 1
                assert tags[u0] == f"{tag}.0"

                def step(i, j):
                    u = (u0 + j) % WSLOTS
                    wg, wu, wd = sources(i, j)
                    o = DC * HB
                    for n, src in enumerate((wg, wu)):
                        sp.dma_start(wring[:, u, n * o:(n + 1) * o].rearrange("p (k n) -> p k n", k=DC), src) \
                            .then_inc(w_landed[u], 16)
                    sp.dma_start(wring[:, u, 2 * o:2 * o + D], wd).then_inc(w_landed[u], 16)

                turns, rest = swiglu_turns(steps)
                for j in range(BODY):
                    slot_free(u0 + j)
                    step(0, j)
                with sp.Fori(1, turns) as i:
                    for j in range(BODY):
                        sp.wait_ge(down_done.sem, i * BODY + (d0 + j + 1 - BODY))
                        step(i, j)
                for j in range(rest):
                    sp.wait_ge(down_done.sem, turns * BODY + d0 + j + 1 - BODY)
                    step(turns, j)
                nxt[0] += steps

            def moe(l):
                u0 = nxt[0]
                assert tags[u0] == f"moe{l}.0.0"
                mats = [A[f"moe_w_{name}"][l].rearrange("e (k p) n -> p e k n", p=P) for name in ("gate", "up", "down")]

                def pair(i, odd):
                    for n in range(PAIR_UNITS):
                        u = u0 + PAIR_UNITS * odd + n
                        if isinstance(i, int):
                            slot_free(u + 2 * PAIR_UNITS * i)
                        else:
                            back, of = divmod(n - WSLOTS, PAIR_UNITS)
                            sp.wait_ge(*pair_full(l, i, odd + back, ("g", "u", "d1")[of // 2]))
                        src, e = mats[n // 2], 2 * odd + n % 2
                        one = slice(4 * i + e, 4 * i + e + 1) if isinstance(i, int) else bass.ds(i * 4 + e, 1)
                        k = src.shape[2]
                        sp.dma_start(wring[:, u % WSLOTS, 0:D * FE // P].rearrange("p (k n) -> p k n", k=k),
                                     src[:, one, :, :].rearrange("p e k n -> p (e k) n")) \
                            .then_inc(w_landed[u % WSLOTS], 48)

                all_pairs(sp, pair)
                nxt[0] += PAIRS * PAIR_UNITS
                sp.wait_ge(flagged, l + 1)
                flag = sp.value_load(over_flag[0:1, l:l + 1], min_val=0, max_val=1)
                with sp.If(flag > 0):
                    sp.wait_ge(*freed[nxt[0] - 1])

                    def expert(one):
                        for n, src in enumerate(mats):
                            sp.dma_start(wring[:, n, 0:D * FE // P].rearrange("p (k n) -> p k n", k=src.shape[2]),
                                         src[:, one, :, :].rearrange("p e k n -> p (e k) n")) \
                                .then_inc(over_landed[l], 16)

                    expert(slice(0, 1))
                    with sp.Fori(1, NE) as e:
                        sp.wait_ge(over_down[l], e * (FE // HB))
                        expert(bass.ds(e, 1))
                    sp.wait_ge(over_down[l], NE * (FE // HB))

            def ffn(w_in, w_out):
                def sources(i, j):
                    def cols(o):
                        return bass.ds(i * (BODY * HB) + (o + j * HB), HB)
                    return (w_in[:, cols(0)].rearrange("(k p) n -> p k n", p=P),
                            w_in[:, cols(FF)].rearrange("(k p) n -> p k n", p=P), w_out[cols(0), :])
                return sources

            for n in range(ADA_FIRST):
                ada(n)
            for n in range(2 * DI // 512):
                load(f"a_w_in{n}", (A["a_w_in"][0][:, n * 512:(n + 1) * 512], DC))
                for a in ADA_IN[n]:
                    ada(a)
            for h in range(NH):
                load(f"qk{h}", (A["a_wq"][0, h], DHC), (A["a_wk"][0, h], DHC))
                load(f"v{h}", (A["a_wv"][0, h], DHC))
            for n in range(D // 256):
                load(f"a_w_out{n}", (A["a_w_out"][0][:, n * 256:(n + 1) * 256], DIC))
            moe(0)
            for name, src, o in (("k", A["b_w_kv"], 0), ("v", A["b_w_kv"], D), ("q", A["b_wq"][0], 0)):
                for n in range(2):
                    load(f"b{name}{n}", (src[:, o + n * 512:o + (n + 1) * 512], DC))
            for n in range(2):
                load(f"bo{n}", (A["b_wo"][0][:, n * 512:(n + 1) * 512], DC))
            moe(1)
            for l in range(DEPTH):
                swiglu(f"f1{l}", FF // HB, ffn(A["ffn1_w_in_2"][l], A["ffn1_w_out_2"][l]))
                t, w = f"m{l}.", A["w_in_2"][l]
                for tag, o, n in (("u", O_U, GMW), ("v", O_V, GMW), ("cq", O_CQ, QR), ("ckv", O_CKV, KVR + ROPE),
                                  ("z", O_Z, SI), ("xbc0", O_XBC, 512), ("xbc1", O_XBC + 512, 512 + SH)):
                    load(t + tag, (w[:, o:o + n], DC))
                load(t + "uq", (A["mla_w_uq_2"][l], QR // P))
                load(t + "ukv", (A["mla_w_ukv_2"][l], KVR // P))
                for n in range(NB):
                    for hf in range(2):
                        o = O_G + n * D + hf * 512
                        load(f"{t}g{n}.{hf}", (w[:, o:o + 512], DC))
                    load(f"{t}br{n}", (A["w_branch_2"][l, n], 4))
                for hf in range(2):
                    load(f"{t}o{hf}", (A["w_out_2"][l][:, hf * 512:(hf + 1) * 512], DC))
                swiglu(f"f2{l}", FF // HB, ffn(A["ffn2_w_in_2"][l], A["ffn2_w_out_2"][l]))
            assert nxt[0] == len(tags)
            for i in range(TT):
                for hf in range(2):
                    sp.wait_ge(*drained(f"out{i}.{hf}"))
            sp.dma_start(out[0].rearrange("(i p) d -> p i d", p=P), xo).then_inc(out_landed, 16)
            sp.wait_ge(out_landed, 16)

        @block.gpsimd
        def _(pool):
            g = nc.gpsimd
            n_steps = [0]

            def link(ins):
                ins.then_inc(pool_steps, 1)
                n_steps[0] += 1
                pool.wait_ge(pool_steps, n_steps[0])

            g.memset(ident[:, :], 0.0)
            g.memset(ones[:, :], 1.0)
            g.memset(upper[:, :, :], 1.0)
            g.memset(strict[:, :, :], 1.0)
            g.memset(neg_st[:, :, :], 0.0)
            g.memset(neg_qk[:, :, :], 0.0)
            g.memset(eps_ln[:, :], LN_EPS)
            g.memset(eps_rms[:, :], RMS_EPS)
            inv = 1.0 / (np.float32(10000.0) ** (np.arange(0, ROPE, 2, dtype=np.float32) / np.float32(ROPE)))
            for d in range(HR):
                g.memset(invf[:, d:d + 1], float(np.float32(inv[d])))
            for n in range(NGRP):
                g.memset(rank4[:, n:n + 1], float(NGRP - n))
            for n in range(NE):
                g.memset(rank16[:, n:n + 1], float(NE - n))
            link(g.iota(alibi[:, :, :], pattern=[[-P, TT], [1, T]], base=0, channel_multiplier=-1,
                        allow_small_or_imprecise_dtypes=True))
            r_less_c = dict(pattern=[[P, TT], [-1, T]], base=0, channel_multiplier=1)
            c_less_r = dict(pattern=[[-P, TT], [1, T]], base=0, channel_multiplier=-1)
            g.affine_select(out=ident[:, :], in_=ident[:, :], compare_op=ALU.not_equal, fill=1.0, base=0,
                            pattern=[[-1, P]], channel_multiplier=1)
            g.affine_select(out=upper[:, :, :], in_=upper[:, :, :], compare_op=ALU.is_ge, fill=0.0, **c_less_r)
            g.affine_select(out=strict[:, :, :], in_=strict[:, :, :], compare_op=ALU.is_gt, fill=0.0, **r_less_c)
            g.affine_select(out=neg_st[:, :, :], in_=neg_st[:, :, :], compare_op=ALU.is_ge, fill=NEG, **c_less_r)
            g.affine_select(out=neg_qk[:, :, :], in_=neg_qk[:, :, :], compare_op=ALU.is_ge, fill=NEG, **r_less_c)
            g.affine_select(out=alibi[:, :, :], in_=alibi[:, :, :], compare_op=ALU.is_ge, fill=NEG, **r_less_c)
            g.iota(slot_no[:, :], pattern=[[1, SLOTS]], base=1, channel_multiplier=0,
                   allow_small_or_imprecise_dtypes=True).then_inc(consts_made, 1)


_INS = ['x', 'c', 'w_ada', 'b_ada', 'ln_g', 'ln_b', 'a_w_in', 'a_conv_w', 'a_conv_b', 'a_wq', 'a_wk', 'a_wv', 'a_w_if',
        'a_b_if', 'a_gn_g', 'a_skip', 'a_w_out', 'b_w_kv', 'b_wq', 'b_wo', 'moe_w_router', 'moe_b_router',
        'moe_w_gate', 'moe_w_up', 'moe_w_down', 'positions_2', 'ffn1_norm_2', 'ffn1_w_in_2', 'ffn1_w_out_2',
        'mix_norm_2', 'w_in_2', 'gm_v_norm_2', 'gm_w_s_2', 'gm_b_s_2', 'mla_q_norm_2', 'mla_kv_norm_2', 'mla_w_uq_2',
        'mla_w_ukv_2', 'mla_q_gain_2', 'mla_k_gain_2', 'ssd_conv_w_2', 'ssd_conv_b_2', 'ssd_dt_bias_2', 'ssd_a_log_2',
        'ssd_d_2', 'ssd_norm_2', 'w_branch_2', 'w_out_2', 'ffn2_norm_2', 'ffn2_w_in_2', 'ffn2_w_out_2']


def kernel(**inputs):
    import numpy as _np
    import concourse.bacc as _bacc
    from concourse import mybir as _mybir
    from concourse.bass_utils import run_bass_kernel_spmd as _run

    nc = _bacc.Bacc("TRN2", target_bir_lowering=False, num_devices=1)
    arrays, aps = {}, {}
    for name in _INS:
        a = _np.ascontiguousarray(inputs[name])
        arrays[f"in_{name}"] = a
        aps[name] = nc.dram_tensor(f"in_{name}", a.shape, _mybir.dt.from_np(a.dtype), kind="ExternalInput").ap()
    out = nc.dram_tensor("out", (1, T, D), _mybir.dt.float32, kind="ExternalOutput").ap()
    build(nc, aps, out)
    r = _run(nc, [arrays], core_ids=[0])
    return r.results[0]["out"]
```

```python
from contextlib import ExitStack

import numpy as np

import concourse.bass as bass
from concourse import mybir

F32 = mybir.dt.float32
F32R = mybir.dt.float32r
I32 = mybir.dt.int32
ALU = mybir.AluOpType
ACT = mybir.ActivationFunctionType
AX = mybir.AxisListType

P = 128
T = 256
TT = T // P
D = 1024
DC = D // P
DEPTH = 2
ALPHA = float(np.float32((2.0 * DEPTH) ** 0.25))
LN_EPS = 1e-5
RMS_EPS = 1e-6
NEG = -1e30

NH = 4
DI = 2 * D
DIC = DI // P
DH = DI // NH
DHC = DH // P
CONV = 4
PAD = CONV - 1
AH = 16
AD = D // AH
NE = 16
NGRP = 4
EPG = NE // NGRP
FE = 512
FF = 2816
GMW = 512
GMG = 4
QR = 384
KVR = 256
MH = 8
NOPE = 64
ROPE = 32
HR = ROPE // 2
QK = NOPE + ROPE
MV = 64
SH = 8
SHD = 64
SI = SH * SHD
SG = 2
XBC = SI + 2 * SG * P
O_U, O_V, O_CQ, O_CKV, O_KR = 0, GMW, 2 * GMW, 2 * GMW + QR, 2 * GMW + QR + KVR
O_Z = O_KR + ROPE
O_XBC = O_Z + SI
O_DT = O_XBC + XBC
O_G = O_DT + SH
NB = 3

WSLOTS = 4
WCOLS = DC * (512 + SH)
ADA_FIRST = 4
ADA_UNITS = (DEPTH * 6 + 2) * D // 512
ADA_MID = 3 * D * 2 // 512
ADA_IN = [[n for n in range(ADA_FIRST, ADA_MID) if (n - ADA_FIRST) * 8 // (ADA_MID - ADA_FIRST) == i]
          for i in range(8)]
ADA_HEAD = [[]] + [[n for n in range(ADA_MID, ADA_UNITS) if (n - ADA_MID) * (NH - 1) // (ADA_UNITS - ADA_MID) == i]
                   for i in range(NH - 1)]
HB = 128
SLOTS = 64
PAIRS = NE // 2
PAIR_UNITS = 6
PAIR_LOOP = (1, PAIRS // 2 - 1)
PAIR_STEPS = ("g", "u", "xg0", "xg1", "hT", "S", "d0", "d1")
LAST_STEPS = ("g", "u", "hT", "S", "d0", "d1")
BODY = 4
STEPS = FF // HB
WBUFS = 3

TABLE = [
    [("c", 8), ("b_ada", 112), ("kvn", 4)],
    [("ln_g", 32), ("ln_b", 32), ("conv_w", 64)],
    [("conv_b", 16), ("gn_g", 16), ("skip", 16), ("ffn1", 16), ("mix", 16), ("ffn2", 16), ("gmv", 8), ("ssdn", 8),
     ("qn", 6)],
    [("conv_w2", 64), ("conv_b2", 16)],
]

SOURCES = {"b_ada": "b_ada", "c": "c", "kvn": "mla_kv_norm_2", "ln_g": "ln_g", "ln_b": "ln_b", "conv_w": "a_conv_w",
           "conv_b": "a_conv_b", "gn_g": "a_gn_g", "skip": "a_skip", "ffn1": "ffn1_norm_2", "mix": "mix_norm_2",
           "ffn2": "ffn2_norm_2", "gmv": "gm_v_norm_2", "ssdn": "ssd_norm_2", "qn": "mla_q_norm_2",
           "conv_w2": "ssd_conv_w_2", "conv_b2": "ssd_conv_b_2"}


class Signal:

    def __init__(self, sem):
        self.sem, self.seen = sem, {}

    def upto(self, who, n=1):
        self.seen[who] = self.seen.get(who, 0) + n
        return self.seen[who]


def build(nc, A, out):
    ctx = ExitStack()
    with ctx:
        def sb(name, shape, dt=F32):
            return ctx.enter_context(nc.sbuf_tensor(name, shape, dt))

        def sem(name):
            return ctx.enter_context(nc.semaphore(name))

        wring = sb("wring", [P, WSLOTS, WCOLS])
        X = sb("X", [P, DC, T])
        H = sb("H", [P, DC, T])
        with nc.sbuf_tensor("H2", [P, DC, T], F32) as H2:
            pass
        x_hi = sb("x_hi", [P, DC, T])
        with nc.sbuf_tensor("ada_parts", [P, DC * T], F32) as ada_parts:
            pass
        x_lo = sb("x_lo", [P, DC, T])
        with nc.sbuf_tensor("SQ", [P, DC, T], F32) as SQ:
            pass
        sq_lo = sb("sq_lo", [P, DC, T])
        pcol = sb("pcol", [P, 4, P])
        ident = sb("ident", [P, P])
        ones = sb("ones", [P, P])
        upper = sb("upper", [P, TT, T])
        neg_st = sb("neg_st", [P, TT, T])
        neg_qk = sb("neg_qk", [P, TT, T])
        alibi = sb("alibi", [P, TT, T])
        slot_no = sb("slot_no", [P, SLOTS])
        over_flag = sb("over_flag", [1, DEPTH], I32)
        mods = sb("mods", [P, 112])
        lnv = sb("lnv", [P, 6, DC])
        gmw = sb("gmw", [P, DEPTH, GMG, P])
        bsb = sb("bsb", [P, DEPTH, GMG, P])
        gainb = sb("gainb", [P, 2, DEPTH, QK])
        wr = sb("wr", [P, DC, NE])
        wif = sb("wif", [P, DIC, 2 * NH])
        bif = sb("bif", [NH, 2])
        brb = sb("brb", [P, NE])
        dtb = sb("dtb", [P, DEPTH, SH])
        alb = sb("alb", [P, DEPTH, SH])
        dsk = sb("dsk", [P, DEPTH, SI // P])
        posi = sb("posi", [P, TT], I32)
        posf = sb("posf", [P, TT])
        invf = sb("invf", [P, HR])
        trig = sb("trig", [P, 2, TT, HR])
        rank4 = sb("rank4", [P, NGRP])
        rank16 = sb("rank16", [P, NE])
        eps_ln = sb("eps_ln", [P, 1])
        eps_rms = sb("eps_rms", [P, 1])
        one_c = sb("one_c", [P, 1])
        nrm = sb("nrm", [P, 2, T])
        sm = sb("sm", [P, 540])

        with nc.sbuf_tensor("arena", [P, 18904], F32) as arena:
            pass
        with ExitStack() as overlay:
            def part(name, shape):
                return overlay.enter_context(nc.sbuf_tensor(name, shape, F32))

            part("before_y", [P, 5120])
            y_hi, y_lo = (part(name, [P, 4, T]) for name in ("y_hi", "y_lo"))
            part("before_w", [P, 8216 - 7168])
            wt_merge = [part(name, [P, WBUFS, DC * P]) for name in ("wm_hi", "wm_lo")]
        with ExitStack() as overlay:
            wt_mix = [part(name, [P, 2, DC * P]) for name in ("wx_hi", "wx_lo")]
        with ExitStack() as overlay:
            part("before_w_in", [P, 12336])
            wt_w_in = [part(name, [P, WBUFS, DC * P]) for name in ("wi_hi", "wi_lo")]
        w_hi = sb("w_hi", [P, 2, 3, DC * HB])
        w_lo = sb("w_lo", [P, 2, 3, DC * HB])
        h_hi = sb("h_hi", [P, DC, T])
        h_lo = sb("h_lo", [P, DC, T])
        hid_hi = sb("hid_hi", [P, 2, T])
        hid_lo = sb("hid_lo", [P, 2, T])
        hid = sb("hid", [P, T])
        sg = sb("sg", [P, 2, T])

        bank = [ctx.enter_context(nc.psum_tensor(f"bank{i}", [P, 512], F32)) for i in range(4)]
        yacc = [ctx.enter_context(nc.psum_tensor(f"yacc{i}", [P, 512], F32)) for i in range(4)]

        def ysum(m):
            return yacc[m // 2][:, (m % 2) * T:(m % 2 + 1) * T]

        def view(off, *shape, parts=P):
            n = int(np.prod(shape))
            v = arena[0:parts, off:off + n]
            if len(shape) == 2:
                return v.rearrange("p (a b) -> p a b", a=shape[0])
            if len(shape) == 3:
                return v.rearrange("p (a b c) -> p a b c", a=shape[0], b=shape[1])
            return v

        col = {}
        for t, rows in enumerate(TABLE):
            r = 0
            for name, n in rows:
                col[name] = (t, r)
                r += n

        def vec(name, i):
            t, r = col[name]
            return pcol[:, t, r + i:r + i + 1]

        def mod(layer, s, which, k):
            i = ((layer * 2 + s) * 3 + which) * DC + k
            return mods[:, i:i + 1]

        w_landed = [sem(f"w_landed{i}") for i in range(WSLOTS)]
        bank_full = [sem(f"bank_full{i}") for i in range(4)]
        bank_drained = [sem(f"bank_drained{i}") for i in range(4)]
        consts_made = sem("consts_made")
        rows_landed = [sem(f"rows_landed{t}") for t in range(len(TABLE))]
        small_landed = sem("small_landed")
        x_landed = sem("x_landed")
        out_landed = sem("out_landed")
        pool_steps = sem("pool_steps")
        act_steps = sem("act_steps")
        dve_steps = sem("dve_steps")
        consts_derived = sem("consts_derived")
        c_ready = sem("c_ready")
        h_ready = Signal(sem("h_ready"))
        h2_ready = Signal(sem("h2_ready"))
        x_ready = Signal(sem("x_ready"))
        sum_ready = Signal(sem("sum_ready"))
        centered = Signal(sem("centered"))
        squared = Signal(sem("squared"))
        conv_summed = Signal(sem("conv_summed"))
        conv_ready = Signal(sem("conv_ready"))
        pad_cleared = Signal(sem("pad_cleared"))
        exp_ready = Signal(sem("exp_ready"))
        plus_one = Signal(sem("plus_one"))
        ln_ready = Signal(sem("ln_ready"))
        rows_made = Signal(sem("rows_made"))
        stab_ready = Signal(sem("stab_ready"))
        emt_ready = Signal(sem("emt_ready"))
        dlog_ready = Signal(sem("dlog_ready"))
        wexp_ready = Signal(sem("wexp_ready"))
        head_ready = Signal(sem("head_ready"))
        hc_ready = Signal(sem("hc_ready"))
        hsq_ready = Signal(sem("hsq_ready"))
        router_exp = Signal(sem("router_exp"))
        route_ready = Signal(sem("route_ready"))
        silu_ready = Signal(sem("silu_ready"))
        h_mix_ready = Signal(sem("h_mix_ready"))
        h_ffn_ready = Signal(sem("h_ffn_ready"))
        h_hi_ready = Signal(sem("h_hi_ready"))
        h_lo_ready = Signal(sem("h_lo_ready"))
        w_hi_ready, w_lo_ready = ([sem(f"{name}_{part}_ready") for name in ("gate", "up", "down")]
                                  for part in ("hi", "lo"))
        hid_ready = sem("hid_ready")
        sum_done = sem("sum_done")
        part_scattered = sem("part_scattered")
        normed = Signal(sem("normed"))
        wt_hi_ready, wt_lo_ready = sem("wt_hi_ready"), sem("wt_lo_ready")
        x_hi_ready, x_lo_ready = Signal(sem("x_hi_ready")), Signal(sem("x_lo_ready"))
        y_hi_ready, y_lo_ready = Signal(sem("y_hi_ready")), Signal(sem("y_lo_ready"))
        slots_ready = sem("slots_ready")
        gated_ready = sem("gated_ready")
        over_summed = sem("over_summed")
        flagged = sem("flagged")
        scattered = sem("scattered")
        over_landed, over_filled, over_moved, over_up, over_silu, over_scaled, over_hid, over_down = (
            [sem(f"over_{what}{l}") for l in range(DEPTH)]
            for what in ("landed", "filled", "moved", "up", "silu", "scaled", "hid", "down"))
        down_done = Signal(sem("down_done"))
        score_ready = Signal(sem("score_ready"))
        prob_exp = Signal(sem("prob_exp"))
        prob_ready = Signal(sem("prob_ready"))
        rope_in = Signal(sem("rope_in"))
        rope_ready = Signal(sem("rope_ready"))
        vsq_ready = Signal(sem("vsq_ready"))
        vn_ready = Signal(sem("vn_ready"))
        sp_ready = Signal(sem("sp_ready"))
        qksq_ready = Signal(sem("qksq_ready"))
        qkss_ready = Signal(sem("qkss_ready"))
        qkstd_ready = Signal(sem("qkstd_ready"))
        qkrot_ready = Signal(sem("qkrot_ready"))
        lat_ready = Signal(sem("lat_ready"))
        abs_ready = Signal(sem("abs_ready"))
        aexp_ready = Signal(sem("aexp_ready"))
        decay_in = Signal(sem("decay_in"))
        decay_ready = Signal(sem("decay_ready"))
        sp_mm_ready = Signal(sem("sp_mm_ready"))
        yz_ready = Signal(sem("yz_ready"))
        yc_ready = Signal(sem("yc_ready"))
        merged_ready = Signal(sem("merged_ready"))
        ysilu_ready = Signal(sem("ysilu_ready"))

        N_CONST = 1
        N_SMALL = 15

        uses = {}
        freed = []
        tags = []

        def bank_of(name):
            return bank[uses[name] % 4]

        def full(name):
            k = uses[name]
            return bank_full[k % 4], k // 4 + 1

        def drained(name):
            k = uses[name]
            return bank_drained[k % 4], k // 4 + 1

        def drain_sem(name):
            return bank_drained[uses[name] % 4]

        def pair_use(l, i, odd, step):
            steps = LAST_STEPS if isinstance(i, int) and 2 * i + odd == PAIRS - 1 else PAIR_STEPS
            k = uses[f"moe{l}.g0"] + len(PAIR_STEPS) * odd + steps.index(step)
            return k % 4, i * (2 * len(PAIR_STEPS) // 4) + k // 4

        def pair_full(l, i, odd, step):
            b, n = pair_use(l, i, odd, step)
            return bank_full[b], n + 1

        def pair_drained(l, i, odd, step):
            b, n = pair_use(l, i, odd, step)
            return bank_drained[b], n + 1

        def pair_bank(l, i, odd, step):
            return bank[pair_use(l, i, odd, step)[0]]

        def pair_drain_sem(l, i, odd, step):
            return bank_drained[pair_use(l, i, odd, step)[0]]

        def all_pairs(eng, pair):
            for odd in range(2):
                pair(0, odd)
            with eng.Fori(*PAIR_LOOP) as turn:
                for odd in range(2):
                    pair(turn, odd)
            for odd in range(2):
                pair(PAIRS // 2 - 1, odd)

        split = {}

        def raw_tile(phase, q):
            _, tag, k, cols, m = split[phase][1][q]
            return wring[:, tags.index(tag) % WSLOTS, 0:k * cols].rearrange("p (k n) -> p k n", k=k)[:, :, m * P:(m + 1) * P]

        def part_tile(lo, phase, q):
            k = split[phase][1][q][2]
            w = (wt_w_in if phase == "w_in" else wt_mix if "mix" in phase else wt_merge)[lo]
            return w[:, q % w.shape[1], 0:k * P].rearrange("p (k n) -> p k n", k=k)

        split["w_in"] = 0, [(f"w_in{m}", f"a_w_in{m // 4}", DC, 512, m % 4) for m in range(2 * DIC)]
        first = 2 * DIC
        for l in range(DEPTH):
            tiles = [(f"m{l}.{tag}{m}", f"m{l}.{unit}", DC, cols, m % 4)
                     for tag, unit, cols, ms in (("cq", "cq", QR, range(3)), ("ckv", "ckv", KVR + ROPE, range(2)),
                                                 ("xbc", "xbc0", 512, range(4)), ("xbc", "xbc1", 512 + SH, range(4, 8)),
                                                 ("u", "u", GMW, range(4)), ("z", "z", SI, range(4))) for m in ms]
            split[f"mix{l}"] = first, tiles
            first += len(tiles)
            tiles = []
            for n in range(NB):
                tiles += [(f"m{l}.g{n}.{m}", f"m{l}.g{n}.{m // 4}", DC, 512, m % 4) for m in range(DC)]
                tiles += [(f"m{l}.br{n}.{m}", f"m{l}.br{n}", 4, D, m) for m in range(DC)]
            tiles += [(f"m{l}.o{m}", f"m{l}.o{m // 4}", DC, 512, m % 4) for m in range(DC)]
            split[f"merge{l}"] = first, tiles
            first += len(tiles)

        prow = view(0, 4, P)
        xin = view(512, TT, D)
        xm = view(0, DIC, PAD + T)
        xc = view(4144, DIC, T)
        sz = view(8240, DIC, T)
        qm = view(12336, DHC, T)
        km = view(13360, DHC, T)
        Pm = [view(14384 + 512 * i, TT, T) for i in range(2)]
        Wm = [view(15408 + 512 * i, TT, T) for i in range(2)]
        lrow = [view(16432 + T * i, T, parts=NH) for i in range(8)]
        den_s = view(18480, T)

        def vm(h, i):
            c = 4 * (h % 2) + 2 * i
            return SQ[:, c:c + 2, :].rearrange("p a t -> p (a t)")

        cT = ada_parts[:, 0:DC * 32].rearrange("p (k n) -> p k n", k=DC)
        adar = [ada_parts[:, 512 * (i + 1):512 * (i + 2)] for i in range(2)]
        hm = H2[:, 0:DHC, :]
        hsq = H2[:, DHC:2 * DHC, :]
        Htok = view(0, TT, D)
        XG = view(2048, DC, P)
        slot = view(3072, TT, 2, SLOTS)
        slot_g = view(3328, TT, 2, SLOTS)
        sge = view(3584, FE)
        hide = view(4096, FE)
        hidT = view(4608, FE // P, P)
        ye = view(5120, D)
        S_e = view(6144, T)
        gbc = view(8192, NE, T)
        gT = view(12288, T, parts=NE)
        sg_o, sgw_o, hid_o = (view(12544 + 256 * i, T) for i in range(3))
        gate_t, mask_t, number_t, gate_o = (
            sm[:, a:a + TT * NE].rearrange("p (n m) -> p n m", n=TT) for a in (0, 304, 336, 200))
        qa = view(0, DC, T)
        ka = view(2048, DC, T)
        va = view(4096, TT, D)
        oa = view(6144, DC, T)
        Es = [view(15320 + 512 * i, TT, T) for i in range(3)]
        Ss = [view(16856 + 512 * i, TT, T) for i in range(2)]
        PTs = [view(17880 + 512 * i, TT, T) for i in range(2)]
        yA, yB, yC = (view(1024 * i, 4, T) for i in range(3))
        zs = view(10264, 4, T)
        xb = view(4096, 8, PAD + T)
        xv = view(6168, 8, T)
        us = view(8216, 4, T)
        vn = view(9240, TT, GMW)
        cq = view(10264, 3, T)
        ckv = view(11032, 2, T)
        krs = view(11544, TT, ROPE)
        wT = view(11608, GMG, P)
        Vt = view(12120, TT, MH * MV)
        O2 = 12760 + 384
        Qt = view(O2, TT, MH, QK)
        Kt = view(O2 + 1536, TT, MH, QK)
        qksq = view(O2 + 3072, 1536)
        rt = [view(O2 + 4608 + T * i, TT, MH, HR) for i in range(4)]
        QT, KT = H, SQ
        xdt = view(O2, TT, SI)
        Mh = [view(O2 + 1024 + 512 * i, TT, T) for i in range(2)]
        Eh = [view(O2 + 2048 + 512 * i, TT, T) for i in range(2)]
        Ph = [view(O2 + 3072 + 512 * i, TT, T) for i in range(2)]
        CB = [view(O2 + 4096 + 512 * i, TT, T) for i in range(SG)]
        sig = [view(14400 + 2048 * i, DC, T) for i in range(2)]
        merged = view(3072, DC, T)
        xo = view(0, TT, D)

        block = ctx.enter_context(nc.Block())

        @block.tensor
        def _(pe):
            mm = nc.tensor.matmul

            def fill(name):
                k = len(uses)
                uses[name] = k
                if k >= 4:
                    pe.wait_ge(bank_drained[k % 4], k // 4)
                return bank[k % 4]

            def filled(name, ins):
                ins.then_inc(bank_full[uses[name] % 4], 1)

            def weights(tag, wait=True):
                u = len(tags)
                tags.append(tag)
                freed.append(None)
                if wait:
                    pe.wait_ge(w_landed[u % WSLOTS], 48 * (u // WSLOTS + 1))
                return wring[:, u % WSLOTS, :]

            def used_by(name):
                freed[-1] = full(name)

            def product(name, w, rhs, fresh=None, part=P):
                b = fill(name)
                n = w.shape[1]
                for k in range(n):
                    if fresh is not None:
                        pe.wait_ge(fresh.sem, fresh.upto("pe"))
                    last = mm(b[0:part, 0:T], w[:, k, :], rhs[:, k, :], start=(k == 0), stop=(k == n - 1))
                filled(name, last)

            def part_product(phase, q, hi, lo, fresh=False):
                first, tiles = split[phase]
                name, _, n, _, _ = tiles[q]
                b = fill(name)
                for i, (w, x) in enumerate(((0, hi), (1, hi), (0, lo))):
                    if i < 2:
                        pe.wait_ge((wt_hi_ready, wt_lo_ready)[i], first + q + 1)
                    w = part_tile(w, phase, q)
                    for k in range(n):
                        if fresh and i != 1:
                            ready = x_lo_ready if i else x_hi_ready
                            pe.wait_ge(ready.sem, ready.upto("pe"))
                        last = mm(b[:, 0:T], w[:, k, :].bitcast(F32R), x[:, k, :].bitcast(F32R),
                                  start=(i + k == 0), stop=(i == 2 and k == n - 1))
                filled(name, last)

            def split_by(phase, q):
                freed[-1] = wt_lo_ready, split[phase][0] + q + 1

            def column_sums(name, src, n, fresh=None, moved=None):
                b = fill(name)
                for k in range(n):
                    if fresh is not None:
                        pe.wait_ge(fresh.sem, fresh.upto("pe"))
                    if moved is not None:
                        pe.wait_ge(*drained(f"{moved}{k}"))
                    last = mm(b[:, 0:T], ones[:, :], src[:, k, :], start=(k == 0), stop=(k == n - 1))
                filled(name, last)

            pe.wait_ge(consts_made, N_CONST)

            def table(t):
                pe.wait_ge(rows_landed[t], 16 * len(TABLE[t]))
                n = sum(m for _, m in TABLE[t])
                b = fill(f"table{t}")
                filled(f"table{t}", nc.tensor.transpose(b[:, 0:n], prow[0:n, t, :], ident[0:n, 0:n]))

            def turn_x():
                pe.wait_ge(x_landed, 16)
                for kk in range(DC // 2):
                    b = fill(f"x{kk}")
                    for k in range(2 * kk, 2 * kk + 2):
                        for i in range(TT):
                            o = (k % 2) * T + i * P
                            last = nc.tensor.transpose(b[:, o:o + P], xin[:, i, k * P:(k + 1) * P], ident[:, :])
                    filled(f"x{kk}", last)

            def ada_unit(n):
                w = weights(f"ada{n}")[:, 0:DC * 512].rearrange("p (k n) -> p k n", k=DC)
                b = fill(f"ada{n}")
                for k in range(DC):
                    g = 32 * (k % 4)
                    last = mm(b[g:g + 32, :], cT[:, k, :], w[:, k, :], start=(k < 4), stop=(k >= DC - 4),
                              skip_group_check=True)
                filled(f"ada{n}", last)
                used_by(f"ada{n}")

            def ada_turn(n):
                pe.wait_ge(*drained(f"ada{n}"))
                b = fill(f"adaT{n}")
                for m in range(4):
                    last = nc.tensor.transpose(b[:, m * P:(m + 1) * P], adar[n % 2][:, m * P:(m + 1) * P], ident[:, :])
                filled(f"adaT{n}", last)

            table(0)
            pe.wait_ge(c_ready, 1)
            for n in range(ADA_FIRST):
                ada_unit(n)
                if n > 0:
                    ada_turn(n - 1)
                if n == 1:
                    turn_x()
            ada_turn(ADA_FIRST - 1)
            for t in range(1, len(TABLE)):
                table(t)

            h_ready.upto("pe", DC)
            for n in range(2 * DI // 512):
                weights(f"a_w_in{n}", wait=False)
                split_by("w_in", 4 * n + 3)
                for m in range(4 * n, 4 * n + 4):
                    part_product("w_in", m, x_hi, sq_lo, m == 0)
                for a in ADA_IN[n]:
                    ada_unit(a)
                    if a > ADA_FIRST:
                        ada_turn(a - 1)
            ada_turn(ADA_MID - 1)
            pe.wait_ge(small_landed, 16 * N_SMALL)
            pe.wait_ge(conv_ready.sem, conv_ready.upto("pe", DIC))
            for g in range(2):
                b = fill(f"gate{g}")
                for k in range(DIC):
                    last = mm(b[0:NH, 0:T], wif[:, k, g * NH:(g + 1) * NH], xc[:, k, :],
                              start=(k == 0), stop=(k == DIC - 1))
                filled(f"gate{g}", last)

            def mlstm_num(h):
                pe.wait_ge(*drained(f"mS{h}"))
                b = fill(f"den{h}")
                mm(b[:, 0:T], ones[:, :], Pm[h % 2][:, 0, :], start=True, stop=False)
                filled(f"den{h}", mm(b[:, P:T], ones[:, :], Pm[h % 2][:, 1, P:T], start=False, stop=True))
                pe.wait_ge(*drained(f"v{h}.0"))
                pe.wait_ge(*drained(f"v{h}.1"))
                for a in range(2):
                    b = fill(f"num{h}.{a}")
                    for m in range(2 * a, 2 * a + 2):
                        o = (m % 2) * T
                        mm(b[:, o:o + T], vm(h, 0)[:, m * P:(m + 1) * P], Pm[h % 2][:, 0, :], start=True, stop=False)
                        last = mm(b[:, o + P:o + T], vm(h, 1)[:, m * P:(m + 1) * P], Pm[h % 2][:, 1, P:T],
                                  start=False, stop=True)
                    filled(f"num{h}.{a}", last)

            def mlstm_mean(h):
                for a in range(2):
                    pe.wait_ge(*drained(f"num{h}.{a}"))
                column_sums(f"gmean{h}", hm, DHC)

            def mlstm_var(h):
                pe.wait_ge(hsq_ready.sem, hsq_ready.upto("pe"))
                column_sums(f"gvar{h}", hsq, DHC)

            for h in range(NH):
                c = DHC * h
                for n, a in enumerate(ADA_HEAD[h]):
                    ada_unit(a)
                    if n:
                        ada_turn(a - 1)
                if ADA_HEAD[h]:
                    ada_turn(ADA_HEAD[h][-1])
                w = weights(f"qk{h}")[:, 0:2 * DHC * DH].rearrange("p (g k n) -> p g k n", g=2, k=DHC)
                for m in range(DHC):
                    product(f"q{h}.{m}", w[:, 0, :, m * P:(m + 1) * P], xc[:, c:c + DHC, :])
                if h > 0:
                    mlstm_num(h - 1)
                for m in range(DHC):
                    product(f"k{h}.{m}", w[:, 1, :, m * P:(m + 1) * P], xc[:, c:c + DHC, :])
                used_by(f"k{h}.{DHC - 1}")
                if h > 0:
                    mlstm_mean(h - 1)
                w = weights(f"v{h}")[:, 0:DHC * DH].rearrange("p (k n) -> p k n", k=DHC)
                for i in range(TT):
                    b = fill(f"v{h}.{i}")
                    for k in range(DHC):
                        last = mm(b[:, :], xm[:, c + k, PAD + i * P:PAD + (i + 1) * P], w[:, k, :],
                                  start=(k == 0), stop=(k == DHC - 1))
                    filled(f"v{h}.{i}", last)
                used_by(f"v{h}.{TT - 1}")
                if h == 0:
                    pe.wait_ge(stab_ready.sem, stab_ready.upto("pe"))
                    b = fill("ucol")
                    for i in range(TT):
                        last = nc.tensor.transpose(b[:, i * NH:(i + 1) * NH], lrow[3][:, i * P:(i + 1) * P],
                                                   ident[0:NH, 0:NH])
                    filled("ucol", last)
                else:
                    mlstm_var(h - 1)
                for m in range(DHC):
                    pe.wait_ge(*drained(f"q{h}.{m}"))
                    pe.wait_ge(*drained(f"k{h}.{m}"))
                b = fill(f"mS{h}")
                for k in range(DHC):
                    mm(b[:, 0:T], km[:, k, 0:P], qm[:, k, :], start=(k == 0), stop=(k == DHC - 1))
                for k in range(DHC):
                    last = mm(b[:, T + P:2 * T], km[:, k, P:T], qm[:, k, P:T], start=(k == 0), stop=(k == DHC - 1))
                filled(f"mS{h}", last)
                if h == 0:
                    pe.wait_ge(emt_ready.sem, emt_ready.upto("pe"))
                b = fill(f"mbc{h}")
                mm(b[:, 0:T], ident[0:NH, h:h + 1].broadcast_to([NH, P]), lrow[5][:, :], start=True, stop=True)
                filled(f"mbc{h}", mm(b[:, T:2 * T], ident[0:NH, h:h + 1].broadcast_to([NH, P]), lrow[6][:, :], start=True, stop=True))
            mlstm_num(NH - 1)
            mlstm_mean(NH - 1)
            mlstm_var(NH - 1)
            for n in range(D // 256):
                w = weights(f"a_w_out{n}")[:, 0:DIC * 256].rearrange("p (k n) -> p k n", k=DIC)
                if n == 0:
                    pe.wait_ge(head_ready.sem, head_ready.upto("pe", NH))
                for m in range(2):
                    product(f"y0.{2 * n + m}", w[:, :, m * P:(m + 1) * P], xc)
                used_by(f"y0.{2 * n + 1}")

            def layer_norm(tag, y=None):
                column_sums(f"{tag}.mean", X, DC, None if y else sum_ready, y)
                column_sums(f"{tag}.var", SQ, DC, squared)

            def rms_norm(tag):
                column_sums(f"{tag}.ms", SQ, DC, squared)

            def swiglu(tag):
                u0, k0, d0 = len(tags), len(uses), down_done.upto("base", 0)

                def r(ap):
                    return ap.bitcast(F32R)

                def up(i, j, fresh=False):
                    k = k0 + j
                    pe.wait_ge(bank_drained[k % 4], i * (BODY // 4) + k // 4)
                    b = bank[k % 4]
                    for g in range(2):
                        for n, (w, x) in enumerate(((w_hi, h_hi), (w_lo, h_hi), (w_hi, h_lo))):
                            if n < 2:
                                pe.wait_ge((w_hi_ready, w_lo_ready)[n][g], i * BODY + (d0 + j + 1))
                            for c in range(DC):
                                if fresh and g == 0 and n != 1:
                                    part = h_lo_ready if n else h_hi_ready
                                    pe.wait_ge(part.sem, part.upto("pe"))
                                last = mm(b[:, g * T:(g + 1) * T], r(w[:, j % 2, g, c * HB:(c + 1) * HB]), r(x[:, c, :]),
                                          start=(n + c == 0), stop=(n == 2 and c == DC - 1))
                    last.then_inc(bank_full[k % 4], 1)

                def down(i, j, first=False, final=False):
                    for ready in (w_hi_ready, w_lo_ready):
                        pe.wait_ge(ready[2], i * BODY + (d0 + j + 1))
                    pe.wait_ge(hid_ready, i * BODY + (d0 + j + 1))
                    for m in range(DC):
                        if final and m and m % 2 == 0:
                            last.then_inc(sum_done, 1)
                        for n, (w, x) in enumerate(((w_hi, hid_hi), (w_lo, hid_hi), (w_hi, hid_lo))):
                            last = mm(ysum(m), r(w[:, j % 2, 2, m * P:(m + 1) * P]), r(x[:, j % 2, :]),
                                      start=first and m % 2 == 0 and n == 0, stop=final and m % 2 == 1 and n == 2,
                                      skip_group_check=True)
                    last.then_inc(down_done.sem, 1)

                up(0, 0, True)
                turns, rest = divmod(STEPS - 1, BODY)
                for j in range(BODY):
                    up(0, j + 1)
                    down(0, j, first=(j == 0))
                with pe.Fori(1, turns) as i:
                    for j in range(BODY):
                        up(i, j + 1)
                        down(i, j)
                for j in range(rest):
                    up(turns, j + 1)
                    down(turns, j)
                down(turns, rest, final=True)
                for s in range(STEPS):
                    uses[f"{tag}.{s}"] = k0 + s
                    tags.append(f"{tag}.{s}")
                    freed.append((w_lo_ready[2], d0 + s + 1))
                down_done.upto("base", STEPS)

            def routing(l):
                b = fill(f"logits{l}")
                for i in range(TT):
                    for k in range(DC):
                        if i == 0:
                            pe.wait_ge(h_ready.sem, h_ready.upto("pe"))
                        last = mm(b[:, i * NE:(i + 1) * NE], H[:, k, i * P:(i + 1) * P], wr[:, k, :],
                                  start=(k == 0), stop=(k == DC - 1))
                filled(f"logits{l}", last)
                for n in range(2 * TT):
                    i, half = divmod(n, 2)
                    b = fill(f"ht{l}.{n}")
                    for c in range(4):
                        last = nc.tensor.transpose(b[:, c * P:(c + 1) * P], H[:, 4 * half + c, i * P:(i + 1) * P],
                                                   ident[:, :])
                    filled(f"ht{l}.{n}", last)
                pe.wait_ge(route_ready.sem, route_ready.upto("pe"))
                b = fill(f"rank{l}")
                for i in range(TT):
                    for j in range(i + 1):
                        last = mm(b[:, i * NE:(i + 1) * NE], upper[:, j, i * P:(i + 1) * P], mask_t[:, j, :],
                                  start=(j == 0), stop=(j == i))
                filled(f"rank{l}", last)

            def gather(banks):
                for k in range(DC):
                    for i in range(TT):
                        last = mm(banks[k // 4][:, (k % 4) * P:(k % 4 + 1) * P], Htok[:, i, k * P:(k + 1) * P],
                                  slot[:, i, :, :].rearrange("p e s -> p (e s)"), start=(i == 0), stop=(i == TT - 1))
                    if k % 4 == 3:
                        yield last

            def moe(l):
                for n in range(2 * TT):
                    pe.wait_ge(*drained(f"ht{l}.{n}"))
                pe.wait_ge(slots_ready, PAIRS * l + 1)
                names = [f"xg{l}.{n}" for n in range(2)]
                for name, ins in zip(names, gather([fill(name) for name in names])):
                    filled(name, ins)
                pe.wait_ge(over_summed, l + 1)
                b = fill(f"over{l}")
                filled(f"over{l}", mm(b[0:1, 0:1], sm[:, 264:265], ones[:, 0:1], start=True, stop=True))

                u0, k0 = len(tags), len(uses)
                uses[f"moe{l}.g0"] = k0

                def unit(i, odd, n, k, cols):
                    u = u0 + PAIR_UNITS * odd + n
                    pe.wait_ge(w_landed[u % WSLOTS], i * (48 * 2 * PAIR_UNITS // WSLOTS) + 48 * (u // WSLOTS + 1))
                    return wring[:, u % WSLOTS, 0:k * cols].rearrange("p (k n) -> p k n", k=k)

                def take(i, odd, step):
                    b, n = pair_use(l, i, odd, step)
                    pe.wait_ge(bank_drained[b], n)
                    return bank[b]

                def done(i, odd, step, ins):
                    ins.then_inc(bank_full[pair_use(l, i, odd, step)[0]], 1)

                def halves(b, x, n, w, cols):
                    for k in range(n):
                        for e in range(2):
                            last = mm(b[e * SLOTS:(e + 1) * SLOTS, :], x[:, k, e * SLOTS:(e + 1) * SLOTS], w[e][:, k, cols],
                                      start=(k == 0), stop=(k == n - 1), skip_group_check=True)
                    return last

                def pair(i, odd):
                    first, last_pair = (isinstance(i, int) and 2 * i + odd == p for p in (0, PAIRS - 1))
                    for n in range(2):
                        pe.wait_ge(*(drained(names[n]) if first else pair_drained(l, i, odd - 1, f"xg{n}")))
                    for n, step in enumerate(("g", "u")):
                        w = [unit(i, odd, 2 * n + e, DC, FE) for e in range(2)]
                        done(i, odd, step, halves(take(i, odd, step), XG, DC, w, slice(0, FE)))
                    if not last_pair:
                        pe.wait_ge(slots_ready, i * 2 + (PAIRS * l + odd + 2))
                        for n, ins in enumerate(gather([take(i, odd, f"xg{n}") for n in range(2)])):
                            done(i, odd, f"xg{n}", ins)
                    pe.wait_ge(*pair_drained(l, i, odd, "u"))
                    b = take(i, odd, "hT")
                    for c in range(FE // P):
                        last = nc.tensor.transpose(b[:, c * P:(c + 1) * P], hide[:, c * P:(c + 1) * P], ident[:, :])
                    done(i, odd, "hT", last)
                    pe.wait_ge(gated_ready, i * 2 + (PAIRS * l + odd + 1))
                    b = take(i, odd, "S")
                    for j in range(TT):
                        last = nc.tensor.transpose(b[:, j * P:(j + 1) * P],
                                                   slot_g[:, j, :, :].rearrange("p e s -> p (e s)"), ident[:, :])
                    done(i, odd, "S", last)
                    w = [unit(i, odd, 4 + e, FE // P, D) for e in range(2)]
                    pe.wait_ge(*pair_drained(l, i, odd, "hT"))
                    for n in range(2):
                        done(i, odd, f"d{n}", halves(take(i, odd, f"d{n}"), hidT, FE // P, w, slice(n * 512, (n + 1) * 512)))
                    for step in ("S", "d0", "d1"):
                        pe.wait_ge(*pair_drained(l, i, odd, step))
                    for m in range(DC):
                        if last_pair and m and m % 2 == 0:
                            last.then_inc(part_scattered, 1)
                        last = mm(ysum(m), ye[:, m * P:(m + 1) * P], S_e, start=first and m % 2 == 0,
                                  stop=last_pair and m % 2 == 1, skip_group_check=True)
                    last.then_inc(scattered, 1)

                all_pairs(pe, pair)
                for p in range(PAIRS):
                    i, odd = divmod(p, 2)
                    for step in LAST_STEPS if p == PAIRS - 1 else PAIR_STEPS:
                        uses[f"moe{l}.{step}{p}"] = len(uses) if (step, p) != ("g", 0) else k0
                    for n in range(PAIR_UNITS):
                        tags.append(f"moe{l}.{p}.{n}")
                        freed.append(pair_full(l, i, odd, ("g", "u", "d1")[n // 2]))
                last_uses = sorted(uses.values())[-4:]
                pe.wait_ge(flagged, l + 1)
                flag = pe.value_load(over_flag[0:1, l:l + 1], min_val=0, max_val=1)
                with pe.If(flag > 0):
                    general(l, last_uses)

            def general(l, last_uses):
                for k in last_uses:
                    pe.wait_ge(bank_drained[k % 4], k // 4 + 1)
                for i in range(TT):
                    last = nc.tensor.transpose(bank[0][0:NE, i * P:(i + 1) * P],
                                               gate_o[:, i, :], ident[:, :])
                last.then_inc(over_filled[l], 1)
                for e in range(0, NE, 2):
                    pe.wait_ge(over_moved[l], e // 2 + 1)
                    for o in range(2):
                        last = mm(bank[0][:, o * T:(o + 1) * T], ident[0:NE, e + o:e + o + 1].broadcast_to([NE, P]), gT,
                                  start=True, stop=True)
                    last.then_inc(over_filled[l], 1)
                w = [wring[:, n, 0:DC * FE].rearrange("p (k n) -> p k n", k=DC) for n in range(2)]
                wd = wring[:, 2, 0:FE * D // P].rearrange("p (k n) -> p k n", k=FE // P)
                blocks = FE // HB
                with pe.Fori(0, NE) as e:
                    pe.wait_ge(over_landed[l], e * 48 + 48)
                    for n in range(blocks):
                        for g in range(2):
                            for k in range(DC):
                                last = mm(bank[1][:, g * T:(g + 1) * T], w[g][:, k, n * HB:(n + 1) * HB], H[:, k, :],
                                          start=(k == 0), stop=(k == DC - 1))
                        last.then_inc(over_up[l], 1)
                        pe.wait_ge(over_hid[l], e * blocks + n + 1)
                        for m in range(DC):
                            last = mm(ysum(m), wd[:, n, m * P:(m + 1) * P], hid_o, start=False, stop=False,
                                      skip_group_check=True)
                        last.then_inc(over_down[l], 1)

            def attention(tag, heads, q_of, k_of, v_of):
                def scores(h):
                    b = fill(f"{tag}.s{h}")
                    mm(b[:, 0:P], q_of(h)[:, 0:P], k_of(h)[:, 0:P], start=True, stop=True)
                    filled(f"{tag}.s{h}", mm(b[:, T:2 * T], q_of(h)[:, P:T], k_of(h), start=True, stop=True))

                def turn(h):
                    pe.wait_ge(prob_ready.sem, prob_ready.upto("pe"))
                    b = fill(f"{tag}.p{h}")
                    E = Es[h % 3]
                    nc.tensor.transpose(b[:, 0:P], E[:, 0, 0:P], ident[:, :])
                    nc.tensor.transpose(b[:, P:T], E[:, 1, 0:P], ident[:, :])
                    filled(f"{tag}.p{h}", nc.tensor.transpose(b[:, T + P:2 * T], E[:, 1, P:T], ident[:, :]))

                def values(h):
                    pe.wait_ge(*drained(f"{tag}.p{h}"))
                    b = fill(f"{tag}.o{h}") if h % 2 == 0 else bank_of(f"{tag}.o{h - 1}")
                    r = 64 * (h % 2)
                    mm(b[r:r + 64, 0:T], v_of(h, 0), PTs[h % 2][:, 0, :], start=True, stop=False)
                    last = mm(b[r:r + 64, P:T], v_of(h, 1), PTs[h % 2][:, 1, P:T], start=False, stop=True)
                    if h % 2:
                        filled(f"{tag}.o{h - 1}", last)

                for it in range(heads + 3):
                    if it < heads:
                        scores(it)
                    if 2 <= it < heads + 2:
                        turn(it - 2)
                    if it >= 3:
                        values(it - 3)

            layer_norm("ln00", "y0.")
            routing(0)
            moe(0)
            layer_norm("ln01")

            for name, src, fresh in (("k", H2, h2_ready), ("v", H2, None), ("q", H, h_ready)):
                for n in range(2):
                    w = weights(f"b{name}{n}")[:, 0:DC * 512].rearrange("p (k n) -> p k n", k=DC)
                    if name == "v":
                        for i in range(TT):
                            b = fill(f"bv{n}.{i}")
                            for k in range(DC):
                                last = mm(b[:, :], H2[:, k, i * P:(i + 1) * P], w[:, k, :],
                                          start=(k == 0), stop=(k == DC - 1))
                            filled(f"bv{n}.{i}", last)
                        used_by(f"bv{n}.{TT - 1}")
                        continue
                    for m in range(4):
                        product(f"b{name}{4 * n + m}", w[:, :, m * P:(m + 1) * P], src, fresh if n + m == 0 else None)
                    used_by(f"b{name}{4 * n + 3}")
            for m in range(DC):
                pe.wait_ge(*drained(f"bk{m}"))
                pe.wait_ge(*drained(f"bq{m}"))
            for n in range(2):
                for i in range(TT):
                    pe.wait_ge(*drained(f"bv{n}.{i}"))
            attention("moba", AH, lambda h: qa[64 * (h % 2):64 * (h % 2) + 64, h // 2, :],
                      lambda h: ka[64 * (h % 2):64 * (h % 2) + 64, h // 2, :],
                      lambda h, i: va[:, i, h * AD:(h + 1) * AD])
            for n in range(2):
                w = weights(f"bo{n}")[:, 0:DC * 512].rearrange("p (k n) -> p k n", k=DC)
                if n == 0:
                    for h in range(0, AH, 2):
                        pe.wait_ge(*drained(f"moba.o{h}"))
                for m in range(4):
                    product(f"y1.{4 * n + m}", w[:, :, m * P:(m + 1) * P], oa)
                used_by(f"y1.{4 * n + 3}")
            layer_norm("ln10", "y1.")
            routing(1)
            moe(1)
            layer_norm("ln11")

            for l in range(DEPTH):
                rms_norm(f"f1{l}")
                swiglu(f"f1{l}")
                rms_norm(f"mx{l}")
                t = f"m{l}."

                def unit(tag, k, n):
                    return weights(t + tag)[:, 0:k * n].rearrange("p (k n) -> p k n", k=k)

                def token_major(name, i, w, src, n):
                    b = fill(name)
                    for k in range(w.shape[1]):
                        last = mm(b[:, 0:n], src[:, k, i * P:(i + 1) * P], w[:, k, :],
                                  start=(k == 0), stop=(k == w.shape[1] - 1))
                    filled(name, last)

                weights(f"{t}cq", wait=False)
                for m in range(QR // P):
                    part_product(f"mix{l}", m, x_hi, x_lo, m == 0)
                split_by(f"mix{l}", 2)
                w = unit("ckv", DC, KVR + ROPE)
                for m in range(KVR // P):
                    part_product(f"mix{l}", 3 + m, x_hi, x_lo)
                for i in range(TT):
                    token_major(f"{t}kr{i}", i, w[:, :, KVR:KVR + ROPE], H, ROPE)
                used_by(f"{t}kr1")
                weights(f"{t}xbc0", wait=False)
                for m in range(4):
                    part_product(f"mix{l}", 5 + m, x_hi, x_lo)
                split_by(f"mix{l}", 8)
                for m in range(3):
                    pe.wait_ge(*drained(f"{t}cq{m}"))
                column_sums(f"{t}cqms", SQ, 3)
                for m in range(2):
                    pe.wait_ge(*drained(f"{t}ckv{m}"))
                column_sums(f"{t}ckvms", SQ[:, 3:5, :], 2)
                w = unit("xbc1", DC, 512 + SH)
                for m in range(4):
                    part_product(f"mix{l}", 9 + m, x_hi, x_lo)
                b = fill(f"{t}dt")
                for i in range(TT):
                    for k in range(DC):
                        last = mm(b[:, i * SH:(i + 1) * SH], H[:, k, i * P:(i + 1) * P], w[:, k, 512:512 + SH],
                                  start=(k == 0), stop=(k == DC - 1))
                filled(f"{t}dt", last)
                used_by(f"{t}dt")
                w = unit("uq", QR // P, MH * QK)
                pe.wait_ge(lat_ready.sem, lat_ready.upto("pe"))
                for i in range(TT):
                    for g in range(2):
                        token_major(f"{t}q{i}.{g}", i, w[:, :, g * 4 * QK:(g + 1) * 4 * QK], cq, 4 * QK)
                used_by(f"{t}q1.1")
                w = unit("ukv", KVR // P, MH * (NOPE + MV))
                pe.wait_ge(lat_ready.sem, lat_ready.upto("pe"))
                for i in range(TT):
                    for g in range(2):
                        token_major(f"{t}kv{i}.{g}", i, w[:, :, g * 512:(g + 1) * 512], ckv, 512)
                used_by(f"{t}kv1.1")
                b = fill(f"{t}wT")
                for g in range(GMG):
                    last = nc.tensor.transpose(b[:, g * P:(g + 1) * P], gmw[:, l, g, :], ident[:, :])
                filled(f"{t}wT", last)
                weights(f"{t}u", wait=False)
                for m in range(4):
                    part_product(f"mix{l}", 13 + m, x_hi, x_lo)
                split_by(f"mix{l}", 16)
                w = unit("v", DC, GMW)
                for i in range(TT):
                    token_major(f"{t}v{i}", i, w, H, GMW)
                used_by(f"{t}v1")
                for name, src in (("qT", Qt), ("kT", Kt)):
                    pe.wait_ge(qkrot_ready.sem, qkrot_ready.upto("pe"))
                    for c in range(MH // 2):
                        b = fill(f"{t}{name}{c}")
                        for h in range(2):
                            for i in range(TT):
                                o = h * T + i * P
                                last = nc.tensor.transpose(b[0:QK, o:o + P], src[:, i, 2 * c + h, :], ident[:, :])
                        filled(f"{t}{name}{c}", last)
                weights(f"{t}z", wait=False)
                for m in range(4):
                    part_product(f"mix{l}", 17 + m, x_hi, x_lo)
                split_by(f"mix{l}", 20)
                pe.wait_ge(*drained(f"{t}wT"))
                pe.wait_ge(vn_ready.sem, vn_ready.upto("pe"))
                for g in range(GMG):
                    b = fill(f"{t}sp{g}")
                    for i in range(TT):
                        last = mm(b[:, i * P:(i + 1) * P], vn[:, i, g * P:(g + 1) * P], wT[:, g, :],
                                  start=True, stop=True)
                    filled(f"{t}sp{g}", last)
                for name in ("qT", "kT"):
                    for c in range(MH // 2):
                        pe.wait_ge(*drained(f"{t}{name}{c}"))
                attention(f"{t}mla", MH, lambda h: QT[0:QK, h, :], lambda h: KT[0:QK, h, :],
                          lambda h, i: Vt[:, i, h * MV:(h + 1) * MV])
                pe.wait_ge(conv_ready.sem, conv_ready.upto("pe", 8))
                for i in range(TT):
                    b = fill(f"{t}xs{i}")
                    for c in range(4):
                        last = nc.tensor.transpose(b[:, c * P:(c + 1) * P], xv[:, c, i * P:(i + 1) * P], ident[:, :])
                    filled(f"{t}xs{i}", last)
                for g in range(SG):
                    b = fill(f"{t}cb{g}")
                    mm(b[:, 0:T], xv[:, 4 + g, 0:P], xv[:, 6 + g, :], start=True, stop=True)
                    filled(f"{t}cb{g}", mm(b[:, T + P:2 * T], xv[:, 4 + g, P:T], xv[:, 6 + g, P:T],
                                           start=True, stop=True))

                def decays(h):
                    pe.wait_ge(decay_in.sem, decay_in.upto("pe"))
                    b = fill(f"{t}ss{h}")
                    M = Mh[h % 2]
                    mm(b[:, 0:T], M[:, 0, 0:P], upper[:, 0, :], start=True, stop=False)
                    mm(b[:, P:T], M[:, 1, 0:P], upper[:, 1, P:T], start=False, stop=True)
                    filled(f"{t}ss{h}", mm(b[:, T + P:2 * T], M[:, 1, P:T], upper[:, 1, P:T], start=True, stop=True))

                def outputs(h):
                    pe.wait_ge(sp_mm_ready.sem, sp_mm_ready.upto("pe"))
                    b = fill(f"{t}y{h}") if h % 2 == 0 else bank_of(f"{t}y{h - 1}")
                    r = SHD * (h % 2)
                    mm(b[r:r + SHD, 0:T], xdt[:, 0, h * SHD:(h + 1) * SHD], Ph[h % 2][:, 0, :], start=True, stop=False)
                    last = mm(b[r:r + SHD, P:T], xdt[:, 1, h * SHD:(h + 1) * SHD], Ph[h % 2][:, 1, P:T],
                              start=False, stop=True)
                    if h % 2:
                        filled(f"{t}y{h - 1}", last)

                for it in range(SH + 1):
                    if it < SH:
                        decays(it)
                    if it >= 1:
                        outputs(it - 1)
                for g in range(SG):
                    column_sums(f"{t}yms{g}", SQ[:, 2 * g:2 * g + 2, :], 2, ysilu_ready)
                q = 0
                for n in range(NB):
                    for hf in range(2):
                        weights(f"{t}g{n}.{hf}", wait=False)
                        split_by(f"merge{l}", q + 3)
                        for m in range(4):
                            part_product(f"merge{l}", q, x_hi, x_lo)
                            q += 1
                    weights(f"{t}br{n}", wait=False)
                    split_by(f"merge{l}", q + DC - 1)
                    pe.wait_ge(y_lo_ready.sem, y_lo_ready.upto("pe"))
                    for m in range(DC):
                        part_product(f"merge{l}", q, y_hi, y_lo)
                        q += 1
                for hf in range(2):
                    weights(f"{t}o{hf}", wait=False)
                    split_by(f"merge{l}", q + 3)
                    for m in range(4):
                        part_product(f"merge{l}", q, x_hi, x_lo, hf + m == 0)
                        q += 1
                rms_norm(f"f2{l}")
                swiglu(f"f2{l}")

            pe.wait_ge(x_ready.sem, DC * (1 + 2 * DEPTH))
            for i in range(TT):
                for hf in range(2):
                    b = fill(f"out{i}.{hf}")
                    for m in range(4):
                        last = nc.tensor.transpose(b[:, m * P:(m + 1) * P], X[:, 4 * hf + m, i * P:(i + 1) * P], ident[:, :])
                    filled(f"out{i}.{hf}", last)

        def swiglu_turns(steps):
            return divmod(steps, BODY)

        @block.scalar
        def _(act):
            f = nc.scalar.activation

            def evac(name, dst, src=None, func=ACT.Copy, last=True, **kw):
                act.wait_ge(*full(name))
                ins = f(dst, bank_of(name)[0:dst.shape[0], 0:T] if src is None else src, func, **kw)
                if last:
                    ins.then_inc(drain_sem(name), 1)

            for t, rows in enumerate(TABLE):
                r = 0
                for name, n in rows:
                    act.dma_start(prow[r:r + n, t, :], A[SOURCES[name]].flatten().rearrange("(r p) -> r p", p=P)) \
                        .then_inc(rows_landed[t], 16)
                    r += n
                if t == 0:
                    act.dma_start(xin, A["x"][0].rearrange("(i p) d -> p i d", p=P)).then_inc(x_landed, 16)
                    act.wait_ge(*drained("table0"))
                    t_c, r_c = col["c"]
                    f(cT[:, :, :], pcol[:, t_c, r_c:r_c + DC].unsqueeze(2).broadcast_to([P, DC, 32]), ACT.Silu).then_inc(c_ready, 1)
            act.wait_ge(consts_made, N_CONST)

            def ada(n):
                evac(f"ada{n}", adar[n % 2], bank_of(f"ada{n}")[:, :])

            for n in range(ADA_FIRST):
                ada(n)

            def conv_silu(m, dst, bias, n):
                act.wait_ge(conv_summed.sem, conv_summed.upto("act"))
                f(dst[:, m, :], dst[:, m, :], ACT.Silu, bias=vec(bias, n)).then_inc(conv_ready.sem, 1)

            def high(phase, q):
                first, tiles = split[phase]
                if q >= len(tiles):
                    return
                u = tags.index(tiles[q][1])
                act.wait_ge(w_landed[u % WSLOTS], 48 * (u // WSLOTS + 1))
                bufs = 2 if "mix" in phase else WBUFS
                if q >= bufs:
                    act.wait_ge(*full(tiles[q - bufs][0]))
                f(part_tile(0, phase, q).bitcast(F32R), raw_tile(phase, q), ACT.Copy).then_inc(wt_hi_ready, 1)

            for k in range(DC):
                act.wait_ge(h_ready.sem, h_ready.upto("act"))
                f(x_hi[:, k, :].bitcast(F32R), H[:, k, :], ACT.Copy).then_inc(x_hi_ready.sem, 1)
            for q in range(WBUFS):
                high("w_in", q)
            act.wait_ge(pad_cleared.sem, pad_cleared.upto("act"))
            for n in range(2 * DIC):
                if n < DIC:
                    evac(f"w_in{n}", xm[:, n, PAD:PAD + T])
                else:
                    evac(f"w_in{n}", sz[:, n - DIC, :], func=ACT.Silu)
                high("w_in", n + WBUFS)
                if 2 <= n < DIC + 2:
                    conv_silu(n - 2, xc, "conv_b", n - 2)
                if n % 4 == 3:
                    for a in ADA_IN[n // 4]:
                        ada(a)
            act.wait_ge(small_landed, 16 * N_SMALL)
            f(alb[:, :, :], alb[:, :, :], ACT.Exp).then_inc(consts_derived, 1)
            for g in range(2):
                evac(f"gate{g}", lrow[g], func=ACT.Identity, bias=bif[:, g:g + 1])

            def softplus_tail(e, u):
                act.wait_ge(abs_ready.sem, abs_ready.upto("act"))
                f(e, e, ACT.Exp, scale=-1.0).then_inc(aexp_ready.sem, 1)
                act.wait_ge(plus_one.sem, plus_one.upto("act"))
                f(u, u, ACT.Ln).then_inc(ln_ready.sem, 1)

            ucol = sm[:, 0:TT * NH]
            for h in range(NH):
                for a in ADA_HEAD[h]:
                    ada(a)
                for m in range(DHC):
                    evac(f"q{h}.{m}", qm[:, m, :])
                    if h == 0 and m == 1:
                        softplus_tail(lrow[7], lrow[2])
                for m in range(DHC):
                    evac(f"k{h}.{m}", km[:, m, :])
                if h == 0:
                    act.wait_ge(rows_made.sem, rows_made.upto("act"))
                    f(lrow[6], lrow[6], ACT.Exp, scale=-1.0).then_inc(emt_ready.sem, 1)
                    evac("ucol", ucol, bank_of("ucol")[:, 0:TT * NH])
                else:
                    mlstm_norm = h - 1
                    act.wait_ge(hc_ready.sem, hc_ready.upto("act"))
                    f(hsq, hm, ACT.Square).then_inc(hsq_ready.sem, 1)
                    evac(f"gvar{mlstm_norm}", nrm[:, 0, :], func=ACT.Sqrt, scale=1.0 / DH, bias=eps_ln[:, :])
                act.wait_ge(dlog_ready.sem, dlog_ready.upto("act"))
                if h == 0:
                    act.wait_ge(*drained("ucol"))
                W = Wm[h % 2]
                f(W[:, 0, :], W[:, 0, :], ACT.Exp, bias=ucol[:, h:h + 1])
                f(W[:, 1, P:T], W[:, 1, P:T], ACT.Exp, bias=ucol[:, NH + h:NH + h + 1]).then_inc(wexp_ready.sem, 1)
            act.wait_ge(hc_ready.sem, hc_ready.upto("act"))
            f(hsq, hm, ACT.Square).then_inc(hsq_ready.sem, 1)
            evac(f"gvar{NH - 1}", nrm[:, 0, :], func=ACT.Sqrt, scale=1.0 / DH, bias=eps_ln[:, :])

            def squares(fresh, moved=None):
                for k in range(DC):
                    if moved is None:
                        act.wait_ge(fresh.sem, fresh.upto("act"))
                    else:
                        act.wait_ge(*drained(f"{moved}{k}"))
                    f(SQ[:, k, :], X[:, k, :], ACT.Square).then_inc(squared.sem, 1)

            def layer_norm(tag, outs):
                squares(centered)
                evac(f"{tag}.var", nrm[:, 0, :], func=ACT.Sqrt, scale=1.0 / D, bias=eps_ln[:, :])
                for n, (dst, ready) in enumerate(outs):
                    for k in range(DC):
                        act.wait_ge(normed.sem, normed.upto("act"))
                        offset = lnv[:, 2 * n + 1, k:k + 1] if dst is not X else vec("ln_b", (2 * DEPTH - 1) * DC + k)
                        f(dst[:, k, :], dst[:, k, :], ACT.Identity, bias=offset).then_inc(ready.sem, 1)

            def rms_norm(tag, moved=None):
                squares(x_ready, moved)
                evac(f"{tag}.ms", nrm[:, 0, :], func=ACT.Sqrt, scale=1.0 / D, bias=eps_rms[:, :])

            def routing(l):
                act.wait_ge(*drained(f"logits{l}"))
                f(sm[:, 32:64], sm[:, 32:64], ACT.Exp).then_inc(router_exp.sem, 1)
                for n in range(2 * TT):
                    i, half = divmod(n, 2)
                    evac(f"ht{l}.{n}", Htok[:, i, half * 512:(half + 1) * 512], bank_of(f"ht{l}.{n}")[:, :])

            def moe(l):
                for n in range(2):
                    evac(f"xg{l}.{n}", XG[:, 4 * n:4 * n + 4, :].rearrange("p k s -> p (k s)"), bank_of(f"xg{l}.{n}")[:, :])

                def move(i, odd, step, dst, func=ACT.Copy):
                    act.wait_ge(*pair_full(l, i, odd, step))
                    f(dst, pair_bank(l, i, odd, step)[:, :], func).then_inc(pair_drain_sem(l, i, odd, step), 1)

                def pair(i, odd):
                    move(i, odd, "g", sge, ACT.Silu)
                    if not (isinstance(i, int) and 2 * i + odd == PAIRS - 1):
                        for n in range(2):
                            move(i, odd, f"xg{n}", XG[:, 4 * n:4 * n + 4, :].rearrange("p k s -> p (k s)"))
                    move(i, odd, "hT", hidT.rearrange("p k s -> p (k s)"))
                    move(i, odd, "d1", ye[:, 512:D])

                all_pairs(act, pair)
                act.wait_ge(flagged, l + 1)
                flag = act.value_load(over_flag[0:1, l:l + 1], min_val=0, max_val=1)
                with act.If(flag > 0):
                    act.wait_ge(over_filled[l], 1)
                    f(gT, bank[0][0:NE, 0:T], ACT.Copy).then_inc(over_moved[l], 1)
                    for e in range(0, NE, 2):
                        act.wait_ge(over_filled[l], e // 2 + 2)
                        f(gbc[:, e:e + 2, :].rearrange("p a t -> p (a t)"), bank[0][:, :], ACT.Copy) \
                            .then_inc(over_moved[l], 1)
                    with act.Fori(0, NE) as e:
                        for n in range(FE // HB):
                            act.wait_ge(over_up[l], e * (FE // HB) + n + 1)
                            f(sg_o, bank[1][:, 0:T], ACT.Silu).then_inc(over_silu[l], 1)

            def swiglu(tag, n):
                k0, d0, u0 = uses[f"{tag}.0"], n * STEPS, tags.index(f"{tag}.0")

                def high(i, j, part):
                    u = u0 + j
                    act.wait_ge(w_landed[u % WSLOTS], i * 48 + 48 * (u // WSLOTS + 1))
                    f(w_hi[:, j % 2, part, :].bitcast(F32R), wring[:, u % WSLOTS, part * DC * HB:(part + 1) * DC * HB],
                      ACT.Copy).then_inc(w_hi_ready[part], 1)

                def step(i, j, ahead=2):
                    k = k0 + j
                    act.wait_ge(bank_full[k % 4], i + k // 4 + 1)
                    f(sg[:, j % 2, :], bank[k % 4][:, 0:T], ACT.Silu).then_inc(silu_ready.sem, 1)
                    if ahead == 2:
                        for part in range(2):
                            high(i, j + 2, part)
                    if ahead >= 1:
                        if not (isinstance(i, int) and i == j == 0):
                            act.wait_ge(down_done.sem, i * BODY + (d0 + j))
                        high(i, j + 1, 2)

                high(0, 0, 0)
                for k in range(DC):
                    act.wait_ge(h_ffn_ready.sem, h_ffn_ready.upto("act"))
                    f(h_hi[:, k, :].bitcast(F32R), H[:, k, :], ACT.Copy).then_inc(h_hi_ready.sem, 1)
                    if k == 3:
                        high(0, 0, 1)
                high(0, 1, 0)
                high(0, 1, 1)
                high(0, 0, 2)
                turns, rest = swiglu_turns(STEPS)
                for j in range(BODY):
                    step(0, j)
                with act.Fori(1, turns) as i:
                    for j in range(BODY):
                        step(i, j)
                for j in range(rest):
                    step(turns, j, min(2, rest - 1 - j))

            def attention(tag, heads, o):
                def exps(h):
                    act.wait_ge(score_ready.sem, score_ready.upto("act"))
                    S, E, c = Ss[h % 2], Es[h % 3], 64 + 8 * (h % 2)
                    f(E[:, 0, 0:P], S[:, 0, 0:P], ACT.Exp, bias=sm[:, c:c + 1], accum_out=sm[:, c + 2:c + 3])
                    f(E[:, 1, :], S[:, 1, :], ACT.Exp, bias=sm[:, c + 1:c + 2], accum_out=sm[:, c + 3:c + 4]) \
                        .then_inc(prob_exp.sem, 1)

                def turned(h):
                    name = f"{tag}.p{h}"
                    evac(name, PTs[h % 2][:, 0, :], last=False)
                    evac(name, PTs[h % 2][:, 1, P:T], bank_of(name)[:, T + P:2 * T])

                for it in range(heads + 3):
                    if it < heads:
                        exps(it)
                    if 2 <= it < heads + 2:
                        turned(it - 2)
                    if it >= 4 and it % 2 == 0:
                        evac(f"{tag}.o{it - 4}", o[:, (it - 4) // 2, :])

            layer_norm("ln00", [(H, h_ready)])
            routing(0)
            moe(0)
            act.wait_ge(rope_in.sem, rope_in.upto("act"))
            for a in range(2):
                last = f(trig[:, a, :, :], trig[:, a, :, :], ACT.Sin)
            last.then_inc(rope_ready.sem, 1)
            layer_norm("ln01", [(H2, h2_ready), (H, h_ready)])

            for m in range(DC):
                evac(f"bk{m}", ka[:, m, :])
            for n in range(2):
                for i in range(TT):
                    evac(f"bv{n}.{i}", va[:, i, n * 512:(n + 1) * 512], bank_of(f"bv{n}.{i}")[:, :])
            for m in range(DC):
                evac(f"bq{m}", qa[:, m, :], scale=AD ** -0.5)
            attention("moba", AH, oa)
            layer_norm("ln10", [(H, h_ready)])
            routing(1)
            moe(1)
            layer_norm("ln11", [(X, x_ready)])

            for l in range(DEPTH):
                rms_norm(f"f1{l}")
                swiglu(f"f1{l}", 2 * l)
                rms_norm(f"mx{l}")
                t = f"m{l}."
                high(f"mix{l}", 0)
                for k in range(DC):
                    act.wait_ge(h_mix_ready.sem, h_mix_ready.upto("act"))
                    f(x_hi[:, k, :].bitcast(F32R), H[:, k, :], ACT.Copy).then_inc(x_hi_ready.sem, 1)
                high(f"mix{l}", 1)
                for m in range(3):
                    high(f"mix{l}", m + 2)
                    evac(f"{t}cq{m}", cq[:, m, :], last=False)
                    evac(f"{t}cq{m}", SQ[:, m, :], func=ACT.Square)
                for m in range(2):
                    high(f"mix{l}", m + 5)
                    evac(f"{t}ckv{m}", ckv[:, m, :], last=False)
                    evac(f"{t}ckv{m}", SQ[:, 3 + m, :], func=ACT.Square)
                for i in range(TT):
                    evac(f"{t}kr{i}", krs[:, i, :], bank_of(f"{t}kr{i}")[:, 0:ROPE])
                act.wait_ge(pad_cleared.sem, pad_cleared.upto("act"))
                for m in range(4):
                    high(f"mix{l}", m + 7)
                    evac(f"{t}xbc{m}", xb[:, m, PAD:PAD + T])
                evac(f"{t}cqms", nrm[:, 0, :], func=ACT.Sqrt, scale=1.0 / QR, bias=eps_rms[:, :])
                evac(f"{t}ckvms", nrm[:, 1, :], func=ACT.Sqrt, scale=1.0 / KVR, bias=eps_rms[:, :])
                for m in range(4, 8):
                    high(f"mix{l}", m + 7)
                    evac(f"{t}xbc{m}", xb[:, m, PAD:PAD + T])
                for i in range(TT):
                    for g in range(2):
                        evac(f"{t}q{i}.{g}", Qt[:, i, 4 * g:4 * g + 4, :].rearrange("p h d -> p (h d)"),
                             bank_of(f"{t}q{i}.{g}")[:, 0:4 * QK])
                qkb = [sm[:, 96:112], sm[:, 112:128]]
                for n, src in enumerate((Qt, Kt)):
                    if n:
                        for i in range(TT):
                            for g in range(2):
                                b = bank_of(f"{t}kv{i}.{g}")[:, :].rearrange("p (h d) -> p h d", h=4)
                                evac(f"{t}kv{i}.{g}", Kt[:, i, 4 * g:4 * g + 4, 0:NOPE], b[:, :, 0:NOPE], last=False)
                                evac(f"{t}kv{i}.{g}", Vt[:, i, 4 * g * MV:(4 * g + 4) * MV].rearrange("p (h d) -> p h d", h=4),
                                     b[:, :, NOPE:NOPE + MV])
                    if n:
                        act.wait_ge(qksq_ready.sem, qksq_ready.upto("act"))
                    for i in range(TT):
                        for g in range(2):
                            act.wait_ge(*drained(f"{t}{'kv' if n else 'q'}{i}.{g}"))
                    f(qksq, src.rearrange("p i h d -> p (i h d)"), ACT.Square).then_inc(qkss_ready.sem, 1)
                    if n:
                        for m in range(2):
                            high(f"mix{l}", m + 15)
                            evac(f"{t}u{m}", us[:, m, :], func=ACT.Gelu)
                    act.wait_ge(qkstd_ready.sem, qkstd_ready.upto("act"))
                    f(qkb[n], qkb[n], ACT.Sqrt, scale=1.0 / QK, bias=eps_rms[:, :]).then_inc(qkstd_ready.sem, 1)
                    qkstd_ready.upto("act")
                for m in range(2, 4):
                    high(f"mix{l}", m + 15)
                    evac(f"{t}u{m}", us[:, m, :], func=ACT.Gelu)
                softplus_tail(sm[:, 144:160], sm[:, 160:176])
                for i in range(TT):
                    evac(f"{t}v{i}", vn[:, i, :], bank_of(f"{t}v{i}")[:, :], ACT.Gelu)
                squares_of_v = SQ[:, 0:4, :].rearrange("p (i a) t -> p i (a t)", i=TT)
                for i in range(TT):
                    act.wait_ge(*drained(f"{t}v{i}"))
                    last = f(squares_of_v[:, i, :], vn[:, i, :], ACT.Square, accum_out=sm[:, 80 + i:81 + i])
                last.then_inc(vsq_ready.sem, 1)
                act.wait_ge(vsq_ready.sem, vsq_ready.upto("act"))
                f(sm[:, 80:82], sm[:, 80:82], ACT.Sqrt, scale=1.0 / GMW, bias=eps_rms[:, :]).then_inc(vsq_ready.sem, 1)
                vsq_ready.upto("act")
                for name, dst in (("qT", QT), ("kT", KT)):
                    for c in range(MH // 2):
                        evac(f"{t}{name}{c}", dst[0:QK, 2 * c:2 * c + 2, :],
                             bank_of(f"{t}{name}{c}")[0:QK, :].rearrange("p (h t) -> p h t", h=2))
                for m in range(4):
                    high(f"mix{l}", m + 19)
                    evac(f"{t}z{m}", zs[:, m, :], func=ACT.Silu)
                for m in range(8):
                    conv_silu(m, xv, "conv_b2", 8 * l + m)
                attention(f"{t}mla", MH, yB)
                for h in range(SH):
                    act.wait_ge(*full(f"{t}ss{h}"))
                    b = bank_of(f"{t}ss{h}")
                    evac(f"{t}ss{h}", Eh[h % 2][:, 0, :], last=False, func=ACT.Exp)
                    evac(f"{t}ss{h}", Eh[h % 2][:, 1, P:T], b[:, T + P:2 * T], func=ACT.Exp)
                    if h >= SH - 2:
                        high(f"merge{l}", h - (SH - 2))
                for c in range(4):
                    act.wait_ge(yz_ready.sem, yz_ready.upto("act"))
                    f(SQ[:, c, :], yC[:, c, :], ACT.Square).then_inc(ysilu_ready.sem, 1)
                for g in range(SG):
                    evac(f"{t}yms{g}", nrm[:, g, :], func=ACT.Sqrt, scale=1.0 / (SI // SG), bias=eps_rms[:, :])
                high(f"merge{l}", 2)
                q = 0
                for n in range(NB):
                    for m in range(DC):
                        evac(f"{t}g{n}.{m}", sig[n % 2][:, m, :], func=ACT.Sigmoid)
                        high(f"merge{l}", q + WBUFS)
                        q += 1
                        if m == 0:
                            if n == 0:
                                act.wait_ge(sp_ready.sem, sp_ready.upto("act"))
                            elif n == 1:
                                for h in range(0, MH, 2):
                                    act.wait_ge(*drained(f"{t}mla.o{h}"))
                            else:
                                act.wait_ge(yc_ready.sem, yc_ready.upto("act"))
                            if n:
                                act.wait_ge(*full(f"{t}br{n - 1}.{DC - 1}"))
                            f(y_hi[:, :, :].bitcast(F32R), (yA, yB, yC)[n], ACT.Copy).then_inc(y_hi_ready.sem, 1)
                    for m in range(DC):
                        high(f"merge{l}", q + WBUFS)
                        q += 1
                        if n == NB - 1:
                            act.wait_ge(merged_ready.sem, merged_ready.upto("act"))
                            f(x_hi[:, m, :].bitcast(F32R), merged[:, m, :], ACT.Copy).then_inc(x_hi_ready.sem, 1)
                for m in range(DC):
                    high(f"merge{l}", q + WBUFS)
                    q += 1
                rms_norm(f"f2{l}", f"{t}o")
                swiglu(f"f2{l}", 2 * l + 1)
            for i in range(TT):
                for hf in range(2):
                    evac(f"out{i}.{hf}", xo[:, i, hf * 512:(hf + 1) * 512], bank_of(f"out{i}.{hf}")[:, :])

        @block.vector
        def _(dve):
            v = nc.vector
            tt, ts, stt = v.tensor_tensor, v.tensor_scalar, v.scalar_tensor_tensor
            steps = [0]

            def link(ins):
                ins.then_inc(dve_steps, 1)
                steps[0] += 1
                dve.wait_ge(dve_steps, steps[0])

            def moved(name, ins):
                ins.then_inc(drain_sem(name), 1)

            def rows(ap, n):
                return ap.unsqueeze(1).broadcast_to([ap.shape[0], n, ap.shape[1]])

            def each(ap, n):
                return ap.unsqueeze(2).broadcast_to([ap.shape[0], ap.shape[1], n])

            def table(t):
                n = sum(m for _, m in TABLE[t])
                dve.wait_ge(*full(f"table{t}"))
                moved(f"table{t}", v.tensor_copy(pcol[:, t, 0:n], bank_of(f"table{t}")[:, 0:n]))

            table(0)

            def ada(n):
                dve.wait_ge(*full(f"adaT{n}"))
                src = bank_of(f"adaT{n}")[:, :].rearrange("p (m g c) -> p m g c", m=4, g=4)[:, :, :, 0]
                moved(f"adaT{n}", v.tensor_reduce(mods[:, 4 * n:4 * n + 4], src, AX.X, ALU.add))

            def finish_ada(n0, n1):
                for n in range(n0, n1):
                    dve.wait_ge(*drained(f"adaT{n}"))
                t, r = col["b_ada"]
                c0, c1 = 4 * n0, 4 * n1
                link(tt(mods[:, c0:c1], mods[:, c0:c1], pcol[:, t, r + c0:r + c1], ALU.add))
                for g in range(0, 4 * ADA_UNITS, 3 * DC):
                    first, end = max(g + DC, c0), min(g + 3 * DC, c1)
                    if first < end:
                        last = ts(mods[:, first:end], mods[:, first:end], 1.0, None, ALU.add)
                link(last)

            def modulate(dst, layer, s, ready):
                for k in range(DC):
                    ts(dst[:, k, :], X[:, k, :], mod(layer, s, 1, k), mod(layer, s, 0, k), ALU.mult, ALU.add) \
                        .then_inc(ready.sem, 1)

            for n in range(ADA_FIRST):
                if n == 1:
                    for kk in range(DC // 2):
                        dve.wait_ge(*full(f"x{kk}"))
                        moved(f"x{kk}", v.tensor_copy(X[:, 2 * kk:2 * kk + 2, :],
                                                      bank_of(f"x{kk}")[:, :].rearrange("p (a t) -> p a t", a=2)))
                ada(n)
            dve.wait_ge(*drained("table0"))
            for kk in range(DC // 2):
                dve.wait_ge(*drained(f"x{kk}"))
            finish_ada(0, ADA_FIRST)

            def scale_residual():
                dve.wait_ge(h_ready.sem, h_ready.upto("dve", DC))
                link(ts(X[:, :, :], X[:, :, :], ALPHA, None, ALU.mult))

            def low(phase, q):
                first, tiles = split[phase]
                if q < len(tiles):
                    dve.wait_ge(wt_hi_ready, first + q + 1)
                    tt(part_tile(1, phase, q).bitcast(F32R), raw_tile(phase, q), part_tile(0, phase, q),
                       ALU.subtract).then_inc(wt_lo_ready, 1)

            def x_low(src, k, lo=x_lo):
                dve.wait_ge(x_hi_ready.sem, x_hi_ready.upto("dve"))
                tt(lo[:, k, :].bitcast(F32R), src[:, k, :], x_hi[:, k, :], ALU.subtract).then_inc(x_lo_ready.sem, 1)

            modulate(H, 0, 0, h_ready)
            for k in range(DC):
                x_low(H, k, sq_lo)
            for q in range(WBUFS):
                low("w_in", q)
            scale_residual()
            for t in range(1, len(TABLE)):
                table(t)
            for t in range(1, len(TABLE)):
                dve.wait_ge(*drained(f"table{t}"))
            v.memset(xm[:, :, 0:PAD], 0.0).then_inc(pad_cleared.sem, 1)
            dve.wait_ge(pad_cleared.sem, pad_cleared.upto("dve"))

            def conv(src, dst, m, taps):
                link(ts(dst[:, m, :], src[:, m, 0:T], taps[0], None, ALU.mult))
                for j in range(1, CONV):
                    ins = stt(dst[:, m, :], src[:, m, j:j + T], taps[j], dst[:, m, :], ALU.mult, ALU.add)
                    if j < CONV - 1:
                        link(ins)
                ins.then_inc(conv_summed.sem, 1)

            for n in range(2 * DIC // 4):
                for m in range(4 * n, 4 * n + 4):
                    if m < DIC:
                        dve.wait_ge(*drained(f"w_in{m}"))
                        conv(xm, xc, m, [vec("conv_w", j * DIC + m) for j in range(CONV)])
                    low("w_in", m + WBUFS)
                for a in ADA_IN[n]:
                    if a > ADA_FIRST:
                        ada(a - 1)
            ada(ADA_MID - 1)
            finish_ada(ADA_FIRST, ADA_MID)

            def log1p_exp(e, u, d, z):
                dve.wait_ge(aexp_ready.sem, aexp_ready.upto("dve"))
                link(ts(u, e, 1.0, None, ALU.add))
                link(ts(d, u, 1.0, None, ALU.subtract))
                ts(z, d, 0.0, None, ALU.is_equal).then_inc(plus_one.sem, 1)
                dve.wait_ge(plus_one.sem, plus_one.upto("dve"))
                link(tt(d, d, z, ALU.add))
                dve.wait_ge(ln_ready.sem, ln_ready.upto("dve"))
                link(tt(u, u, z, ALU.add))
                link(v.reciprocal(d, d))
                link(tt(u, u, d, ALU.mult))
                link(tt(u, u, e, ALU.mult))

            for g in range(2):
                dve.wait_ge(*drained(f"gate{g}"))
            v.memset(lrow[6], 1.0)
            stt(lrow[7], lrow[1], -1.0, lrow[1], ALU.mult, ALU.max).then_inc(abs_ready.sem, 1)
            dve.wait_ge(abs_ready.sem, abs_ready.upto("dve"))
            log1p_exp(lrow[7], lrow[2], lrow[3], lrow[4])
            link(stt(lrow[1], lrow[1], 0.0, lrow[2], ALU.min, ALU.subtract))
            link(v.tensor_tensor_scan(lrow[4], lrow[6], lrow[1], 0.0, ALU.mult, ALU.add))
            tt(lrow[3], lrow[0], lrow[4], ALU.subtract).then_inc(stab_ready.sem, 1)
            dve.wait_ge(stab_ready.sem, stab_ready.upto("dve"))
            link(v.tensor_tensor_scan(lrow[2], lrow[3], lrow[3], 0.0, ALU.max, ALU.max))
            ts(lrow[5], lrow[2], -1.0, None, ALU.mult)
            tt(lrow[6], lrow[4], lrow[2], ALU.add).then_inc(rows_made.sem, 1)

            def mlstm_num(h):
                dve.wait_ge(*full(f"den{h}"))
                moved(f"den{h}", v.tensor_copy(nrm[:, 1, :], bank_of(f"den{h}")[:, 0:T]))
                dve.wait_ge(*drained(f"den{h}"))
                dve.wait_ge(*drained(f"mbc{h}"))
                link(tt(den_s, den_s, nrm[:, 1, :], ALU.max))
                link(stt(den_s, nrm[:, 1, :], -1.0, den_s, ALU.mult, ALU.max))
                link(v.reciprocal(den_s, den_s))
                for a in range(2):
                    name = f"num{h}.{a}"
                    dve.wait_ge(*full(name))
                    moved(name, tt(hm[:, 2 * a:2 * a + 2, :], bank_of(name)[:, :].rearrange("p (a t) -> p a t", a=2),
                                   rows(den_s, 2), ALU.mult))
                dve.wait_ge(*full(f"gmean{h}"))
                moved(f"gmean{h}", ts(nrm[:, 1, :], bank_of(f"gmean{h}")[:, 0:T], -1.0 / DH, None, ALU.mult))
                dve.wait_ge(*drained(f"gmean{h}"))
                tt(hm, hm, rows(nrm[:, 1, :], DHC), ALU.add).then_inc(hc_ready.sem, 1)

            def mlstm_out(h):
                dve.wait_ge(*drained(f"gvar{h}"))
                link(v.reciprocal(nrm[:, 0, :], nrm[:, 0, :]))
                link(tt(hm, hm, rows(nrm[:, 0, :], DHC), ALU.mult))
                c = DHC * h
                for m in range(DHC):
                    last = ts(xc[:, c + m, :], xc[:, c + m, :], vec("skip", c + m), None, ALU.mult)
                link(last)
                for m in range(DHC):
                    last = stt(xc[:, c + m, :], hm[:, m, :], vec("gn_g", c + m), xc[:, c + m, :], ALU.mult, ALU.add)
                link(last)
                tt(xc[:, c:c + DHC, :], xc[:, c:c + DHC, :], sz[:, c:c + DHC, :], ALU.mult).then_inc(head_ready.sem, 1)

            for h in range(NH):
                for a in ADA_HEAD[h]:
                    ada(a)
                if h > 0:
                    mlstm_num(h - 1)
                if h == NH - 1:
                    finish_ada(ADA_MID, ADA_UNITS)
                for i in range(TT):
                    dve.wait_ge(*full(f"v{h}.{i}"))
                    moved(f"v{h}.{i}", v.tensor_copy(vm(h, i), bank_of(f"v{h}.{i}")[:, :]))
                if h > 0:
                    mlstm_out(h - 1)
                dve.wait_ge(*full(f"mbc{h}"))
                b, W = bank_of(f"mbc{h}"), Wm[h % 2]
                tt(W[:, 0, :], b[:, 0:T], neg_st[:, 0, :], ALU.add)
                tt(W[:, 1, P:T], b[:, P:T], neg_st[:, 1, P:T], ALU.add).then_inc(dlog_ready.sem, 1)
                moved(f"mbc{h}", v.tensor_copy(den_s, b[:, T:2 * T]))
                dve.wait_ge(*full(f"mS{h}"))
                dve.wait_ge(wexp_ready.sem, wexp_ready.upto("dve"))
                b = bank_of(f"mS{h}")
                stt(Pm[h % 2][:, 0, :], b[:, 0:T], DH ** -0.5, W[:, 0, :], ALU.mult, ALU.mult)
                moved(f"mS{h}", stt(Pm[h % 2][:, 1, P:T], b[:, T + P:2 * T], DH ** -0.5, W[:, 1, P:T], ALU.mult, ALU.mult))
            mlstm_num(NH - 1)
            mlstm_out(NH - 1)

            def layer_norm(tag, layer, s, y=None, outs=()):
                t, r = col["ln_g"]
                g = pcol[:, t, r + (layer * 2 + s) * DC:r + (layer * 2 + s + 1) * DC]
                t, r = col["ln_b"]
                b = pcol[:, t, r + (layer * 2 + s) * DC:r + (layer * 2 + s + 1) * DC]
                for n, (_, shift, scale, _) in enumerate(outs):
                    tt(lnv[:, 2 * n, :], g, mods[:, scale:scale + DC], ALU.mult)
                    tt(lnv[:, 2 * n + 1, :], b, mods[:, scale:scale + DC], ALU.mult)
                ts(lnv[:, 4, :], g, ALPHA, None, ALU.mult)
                link(ts(lnv[:, 5, :], b, ALPHA, None, ALU.mult))
                for n, (_, shift, scale, _) in enumerate(outs):
                    link(tt(lnv[:, 2 * n + 1, :], lnv[:, 2 * n + 1, :], mods[:, shift:shift + DC], ALU.add))
                for m in range(DC):
                    if y:
                        dve.wait_ge(*full(f"{y}{m}"))
                        moved(f"{y}{m}", stt(X[:, m, :], bank_of(f"{y}{m}")[:, 0:T], mod(layer, s, 2, m), X[:, m, :],
                                             ALU.mult, ALU.add))
                    else:
                        if m < DC - 2:
                            dve.wait_ge(part_scattered, layer * (DC // 2 - 1) + m // 2 + 1)
                        else:
                            dve.wait_ge(scattered, PAIRS * (layer + 1))
                        stt(X[:, m, :], ysum(m), mod(layer, s, 2, m), X[:, m, :], ALU.mult, ALU.add) \
                            .then_inc(sum_ready.sem, 1)
                dve.wait_ge(*full(f"{tag}.mean"))
                moved(f"{tag}.mean", ts(nrm[:, 1, :], bank_of(f"{tag}.mean")[:, 0:T], -1.0 / D, None, ALU.mult))
                dve.wait_ge(*drained(f"{tag}.mean"))
                for m in range(DC):
                    tt(X[:, m, :], X[:, m, :], nrm[:, 1, :], ALU.add).then_inc(centered.sem, 1)
                dve.wait_ge(*drained(f"{tag}.var"))
                link(v.reciprocal(nrm[:, 0, :], nrm[:, 0, :]))
                if not outs:
                    for m in range(DC):
                        stt(X[:, m, :], X[:, m, :], g[:, m:m + 1], nrm[:, 0, :], ALU.mult, ALU.mult).then_inc(normed.sem, 1)
                    normed.upto("dve", DC)
                    return
                for n, (dst, _, _, ready) in enumerate(outs):
                    for m in range(DC):
                        stt(dst[:, m, :], X[:, m, :], lnv[:, 2 * n, m:m + 1], nrm[:, 0, :], ALU.mult, ALU.mult) \
                            .then_inc(normed.sem, 1)
                    ready.upto("dve", DC)
                dve.wait_ge(normed.sem, normed.upto("dve", DC * len(outs)))
                for m in range(DC):
                    last = stt(X[:, m, :], X[:, m, :], lnv[:, 4, m:m + 1], nrm[:, 0, :], ALU.mult, ALU.mult)
                link(last)
                for m in range(DC):
                    last = ts(X[:, m, :], X[:, m, :], lnv[:, 5, m:m + 1], None, ALU.add)
                link(last)

            def modulation(layer, s):
                return (layer * 2 + s) * 3 * DC, ((layer * 2 + s) * 3 + 1) * DC

            def rms_norm(tag, gain, l, ready):
                dve.wait_ge(*drained(f"{tag}.ms"))
                link(v.reciprocal(nrm[:, 0, :], nrm[:, 0, :]))
                for k in range(DC):
                    stt(H[:, k, :], X[:, k, :], vec(gain, l * DC + k), nrm[:, 0, :], ALU.mult, ALU.mult) \
                        .then_inc(ready.sem, 1)
                dve.wait_ge(ready.sem, ready.upto("dve", DC))

            def routing(l):
                def s3(a, n, m):
                    return sm[:, a:a + n * m].rearrange("p (n m) -> p n m", n=n)

                gate, e, selp = s3(0, TT, NE), s3(32, TT, NE), s3(200, TT, NE)
                top, tot = sm[:, 192:194], sm[:, 194:196]
                dve.wait_ge(*full(f"logits{l}"))
                b = bank_of(f"logits{l}")[:, 0:TT * NE].rearrange("p (n m) -> p n m", n=TT)
                link(v.tensor_reduce(top, b, AX.X, ALU.max))
                moved(f"logits{l}", tt(e, b, each(top, NE), ALU.subtract))
                dve.wait_ge(router_exp.sem, router_exp.upto("dve"))
                link(v.tensor_reduce(tot, e, AX.X, ALU.add))
                link(v.reciprocal(tot, tot))
                link(tt(e, e, each(tot, NE), ALU.mult))
                link(tt(selp, e, rows(brb[:, :], TT), ALU.add))
                s4 = s3(200, TT * NGRP, EPG)
                pairs = s3(232, 6, TT * NGRP)
                for n, (i, j) in enumerate([(i, j) for i in range(EPG) for j in range(i + 1, EPG)]):
                    last = tt(pairs[:, n, :], s4[:, :, i], s4[:, :, j], ALU.add)
                link(last)
                gs, gm, g1 = sm[:, 280:288], sm[:, 288:290], sm[:, 290:298]
                link(v.tensor_reduce(gs, pairs.rearrange("p s n -> p n s"), AX.X, ALU.max))

                def first_best(score, best, onehot, rank, n):
                    link(v.tensor_reduce(best, score, AX.X, ALU.max))
                    link(tt(onehot, score, each(best, n), ALU.is_equal))
                    link(tt(onehot, onehot, rows(rank, TT), ALU.mult))
                    link(v.tensor_reduce(best, onehot, AX.X, ALU.max))
                    link(tt(onehot, onehot, each(best, n), ALU.is_equal))

                first_best(s3(280, TT, NGRP), gm, s3(290, TT, NGRP), rank4[:, :], NGRP)
                link(ts(g1, g1, -NEG, NEG, ALU.mult, ALU.add))
                link(tt(s4, s4, each(g1, EPG), ALU.add))
                o1, o2 = s3(304, TT, NE), s3(336, TT, NE)
                first_best(selp, top, o1, rank16[:, :], NE)
                link(stt(sm[:, 200:232], sm[:, 304:336], 2 * NEG, sm[:, 200:232], ALU.mult, ALU.add))
                first_best(selp, top, o2, rank16[:, :], NE)
                tt(sm[:, 304:336], sm[:, 304:336], sm[:, 336:368], ALU.add).then_inc(route_ready.sem, 1)
                dve.wait_ge(route_ready.sem, route_ready.upto("dve"))
                link(tt(gate, e, o1, ALU.mult))
                link(v.tensor_reduce(tot, gate, AX.X, ALU.add))
                link(v.reciprocal(tot, tot))
                link(tt(gate, gate, each(tot, NE), ALU.mult))
                dve.wait_ge(*full(f"rank{l}"))
                b = bank_of(f"rank{l}")[:, 0:TT * NE].rearrange("p (n m) -> p n m", n=TT)
                moved(f"rank{l}", tt(number_t, mask_t, b, ALU.mult))
                dve.wait_ge(*drained(f"rank{l}"))

            def by_slots(table, i, odd):
                cols = bass.ds(i * 4 + 2 * odd, 2) if not isinstance(i, int) else slice(4 * i + 2 * odd, 4 * i + 2 * odd + 2)
                return table[:, :, cols].unsqueeze(3).broadcast_to([P, TT, 2, SLOTS])

            def fill_slots(l, i, odd):
                numbers = slot_no[:, :].unsqueeze(1).unsqueeze(1).broadcast_to([P, TT, 2, SLOTS])
                tt(slot, numbers, by_slots(number_t, i, odd), ALU.is_equal).then_inc(slots_ready, 1)

            def weigh_slots(l, i, odd):
                dve.wait_ge(slots_ready, i * 2 + (PAIRS * l + odd + 1))
                tt(slot_g, slot, by_slots(gate_t, i, odd), ALU.mult).then_inc(gated_ready, 1)

            def moe(l):
                fill_slots(l, 0, 0)
                weigh_slots(l, 0, 0)
                over = sm[:, 232:264].rearrange("p (n m) -> p n m", n=TT)
                link(ts(over, number_t, SLOTS + 0.5, None, ALU.is_gt))
                tt(gate_o, gate_t, over, ALU.mult)
                v.tensor_reduce(sm[:, 264:265], sm[:, 232:264], AX.X, ALU.add).then_inc(over_summed, 1)
                dve.wait_ge(*full(f"over{l}"))
                moved(f"over{l}", v.tensor_copy(sm[0:1, 265:266], bank_of(f"over{l}")[0:1, 0:1]))
                dve.wait_ge(*drained(f"over{l}"))
                ts(over_flag[0:1, l:l + 1], sm[0:1, 265:266], 0.5, None, ALU.is_gt).then_inc(flagged, 1)

                def pair(i, odd):
                    last_pair = isinstance(i, int) and 2 * i + odd == PAIRS - 1
                    if not last_pair:
                        first = isinstance(i, int) and 2 * i + odd == 0
                        dve.wait_ge(*(full(f"xg{l}.1") if first else pair_full(l, i, odd - 1, "xg1")))
                        dve.wait_ge(gated_ready, i * 2 + (PAIRS * l + odd + 1))
                        fill_slots(l, i, odd + 1)
                    dve.wait_ge(*pair_drained(l, i, odd, "g"))
                    dve.wait_ge(*pair_full(l, i, odd, "u"))
                    tt(hide, sge, pair_bank(l, i, odd, "u")[:, :], ALU.mult).then_inc(pair_drain_sem(l, i, odd, "u"), 1)
                    dve.wait_ge(*pair_full(l, i, odd, "S"))
                    v.tensor_copy(S_e, pair_bank(l, i, odd, "S")[:, 0:T]).then_inc(pair_drain_sem(l, i, odd, "S"), 1)
                    if not last_pair:
                        weigh_slots(l, i, odd + 1)
                    dve.wait_ge(*pair_full(l, i, odd, "d0"))
                    v.tensor_copy(ye[:, 0:512], pair_bank(l, i, odd, "d0")[:, :]) \
                        .then_inc(pair_drain_sem(l, i, odd, "d0"), 1)

                all_pairs(dve, pair)
                dve.wait_ge(flagged, l + 1)
                flag = dve.value_load(over_flag[0:1, l:l + 1], min_val=0, max_val=1)
                with dve.If(flag > 0):
                    blocks = FE // HB
                    dve.wait_ge(over_moved[l], NE // 2 + 1)
                    with dve.Fori(0, NE) as e:
                        for n in range(blocks):
                            dve.wait_ge(over_silu[l], e * blocks + n + 1)
                            tt(sgw_o, sg_o, gbc[:, bass.ds(e, 1), :].rearrange("p a t -> p (a t)"), ALU.mult) \
                                .then_inc(over_scaled[l], 1)
                            dve.wait_ge(over_scaled[l], e * blocks + n + 1)
                            tt(hid_o, sgw_o, bank[1][:, T:2 * T], ALU.mult).then_inc(over_hid[l], 1)
                    dve.wait_ge(over_down[l], NE * blocks)

            def swiglu(tag, n):
                k0, d0, u0 = uses[f"{tag}.0"], n * STEPS, tags.index(f"{tag}.0")

                def low(i, j, part):
                    dve.wait_ge(w_hi_ready[part], i * BODY + (d0 + j + 1))
                    tt(w_lo[:, j % 2, part, :].bitcast(F32R),
                       wring[:, (u0 + j) % WSLOTS, part * DC * HB:(part + 1) * DC * HB], w_hi[:, j % 2, part, :],
                       ALU.subtract).then_inc(w_lo_ready[part], 1)

                def step(i, j, ahead=2):
                    k = k0 + j
                    dve.wait_ge(silu_ready.sem, i * BODY + (d0 + j + 1))
                    if not (isinstance(i, int) and i == j == 0):
                        dve.wait_ge(hid_ready, i * BODY + (d0 + j))
                    up = bank[k % 4][:, T:2 * T]
                    tt(hid[:, :], sg[:, j % 2, :], up, ALU.mult)
                    tt(hid_hi[:, j % 2, :].bitcast(F32R), sg[:, j % 2, :], up, ALU.mult).then_inc(bank_drained[k % 4], 1)
                    dve.wait_ge(bank_drained[k % 4], i + k // 4 + 1)
                    tt(hid_lo[:, j % 2, :].bitcast(F32R), hid[:, :], hid_hi[:, j % 2, :], ALU.subtract) \
                        .then_inc(hid_ready, 1)
                    if ahead == 2:
                        for part in range(2):
                            low(i, j + 2, part)
                    if ahead >= 1:
                        low(i, j + 1, 2)

                low(0, 0, 0)
                for k in range(DC):
                    dve.wait_ge(h_hi_ready.sem, h_hi_ready.upto("dve"))
                    tt(h_lo[:, k, :].bitcast(F32R), H[:, k, :], h_hi[:, k, :], ALU.subtract).then_inc(h_lo_ready.sem, 1)
                low(0, 0, 1)
                low(0, 1, 0)
                low(0, 1, 1)
                low(0, 0, 2)
                turns, rest = swiglu_turns(STEPS)
                for j in range(BODY):
                    step(0, j)
                with dve.Fori(1, turns) as i:
                    for j in range(BODY):
                        step(i, j)
                for j in range(rest):
                    step(turns, j, min(2, rest - 1 - j))

            def attention(tag, heads, score):
                for i in range(2):
                    last = v.memset(Ss[i][:, 0, P:T], NEG)
                link(last)

                def scores(h):
                    name, c, S = f"{tag}.s{h}", 64 + 8 * (h % 2), Ss[h % 2]
                    dve.wait_ge(*full(name))
                    b = bank_of(name)
                    score(h, S[:, 0, 0:P], b[:, 0:P], 0, P)
                    moved(name, score(h, S[:, 1, :], b[:, T:2 * T], 1, T))
                    dve.wait_ge(*drained(name))
                    link(v.tensor_reduce(sm[:, c + 4:c + 6], S, AX.X, ALU.max))
                    ts(sm[:, c:c + 2], sm[:, c + 4:c + 6], -1.0, None, ALU.mult).then_inc(score_ready.sem, 1)

                def normed(h):
                    c, E = 64 + 8 * (h % 2), Es[h % 3]
                    dve.wait_ge(prob_exp.sem, prob_exp.upto("dve"))
                    link(v.reciprocal(sm[:, c + 6:c + 8], sm[:, c + 2:c + 4]))
                    ts(E[:, 0, 0:P], E[:, 0, 0:P], sm[:, c + 6:c + 7], None, ALU.mult)
                    ts(E[:, 1, :], E[:, 1, :], sm[:, c + 7:c + 8], None, ALU.mult).then_inc(prob_ready.sem, 1)

                for it in range(heads + 1):
                    if it < heads:
                        scores(it)
                    if it >= 1:
                        normed(it - 1)

            def rotary_angles():
                two_pi = 2 * np.pi
                c1 = 6.28125
                c2 = float(np.float32(np.round((two_pi - c1) * 2.0 ** 22) / 2.0 ** 22))
                c3 = float(np.float32(two_pi - c1 - c2))
                magic = 1.5 * 2.0 ** 23
                dve.wait_ge(small_landed, 16 * N_SMALL)
                link(v.tensor_copy(posf[:, :], posi[:, :]))
                ang, sn, cs = sm[:, 500:532], trig[:, 1, :, :].rearrange("p i d -> p (i d)"), trig[:, 0, :, :].rearrange("p i d -> p (i d)")
                for i in range(TT):
                    last = ts(ang[:, i * HR:(i + 1) * HR], invf[:, :], posf[:, i:i + 1], None, ALU.mult)
                link(last)
                link(ts(cs, ang, 1.0 / two_pi, magic, ALU.mult, ALU.add))
                link(ts(cs, cs, magic, None, ALU.subtract))
                for c in (c1, c2, c3):
                    link(stt(ang, cs, -c, ang, ALU.mult, ALU.add))
                lim = 3.1415925
                link(ts(sn, ang, lim, -lim, ALU.min, ALU.max))
                link(ts(cs, ang, np.pi / 2, None, ALU.add))
                link(ts(ang, cs, np.pi, None, ALU.is_gt))
                link(stt(cs, ang, -two_pi, cs, ALU.mult, ALU.add))
                ts(cs, cs, lim, -lim, ALU.min, ALU.max).then_inc(rope_in.sem, 1)

            layer_norm("ln00", 0, 0, "y0.", [(H, *modulation(0, 1), h_ready)])
            routing(0)
            rotary_angles()
            moe(0)
            kv_shift = DEPTH * 6 * DC
            layer_norm("ln01", 0, 1, None, [(H2, kv_shift, kv_shift + DC, h2_ready), (H, *modulation(1, 0), h_ready)])
            attention("moba", AH, lambda h, dst, b, i, n: stt(dst, alibi[:, i, 0:n], 2.0 ** (-8.0 * (h + 1) / AH), b,
                                                              ALU.mult, ALU.add))
            layer_norm("ln10", 1, 0, "y1.", [(H, *modulation(1, 1), h_ready)])
            routing(1)
            moe(1)
            layer_norm("ln11", 1, 1)

            done = [0]

            def half_step(tag):
                swiglu(tag, done[0] // STEPS)
                done[0] += STEPS
                for m in range(DC):
                    if m < DC - 2:
                        dve.wait_ge(sum_done, (done[0] // STEPS - 1) * (DC // 2 - 1) + m // 2 + 1)
                    else:
                        dve.wait_ge(down_done.sem, done[0])
                    stt(X[:, m, :], ysum(m), 0.5, X[:, m, :], ALU.mult, ALU.add).then_inc(x_ready.sem, 1)

            for l in range(DEPTH):
                rms_norm(f"f1{l}", "ffn1", l, h_ffn_ready)
                half_step(f"f1{l}")
                rms_norm(f"mx{l}", "mix", l, h_mix_ready)
                for k in range(DC):
                    x_low(H, k)
                t = f"m{l}."
                v.memset(xb[:, :, 0:PAD], 0.0).then_inc(pad_cleared.sem, 1)
                dve.wait_ge(pad_cleared.sem, pad_cleared.upto("dve"))
                x8, a8, u8 = sm[:, 128:144], sm[:, 144:160], sm[:, 160:176]
                dtv, da = sm[:, 416:432].rearrange("p (i h) -> p i h", i=TT), sm[:, 432:448].rearrange("p (i h) -> p i h", i=TT)
                for name, src, n, gain, r in (("cq", cq, 3, "qn", 0), ("ckv", ckv, 2, "kvn", 1)):
                    dve.wait_ge(*drained(f"{t}{name}ms"))
                    link(v.reciprocal(nrm[:, r, :], nrm[:, r, :]))
                    for m in range(n):
                        last = stt(src[:, m, :], src[:, m, :], vec(gain, l * n + m), nrm[:, r, :], ALU.mult, ALU.mult)
                    last.then_inc(lat_ready.sem, 1)
                for i in range(TT):
                    dve.wait_ge(*drained(f"{t}kr{i}"))
                    last = v.tensor_copy(Kt[:, i, :, NOPE:QK], rows(krs[:, i, :], MH))
                last.then_inc(qksq_ready.sem, 1)
                dve.wait_ge(*full(f"{t}dt"))
                moved(f"{t}dt", tt(x8.rearrange("p (i h) -> p i h", i=TT),
                                   bank_of(f"{t}dt")[:, 0:TT * SH].rearrange("p (i h) -> p i h", i=TT),
                                   rows(dtb[:, l, :], TT), ALU.add))
                dve.wait_ge(*drained(f"{t}dt"))
                stt(a8, x8, -1.0, x8, ALU.mult, ALU.max).then_inc(abs_ready.sem, 1)
                for m in range(8):
                    dve.wait_ge(*drained(f"{t}xbc{m}"))
                    conv(xb, xv, m, [vec("conv_w2", (l * CONV + j) * 8 + m) for j in range(CONV)])
                if l == 0:
                    dve.wait_ge(rope_ready.sem, rope_ready.upto("dve"))
                for n, src in enumerate((Qt, Kt)):
                    ss = sm[:, 96 + 16 * n:112 + 16 * n]
                    if n:
                        dve.wait_ge(*full(f"{t}wT"))
                        moved(f"{t}wT", tt(wT, bank_of(f"{t}wT")[:, :].rearrange("p (g t) -> p g t", g=GMG),
                                           rows(upper[:, 0, 0:P], GMG), ALU.mult))
                    dve.wait_ge(qkss_ready.sem, qkss_ready.upto("dve"))
                    v.tensor_reduce(ss, qksq.rearrange("p (h d) -> p h d", d=QK), AX.X, ALU.add).then_inc(qkstd_ready.sem, 1)
                    dve.wait_ge(qkstd_ready.sem, qkstd_ready.upto("dve", 2))
                    link(v.reciprocal(ss, ss))
                    flat = src.rearrange("p i h d -> p (i h) d")
                    link(tt(flat, flat, each(ss, QK), ALU.mult))
                    link(tt(flat, flat, rows(gainb[:, n, l, :], TT * MH), ALU.mult))
                    for i in range(TT):
                        x1, x2 = src[:, i, :, NOPE:NOPE + HR], src[:, i, :, NOPE + HR:QK]
                        cs, sn = rows(trig[:, 0, i, :], MH), rows(trig[:, 1, i, :], MH)
                        for a, (x, c) in enumerate(((x1, cs), (x2, sn), (x2, cs), (x1, sn))):
                            last = tt(rt[a][:, i, :, :], x, c, ALU.mult)
                    link(last)
                    x1, x2 = src[:, :, :, NOPE:NOPE + HR], src[:, :, :, NOPE + HR:QK]
                    tt(x1, rt[0], rt[1], ALU.subtract)
                    tt(x2, rt[2], rt[3], ALU.add).then_inc(qkrot_ready.sem, 1)
                dve.wait_ge(qkrot_ready.sem, qkrot_ready.upto("dve", 2))
                dve.wait_ge(abs_ready.sem, abs_ready.upto("dve"))
                log1p_exp(a8, u8, sm[:, 176:192], sm[:, 400:416])
                link(stt(sm[:, 416:432], x8, 0.0, u8, ALU.max, ALU.add))
                dve.wait_ge(consts_derived, 1)
                link(tt(da, dtv, rows(alb[:, l, :], TT), ALU.mult))
                dve.wait_ge(vsq_ready.sem, vsq_ready.upto("dve", 2))
                link(v.reciprocal(sm[:, 80:82], sm[:, 80:82]))
                for i in range(TT):
                    last = ts(vn[:, i, :], vn[:, i, :], sm[:, 80 + i:81 + i], None, ALU.mult)
                last.then_inc(vn_ready.sem, 1)
                for g in range(GMG):
                    dve.wait_ge(*full(f"{t}sp{g}"))
                    moved(f"{t}sp{g}", stt(yA[:, g, :].rearrange("p (i t) -> p i t", i=TT),
                                           bank_of(f"{t}sp{g}")[:, 0:T].rearrange("p (i t) -> p i t", i=TT),
                                           vec("gmv", l * GMG + g), rows(bsb[:, l, g, :], TT), ALU.mult, ALU.add))
                    dve.wait_ge(*drained(f"{t}sp{g}"))
                    last = tt(yA[:, g, :], yA[:, g, :], us[:, g, :], ALU.mult)
                last.then_inc(sp_ready.sem, 1)
                attention(f"{t}mla", MH, lambda h, dst, b, i, n: stt(dst, b, QK ** -0.5, neg_qk[:, i, 0:n], ALU.mult, ALU.add))
                for i in range(TT):
                    dve.wait_ge(*full(f"{t}xs{i}"))
                    moved(f"{t}xs{i}", tt(xdt[:, i, :].rearrange("p (h d) -> p h d", h=SH),
                                          bank_of(f"{t}xs{i}")[:, :].rearrange("p (h d) -> p h d", h=SH),
                                          each(dtv[:, i, :], SHD), ALU.mult))
                for g in range(SG):
                    dve.wait_ge(*full(f"{t}cb{g}"))
                    b = bank_of(f"{t}cb{g}")
                    tt(CB[g][:, 0, :], b[:, 0:T], upper[:, 0, :], ALU.mult)
                    moved(f"{t}cb{g}", tt(CB[g][:, 1, P:T], b[:, T + P:2 * T], upper[:, 1, P:T], ALU.mult))
                for g in range(SG):
                    dve.wait_ge(*drained(f"{t}cb{g}"))

                def decay_terms(h):
                    ts(Mh[h % 2][:, 0, 0:P], upper[:, 0, 0:P], 1.0, da[:, 0, h:h + 1], ALU.subtract, ALU.mult)
                    ts(Mh[h % 2][:, 1, :], upper[:, 1, :], 1.0, da[:, 1, h:h + 1], ALU.subtract, ALU.mult) \
                        .then_inc(decay_in.sem, 1)

                def output(c):
                    name = f"{t}y{2 * c}"
                    dve.wait_ge(*full(name))
                    moved(name, stt(yC[:, c, :], xv[:, c, :], dsk[:, l, c:c + 1], bank_of(name)[:, 0:T], ALU.mult, ALU.add))
                    dve.wait_ge(*drained(name))
                    tt(yC[:, c, :], yC[:, c, :], zs[:, c, :], ALU.mult).then_inc(yz_ready.sem, 1)

                decay_terms(0)
                decay_terms(1)
                for h in range(SH):
                    dve.wait_ge(*drained(f"{t}ss{h}"))
                    g = h // (SH // SG)
                    tt(Ph[h % 2][:, 0, :], Eh[h % 2][:, 0, :], CB[g][:, 0, :], ALU.mult)
                    tt(Ph[h % 2][:, 1, P:T], Eh[h % 2][:, 1, P:T], CB[g][:, 1, P:T], ALU.mult).then_inc(sp_mm_ready.sem, 1)
                    if h + 2 < SH:
                        decay_terms(h + 2)
                    if h % 2:
                        output(h // 2)
                    if h >= SH - 2:
                        low(f"merge{l}", h - (SH - 2))
                for g in range(SG):
                    dve.wait_ge(*drained(f"{t}yms{g}"))
                    link(v.reciprocal(nrm[:, g, :], nrm[:, g, :]))
                    for c in range(2 * g, 2 * g + 2):
                        last = stt(yC[:, c, :], yC[:, c, :], vec("ssdn", l * 4 + c), nrm[:, g, :], ALU.mult, ALU.mult)
                last.then_inc(yc_ready.sem, 1)
                low(f"merge{l}", 2)
                q = 0
                for n in range(NB):
                    for m in range(DC):
                        low(f"merge{l}", q + WBUFS)
                        q += 1
                        if m == 0:
                            dve.wait_ge(y_hi_ready.sem, y_hi_ready.upto("dve"))
                            tt(y_lo[:, :, :].bitcast(F32R), (yA, yB, yC)[n], y_hi[:, :, :], ALU.subtract) \
                                .then_inc(y_lo_ready.sem, 1)
                    for m in range(DC):
                        name, gate = f"{t}br{n}.{m}", sig[n % 2][:, m, :]
                        dve.wait_ge(*full(name))
                        dve.wait_ge(*drained(f"{t}g{n}.{m}"))
                        moved(name, tt(merged[:, m, :] if n == 0 else gate, bank_of(name)[:, 0:T], gate, ALU.mult))
                        dve.wait_ge(*drained(name))
                        if n:
                            last = tt(merged[:, m, :], merged[:, m, :], gate, ALU.add)
                            if n == NB - 1:
                                last.then_inc(merged_ready.sem, 1)
                                dve.wait_ge(merged_ready.sem, merged_ready.upto("dve"))
                            else:
                                link(last)
                        low(f"merge{l}", q + WBUFS)
                        q += 1
                        if n == NB - 1:
                            x_low(merged, m)
                for m in range(DC):
                    dve.wait_ge(*full(f"{t}o{m}"))
                    moved(f"{t}o{m}", tt(X[:, m, :], bank_of(f"{t}o{m}")[:, 0:T], X[:, m, :], ALU.add))
                    low(f"merge{l}", q + WBUFS)
                    q += 1
                rms_norm(f"f2{l}", "ffn2", l, h_ffn_ready)
                half_step(f"f2{l}")

        @block.sync
        def _(sp):
            nxt = [0]

            def slot_free(u):
                if u >= WSLOTS:
                    sp.wait_ge(*freed[u - WSLOTS])

            def load(tag, *pieces):
                u = nxt[0]
                nxt[0] += 1
                assert tags[u] == tag, (tags[u], tag)
                slot_free(u)
                o = 0
                for n, (src, k) in enumerate(pieces):
                    cols = src.shape[1]
                    inc = 48 - 16 * (len(pieces) - 1) if n == 0 else 16
                    sp.dma_start(wring[:, u % WSLOTS, o:o + k * cols].rearrange("p (k n) -> p k n", k=k),
                                 src.rearrange("(k p) n -> p k n", p=P)).then_inc(w_landed[u % WSLOTS], inc)
                    o += k * cols

            def ada(n):
                load(f"ada{n}", (A["w_ada"][:, n * 512:(n + 1) * 512], DC))

            def swiglu(tag, sources):
                u0, d0 = nxt[0], freed[nxt[0]][1] - 1
                assert tags[u0] == f"{tag}.0"

                def step(i, j):
                    u = (u0 + j) % WSLOTS
                    wg, wu, wd = sources(i, j)
                    o = DC * HB
                    for n, src in enumerate((wg, wu)):
                        sp.dma_start(wring[:, u, n * o:(n + 1) * o].rearrange("p (k n) -> p k n", k=DC), src) \
                            .then_inc(w_landed[u], 16)
                    sp.dma_start(wring[:, u, 2 * o:2 * o + D], wd).then_inc(w_landed[u], 16)

                turns, rest = swiglu_turns(STEPS)
                for j in range(BODY):
                    slot_free(u0 + j)
                    step(0, j)
                with sp.Fori(1, turns) as i:
                    for j in range(BODY):
                        sp.wait_ge(w_lo_ready[2], i * BODY + (d0 + j + 1 - BODY))
                        step(i, j)
                for j in range(rest):
                    sp.wait_ge(w_lo_ready[2], turns * BODY + d0 + j + 1 - BODY)
                    step(turns, j)
                nxt[0] += STEPS

            def moe(l):
                u0 = nxt[0]
                assert tags[u0] == f"moe{l}.0.0"
                mats = [A[f"moe_w_{name}"][l].rearrange("e (k p) n -> p e k n", p=P) for name in ("gate", "up", "down")]

                def pair(i, odd):
                    for n in range(PAIR_UNITS):
                        u = u0 + PAIR_UNITS * odd + n
                        if isinstance(i, int):
                            slot_free(u + 2 * PAIR_UNITS * i)
                        else:
                            back, of = divmod(n - WSLOTS, PAIR_UNITS)
                            sp.wait_ge(*pair_full(l, i, odd + back, ("g", "u", "d1")[of // 2]))
                        src, e = mats[n // 2], 2 * odd + n % 2
                        one = slice(4 * i + e, 4 * i + e + 1) if isinstance(i, int) else bass.ds(i * 4 + e, 1)
                        k = src.shape[2]
                        sp.dma_start(wring[:, u % WSLOTS, 0:D * FE // P].rearrange("p (k n) -> p k n", k=k),
                                     src[:, one, :, :].rearrange("p e k n -> p (e k) n")) \
                            .then_inc(w_landed[u % WSLOTS], 48)

                all_pairs(sp, pair)
                nxt[0] += PAIRS * PAIR_UNITS
                sp.wait_ge(flagged, l + 1)
                flag = sp.value_load(over_flag[0:1, l:l + 1], min_val=0, max_val=1)
                with sp.If(flag > 0):
                    sp.wait_ge(*freed[nxt[0] - 1])

                    def expert(one):
                        for n, src in enumerate(mats):
                            sp.dma_start(wring[:, n, 0:D * FE // P].rearrange("p (k n) -> p k n", k=src.shape[2]),
                                         src[:, one, :, :].rearrange("p e k n -> p (e k) n")) \
                                .then_inc(over_landed[l], 16)

                    expert(slice(0, 1))
                    with sp.Fori(1, NE) as e:
                        sp.wait_ge(over_down[l], e * (FE // HB))
                        expert(bass.ds(e, 1))
                    sp.wait_ge(over_down[l], NE * (FE // HB))

            def ffn(w_in, w_out):
                def sources(i, j):
                    def cols(o):
                        return bass.ds(i * (BODY * HB) + (o + j * HB), HB)
                    return (w_in[:, cols(0)].rearrange("(k p) n -> p k n", p=P),
                            w_in[:, cols(FF)].rearrange("(k p) n -> p k n", p=P), w_out[cols(0), :])
                return sources

            sp.wait_ge(rows_landed[0], 16 * len(TABLE[0]))
            for n in range(ADA_FIRST):
                ada(n)
            for n in range(2 * DI // 512):
                load(f"a_w_in{n}", (A["a_w_in"][0][:, n * 512:(n + 1) * 512], DC))
                if n == 2:
                    with nc.allow_non_contiguous_dma(reason="small tables"):
                        sp.dma_start(wif[:, :, :], A["a_w_if"][0].rearrange("(k p) n -> p k n", p=P)).then_inc(small_landed, 16)
                        sp.dma_start(bif[:, :], A["a_b_if"].rearrange("o (g h) -> h (o g)", h=NH)).then_inc(small_landed, 16)
                        sp.dma_start(wr[:, :, :], A["moe_w_router"].rearrange("(k p) n -> p k n", p=P)).then_inc(small_landed, 16)
                        sp.dma_start(brb[:, :], A["moe_b_router"].partition_broadcast(P)).then_inc(small_landed, 16)
                        sp.dma_start(posi[:, :], A["positions_2"].rearrange("o (i p) -> p (o i)", p=P)).then_inc(small_landed, 16)
                        sp.dma_start(dtb[:, :, :], A["ssd_dt_bias_2"].partition_broadcast(P)).then_inc(small_landed, 16)
                        sp.dma_start(alb[:, :, :], A["ssd_a_log_2"].partition_broadcast(P)).then_inc(small_landed, 16)
                        sp.dma_start(gmw[:, :, :, :], A["gm_w_s_2"].rearrange("l g t s -> t l g s")).then_inc(small_landed, 16)
                        sp.dma_start(bsb[:, :, :, :], A["gm_b_s_2"].partition_broadcast(P)).then_inc(small_landed, 16)
                        sp.dma_start(gainb[:, 0, :, :], A["mla_q_gain_2"].partition_broadcast(P)).then_inc(small_landed, 16)
                        sp.dma_start(gainb[:, 1, :, :], A["mla_k_gain_2"].partition_broadcast(P)).then_inc(small_landed, 16)
                        for l in range(DEPTH):
                            for o in range(2):
                                sp.dma_start(dsk[o * SHD:(o + 1) * SHD, l, :],
                                              A["ssd_d_2"][l].rearrange("(c o) -> o c", o=2)[o].partition_broadcast(SHD)) \
                                    .then_inc(small_landed, 16)
                for a in ADA_IN[n]:
                    ada(a)
            for h in range(NH):
                for a in ADA_HEAD[h]:
                    ada(a)
                load(f"qk{h}", (A["a_wq"][0, h], DHC), (A["a_wk"][0, h], DHC))
                load(f"v{h}", (A["a_wv"][0, h], DHC))
            for n in range(D // 256):
                load(f"a_w_out{n}", (A["a_w_out"][0][:, n * 256:(n + 1) * 256], DIC))
            moe(0)
            for name, src, o in (("k", A["b_w_kv"], 0), ("v", A["b_w_kv"], D), ("q", A["b_wq"][0], 0)):
                for n in range(2):
                    load(f"b{name}{n}", (src[:, o + n * 512:o + (n + 1) * 512], DC))
            for n in range(2):
                load(f"bo{n}", (A["b_wo"][0][:, n * 512:(n + 1) * 512], DC))
            moe(1)
            for l in range(DEPTH):
                swiglu(f"f1{l}", ffn(A["ffn1_w_in_2"][l], A["ffn1_w_out_2"][l]))
                t, w = f"m{l}.", A["w_in_2"][l]
                for tag, o, n in (("cq", O_CQ, QR), ("ckv", O_CKV, KVR + ROPE), ("xbc0", O_XBC, 512),
                                  ("xbc1", O_XBC + 512, 512 + SH)):
                    load(t + tag, (w[:, o:o + n], DC))
                load(t + "uq", (A["mla_w_uq_2"][l], QR // P))
                load(t + "ukv", (A["mla_w_ukv_2"][l], KVR // P))
                for tag, o in (("u", O_U), ("v", O_V), ("z", O_Z)):
                    load(t + tag, (w[:, o:o + 512], DC))
                for n in range(NB):
                    for hf in range(2):
                        o = O_G + n * D + hf * 512
                        load(f"{t}g{n}.{hf}", (w[:, o:o + 512], DC))
                    load(f"{t}br{n}", (A["w_branch_2"][l, n], 4))
                for hf in range(2):
                    load(f"{t}o{hf}", (A["w_out_2"][l][:, hf * 512:(hf + 1) * 512], DC))
                swiglu(f"f2{l}", ffn(A["ffn2_w_in_2"][l], A["ffn2_w_out_2"][l]))
            assert nxt[0] == len(tags)
            for i in range(TT):
                for hf in range(2):
                    sp.wait_ge(*drained(f"out{i}.{hf}"))
            sp.dma_start(out[0].rearrange("(i p) d -> p i d", p=P), xo).then_inc(out_landed, 16)
            sp.wait_ge(out_landed, 16)

        @block.gpsimd
        def _(pool):
            g = nc.gpsimd
            n_steps = [0]

            def link(ins):
                ins.then_inc(pool_steps, 1)
                n_steps[0] += 1
                pool.wait_ge(pool_steps, n_steps[0])

            g.memset(ident[:, :], 0.0)
            g.memset(ones[:, :], 1.0)
            g.memset(upper[:, :, :], 1.0)
            g.memset(neg_st[:, :, :], 0.0)
            g.memset(neg_qk[:, :, :], 0.0)
            g.memset(eps_ln[:, :], LN_EPS)
            g.memset(eps_rms[:, :], RMS_EPS)
            inv = 1.0 / (np.float32(10000.0) ** (np.arange(0, ROPE, 2, dtype=np.float32) / np.float32(ROPE)))
            for d in range(HR):
                g.memset(invf[:, d:d + 1], float(np.float32(inv[d])))
            for n in range(NGRP):
                g.memset(rank4[:, n:n + 1], float(NGRP - n))
            for n in range(NE):
                g.memset(rank16[:, n:n + 1], float(NE - n))
            link(g.iota(alibi[:, :, :], pattern=[[-P, TT], [1, T]], base=0, channel_multiplier=-1,
                        allow_small_or_imprecise_dtypes=True))
            r_less_c = dict(pattern=[[P, TT], [-1, T]], base=0, channel_multiplier=1)
            c_less_r = dict(pattern=[[-P, TT], [1, T]], base=0, channel_multiplier=-1)
            g.affine_select(out=ident[:, :], in_=ident[:, :], compare_op=ALU.not_equal, fill=1.0, base=0,
                            pattern=[[-1, P]], channel_multiplier=1)
            g.affine_select(out=upper[:, :, :], in_=upper[:, :, :], compare_op=ALU.is_ge, fill=0.0, **c_less_r)
            g.affine_select(out=neg_st[:, :, :], in_=neg_st[:, :, :], compare_op=ALU.is_ge, fill=NEG, **c_less_r)
            g.affine_select(out=neg_qk[:, :, :], in_=neg_qk[:, :, :], compare_op=ALU.is_ge, fill=NEG, **r_less_c)
            g.affine_select(out=alibi[:, :, :], in_=alibi[:, :, :], compare_op=ALU.is_ge, fill=NEG, **r_less_c)
            g.iota(slot_no[:, :], pattern=[[1, SLOTS]], base=1, channel_multiplier=0,
                   allow_small_or_imprecise_dtypes=True).then_inc(consts_made, 1)
            for l in range(DEPTH):
                first, tiles = split[f"mix{l}"]
                for q in range(len(tiles)):
                    pool.wait_ge(wt_hi_ready, first + q + 1)
                    g.tensor_tensor(part_tile(1, f"mix{l}", q).bitcast(F32R), raw_tile(f"mix{l}", q),
                                    part_tile(0, f"mix{l}", q), ALU.subtract).then_inc(wt_lo_ready, 1)


_INS = ['x', 'c', 'w_ada', 'b_ada', 'ln_g', 'ln_b', 'a_w_in', 'a_conv_w', 'a_conv_b', 'a_wq', 'a_wk', 'a_wv', 'a_w_if',
        'a_b_if', 'a_gn_g', 'a_skip', 'a_w_out', 'b_w_kv', 'b_wq', 'b_wo', 'moe_w_router', 'moe_b_router',
        'moe_w_gate', 'moe_w_up', 'moe_w_down', 'positions_2', 'ffn1_norm_2', 'ffn1_w_in_2', 'ffn1_w_out_2',
        'mix_norm_2', 'w_in_2', 'gm_v_norm_2', 'gm_w_s_2', 'gm_b_s_2', 'mla_q_norm_2', 'mla_kv_norm_2', 'mla_w_uq_2',
        'mla_w_ukv_2', 'mla_q_gain_2', 'mla_k_gain_2', 'ssd_conv_w_2', 'ssd_conv_b_2', 'ssd_dt_bias_2', 'ssd_a_log_2',
        'ssd_d_2', 'ssd_norm_2', 'w_branch_2', 'w_out_2', 'ffn2_norm_2', 'ffn2_w_in_2', 'ffn2_w_out_2']


def kernel(**inputs):
    import numpy as _np
    import concourse.bacc as _bacc
    from concourse import mybir as _mybir
    from concourse.bass_utils import run_bass_kernel_spmd as _run

    nc = _bacc.Bacc("TRN2", target_bir_lowering=False, num_devices=1)
    arrays, aps = {}, {}
    for name in _INS:
        a = _np.ascontiguousarray(inputs[name])
        arrays[f"in_{name}"] = a
        aps[name] = nc.dram_tensor(f"in_{name}", a.shape, _mybir.dt.from_np(a.dtype), kind="ExternalInput").ap()
    out = nc.dram_tensor("out", (1, T, D), _mybir.dt.float32, kind="ExternalOutput").ap()
    build(nc, aps, out)
    r = _run(nc, [arrays], core_ids=[0])
    return r.results[0]["out"]
```
